# Optimizing a Trainium2 kernel written in Bass

```python
import jax, jax.numpy as jnp
from jax import lax
import numpy as np

D_MODEL = 1024
BATCH = 1
SEQ = 1024
DEPTH = 1

GRID_W = 64
CTX_LEN = 256
D_RWKV = 512
D_CONV = 512
RWKV_HEAD = 64
RWKV_HEADS = D_RWKV // RWKV_HEAD
CONV_WIDTH = 3
LORA_W = 64
LORA_A = 64
LORA_G = 128
N_EXPERTS = 16
EC_CAPACITY = 2
D_EXPERT = 1024
NORM_EPS = 1e-6
GN_EPS = 64e-5
RWKV_COLS = 3 * D_RWKV + LORA_W + LORA_A + LORA_G
CONV_COLS = 3 * D_CONV
D_IN = RWKV_COLS + CONV_COLS


def rmsnorm(x, g):
    xf = x.astype(jnp.float32)
    y = xf * lax.rsqrt(jnp.mean(xf * xf, axis=-1, keepdims=True) + NORM_EPS)
    return (y * g.astype(jnp.float32)).astype(x.dtype)

def modulate(h, shift, scale):
    return h * (1 + scale) + shift

def grid_shift(p, rows):
    b, t, ch = p.shape
    q = p.reshape(b, rows, GRID_W, ch // 4, 4)
    zc = jnp.zeros_like(q[:, :, :1, :, 0])
    zr = jnp.zeros_like(q[:, :1, :, :, 0])
    left = jnp.concatenate([zc, q[:, :, :-1, :, 0]], axis=2)
    right = jnp.concatenate([q[:, :, 1:, :, 1], zc], axis=2)
    up = jnp.concatenate([zr, q[:, :-1, :, :, 2]], axis=1)
    down = jnp.concatenate([q[:, 1:, :, :, 3], zr], axis=1)
    return jnp.stack([left, right, up, down], axis=-1).reshape(b, t, ch)

def seq_shift(p):
    b, t, ch = p.shape
    q = p.reshape(b, t, ch // 2, 2)
    z = jnp.zeros_like(q[:, :1, :, 0])
    prev = jnp.concatenate([z, q[:, :-1, :, 0]], axis=1)
    nxt = jnp.concatenate([q[:, 1:, :, 1], z], axis=1)
    return jnp.stack([prev, nxt], axis=-1).reshape(b, t, ch)

def split_rwkv(p, mu, shifted):
    p = p + mu * (shifted - p)
    o = 3 * D_RWKV
    return jnp.split(p, [D_RWKV, 2 * D_RWKV, o, o + LORA_W, o + LORA_W + LORA_A], axis=-1)

def wkv_scan(s0, r, w, k, v, a, b, reverse):
    def step(s, inp):
        r_t, w_t, k_t, v_t, a_t, b_t = inp
        sa = jnp.einsum('bhvk,bhk->bhv', s, a_t)
        s = s * w_t[:, :, None, :] + sa[..., :, None] * b_t[:, :, None, :] + v_t[..., :, None] * k_t[:, :, None, :]
        return s, jnp.einsum('bhvk,bhk->bhv', s, r_t)
    xs = tuple(jnp.moveaxis(z, 1, 0) for z in (r, w, k, v, a, b))
    s, y = lax.scan(step, s0, xs, reverse=reverse)
    return jnp.moveaxis(y, 0, 1), s

def rwkv_bidir(xr, xk, xv, xw, xa, w0, w_up, a0, a_up, k_k, k_a, s0_f, s0_b):
    bsz, t = xr.shape[0], xr.shape[1]
    f32 = jnp.float32
    heads = lambda z: z.astype(f32).reshape(bsz, t, RWKV_HEADS, RWKV_HEAD)
    per_head = lambda z: z.astype(f32).reshape(RWKV_HEADS, RWKV_HEAD)
    r, k, v = heads(xr), heads(xk), heads(xv)
    kk = k * per_head(k_k)
    kk = kk / jnp.maximum(jnp.sqrt(jnp.sum(kk * kk, axis=-1, keepdims=True)), 1e-12)
    tw = jnp.tanh(xw.astype(f32))
    xa = xa.astype(f32)
    k_a_h = per_head(k_a)
    y_sum, k_sum, states = 0.0, 0.0, []
    for d, (rev, s0) in enumerate(((False, s0_f), (True, s0_b))):
        wl = -jax.nn.softplus(-(w0[d].astype(f32) + tw @ w_up[d].astype(f32))) - 0.5
        decay = jnp.exp(-jnp.exp(heads(wl)))
        a = heads(jax.nn.sigmoid(a0[d].astype(f32) + xa @ a_up[d].astype(f32)))
        kd = k * (1 + (a - 1) * k_a_h)
        y, s = wkv_scan(s0, r, decay, kd, v, -kk, kk * a, rev)
        y_sum = y_sum + y
        k_sum = k_sum + kd
        states.append(s)
    return y_sum, states[0], states[1], r, k_sum, v

def rwkv_out(y, r, k_sum, v, xg, g_up, r_k, gn_g, gn_b):
    bsz, t = y.shape[0], y.shape[1]
    f32 = jnp.float32
    mu = jnp.mean(y, axis=-1, keepdims=True)
    var = jnp.mean(jnp.square(y - mu), axis=-1, keepdims=True)
    yn = ((y - mu) * lax.rsqrt(var + GN_EPS)).reshape(bsz, t, D_RWKV) * gn_g.astype(f32) + gn_b.astype(f32)
    bonus = (jnp.sum(r * k_sum * r_k.astype(f32), axis=-1, keepdims=True) * v).reshape(bsz, t, D_RWKV)
    g = jax.nn.sigmoid(xg.astype(f32)) @ g_up.astype(f32)
    return (yn + bonus) * g

def dwconv3(u, w):
    return lax.conv_general_dilated(u, w[:, None, :].astype(u.dtype), window_strides=(1,), padding=((1, 1),),
                                    dimension_numbers=('NWC', 'WIO', 'NWC'), feature_group_count=u.shape[-1])

def short_conv(p, conv_w):
    b_gate, c_gate, u = jnp.split(p, 3, axis=-1)
    return b_gate * dwconv3(c_gate * u, conv_w)

def expert_choice_ffn(h, router_w, w_gate, w_up, w_down):
    bsz, t, d = h.shape
    cap = EC_CAPACITY * t // N_EXPERTS
    aff = jax.nn.softmax((h @ router_w).astype(jnp.float32), axis=-1)
    vals, idx = lax.top_k(jnp.swapaxes(aff, 1, 2), cap)
    xs = jax.vmap(lambda hb, ib: hb[ib])(h, idx)
    hid = jax.nn.silu(jnp.einsum('becd,edf->becf', xs, w_gate)) * jnp.einsum('becd,edf->becf', xs, w_up)
    out = jnp.einsum('becf,efd->becd', hid, w_down) * vals[..., None].astype(h.dtype)
    return jax.vmap(lambda ob, ib: jnp.zeros((t, d), h.dtype).at[ib.reshape(-1)].add(ob.reshape(-1, d)))(out, idx)

def first_inputs(seed: int = 0) -> dict:
    key = jax.random.key(seed)
    ks = jax.random.split(key, 28)
    L = DEPTH
    nrm = lambda k, shape, scale: jax.random.normal(k, shape, jnp.float32) * scale
    return {
        'x': nrm(ks[0], (BATCH, SEQ, D_MODEL), 1.0),
        'c': nrm(ks[1], (BATCH, D_MODEL), 1.0),
        'ctx': nrm(ks[2], (BATCH, CTX_LEN, D_MODEL), 1.0),
        'c_ctx': nrm(ks[3], (D_MODEL,), 1.0),
        'ada_w': nrm(ks[4], (L, D_MODEL, 6 * D_MODEL), 0.5 * D_MODEL ** -0.5),
        'ada_b': nrm(ks[5], (L, 6 * D_MODEL), 0.02),
        'norm1_g': 1.0 + nrm(ks[6], (L, D_MODEL), 0.02),
        'norm2_g': 1.0 + nrm(ks[7], (L, D_MODEL), 0.02),
        'w_in': nrm(ks[8], (L, D_MODEL, D_IN), D_MODEL ** -0.5),
        'shift_mu': jax.random.uniform(ks[9], (L, RWKV_COLS), jnp.float32),
        'w0': jax.random.uniform(ks[10], (L, 2, D_RWKV), jnp.float32, minval=-6.0, maxval=1.0),
        'w_lora_up': nrm(ks[11], (L, 2, LORA_W, D_RWKV), 0.1 * LORA_W ** -0.5),
        'a0': nrm(ks[12], (L, 2, D_RWKV), 0.5),
        'a_lora_up': nrm(ks[13], (L, 2, LORA_A, D_RWKV), LORA_A ** -0.5),
        'k_k': 0.85 + nrm(ks[14], (L, D_RWKV), 0.05),
        'k_a': 1.0 + nrm(ks[15], (L, D_RWKV), 0.05),
        'r_k': nrm(ks[16], (L, RWKV_HEADS, RWKV_HEAD), 0.1),
        'g_lora_up': nrm(ks[17], (L, LORA_G, D_RWKV), LORA_G ** -0.5),
        'gn_g': 1.0 + nrm(ks[18], (L, D_RWKV), 0.02),
        'gn_b': nrm(ks[19], (L, D_RWKV), 0.02),
        'conv_w': nrm(ks[20], (L, CONV_WIDTH, D_CONV), CONV_WIDTH ** -0.5),
        'w_out': nrm(ks[21], (L, D_RWKV + D_CONV, D_MODEL), (D_RWKV + D_CONV) ** -0.5),
        'router_w': nrm(ks[22], (L, D_MODEL, N_EXPERTS), D_MODEL ** -0.5),
        'exp_w_gate': nrm(ks[23], (L, N_EXPERTS, D_MODEL, D_EXPERT), D_MODEL ** -0.5),
        'exp_w_up': nrm(ks[24], (L, N_EXPERTS, D_MODEL, D_EXPERT), D_MODEL ** -0.5),
        'exp_w_down': nrm(ks[25], (L, N_EXPERTS, D_EXPERT, D_MODEL), D_EXPERT ** -0.5),
        'final_g': 1.0 + nrm(ks[26], (D_MODEL,), 0.02),
    }

def first_block(x, c, ctx, c_ctx, ada_w, ada_b, norm1_g, norm2_g, w_in, shift_mu, w0, w_lora_up, a0, a_lora_up,
              k_k, k_a, r_k, g_lora_up, gn_g, gn_b, conv_w, w_out, router_w, exp_w_gate, exp_w_up, exp_w_down,
              final_g):
    bsz, t, _ = x.shape
    rows = t // GRID_W
    s_zero = jnp.zeros((bsz, RWKV_HEADS, RWKV_HEAD, RWKV_HEAD), jnp.float32)
    for l in range(DEPTH):
        last = l == DEPTH - 1
        mod = jax.nn.silu(c) @ ada_w[l] + ada_b[l]
        mod_c = jax.nn.silu(c_ctx) @ ada_w[l] + ada_b[l]
        sh1, sc1, g1, sh2, sc2, g2 = jnp.split(mod[:, None, :], 6, axis=-1)
        csh1, csc1, cg1, csh2, csc2, cg2 = jnp.split(mod_c, 6, axis=-1)

        pc = modulate(rmsnorm(ctx, norm1_g[l]), csh1, csc1) @ w_in[l]
        px = modulate(rmsnorm(x, norm1_g[l]), sh1, sc1) @ w_in[l]
        pc_rw, pc_cv = pc[..., :RWKV_COLS], pc[..., RWKV_COLS:]
        px_rw, px_cv = px[..., :RWKV_COLS], px[..., RWKV_COLS:]

        cr, ck, cv, cw, ca, cgl = split_rwkv(pc_rw, shift_mu[l], seq_shift(pc_rw))
        xr, xk, xv, xw, xa, xgl = split_rwkv(px_rw, shift_mu[l], grid_shift(px_rw, rows))

        yc, sf, sb, rc, kc, vc = rwkv_bidir(cr, ck, cv, cw, ca, w0[l], w_lora_up[l], a0[l], a_lora_up[l],
                                            k_k[l], k_a[l], s_zero, s_zero)
        yx, _, _, rx, kx, vx = rwkv_bidir(xr, xk, xv, xw, xa, w0[l], w_lora_up[l], a0[l], a_lora_up[l],
                                          k_k[l], k_a[l], sf, sb)
        a_x = rwkv_out(yx, rx, kx, vx, xgl, g_lora_up[l], r_k[l], gn_g[l], gn_b[l]).astype(x.dtype)
        b_x = short_conv(px_cv, conv_w[l])
        x = x + g1 * (jnp.concatenate([a_x, b_x], axis=-1) @ w_out[l])
        if not last:
            a_c = rwkv_out(yc, rc, kc, vc, cgl, g_lora_up[l], r_k[l], gn_g[l], gn_b[l]).astype(ctx.dtype)
            b_c = short_conv(pc_cv, conv_w[l])
            ctx = ctx + cg1 * (jnp.concatenate([a_c, b_c], axis=-1) @ w_out[l])

        hx = modulate(rmsnorm(x, norm2_g[l]), sh2, sc2)
        x = x + g2 * expert_choice_ffn(hx, router_w[l], exp_w_gate[l], exp_w_up[l], exp_w_down[l])
        if not last:
            hc = modulate(rmsnorm(ctx, norm2_g[l]), csh2, csc2)
            ctx = ctx + cg2 * expert_choice_ffn(hc, router_w[l], exp_w_gate[l], exp_w_up[l], exp_w_down[l])
    return rmsnorm(x, final_g)


HEAD_DIM = 64
A_HEADS = D_MODEL // (2 * HEAD_DIM)
A_KV_HEADS = max(1, A_HEADS // 4)
A_WINDOW = 128
B_HEADS = D_MODEL // (2 * HEAD_DIM)
B_PATTERNS = ((128, 1), (512, 4), (2048, 16))
BLOCK = 128
ROPE_THETA = 10000.0
EPS = 1e-6
NEG = -1e30

A_WIDTH = A_HEADS * HEAD_DIM
A_KV_WIDTH = A_KV_HEADS * HEAD_DIM
B_WIDTH = B_HEADS * HEAD_DIM
MIX_WIDTH = A_WIDTH + B_WIDTH
IN_SPLITS = (A_WIDTH, A_KV_WIDTH, A_KV_WIDTH, A_WIDTH, B_WIDTH, B_WIDTH, B_WIDTH, B_WIDTH)
IN_WIDTH = sum(IN_SPLITS)


def rmsnorm_2(t, gain):
    tf = t.astype(jnp.float32)
    tf = tf * lax.rsqrt(jnp.mean(tf * tf, axis=-1, keepdims=True) + EPS)
    return (tf * gain.astype(jnp.float32)).astype(t.dtype)

def rope(t, pos):
    half = HEAD_DIM // 2
    inv = ROPE_THETA ** (-jnp.arange(half, dtype=jnp.float32) / half)
    ang = pos.astype(jnp.float32)[:, None] * inv[None, :]
    cos = jnp.cos(ang)[:, None, :]
    sin = jnp.sin(ang)[:, None, :]
    tf = t.astype(jnp.float32)
    t1, t2 = tf[..., :half], tf[..., half:]
    return jnp.concatenate([t1 * cos - t2 * sin, t2 * cos + t1 * sin], axis=-1).astype(t.dtype)

def banded_attention(q, k, v, max_dist, sinks=None):
    n, L, h, d = q.shape
    hkv = k.shape[2]
    g = h // hkv
    nb = -(-L // BLOCK)
    lp = nb * BLOCK
    pad = lp - L
    q = jnp.pad(q, ((0, 0), (0, pad), (0, 0), (0, 0)))
    k = jnp.pad(k, ((0, 0), (BLOCK, pad), (0, 0), (0, 0)))
    v = jnp.pad(v, ((0, 0), (BLOCK, pad), (0, 0), (0, 0)))
    qb = q.reshape(n, nb, BLOCK, hkv, g, d)
    kb = k.reshape(n, nb + 1, BLOCK, hkv, d)
    vb = v.reshape(n, nb + 1, BLOCK, hkv, d)
    kw = jnp.concatenate([kb[:, :-1], kb[:, 1:]], axis=2)
    vw = jnp.concatenate([vb[:, :-1], vb[:, 1:]], axis=2)
    s = jnp.einsum("nbqkgd,nbskd->nbkgqs", qb, kw,
                   preferred_element_type=jnp.float32) * (d ** -0.5)
    qi = jnp.arange(BLOCK)[:, None]
    sj = jnp.arange(2 * BLOCK)[None, :]
    dist = qi - sj + BLOCK
    key_pos = jnp.arange(nb)[:, None] * BLOCK - BLOCK + sj
    valid = ((dist >= 0) & (dist <= max_dist))[None] & (key_pos >= 0)[:, None, :]
    s = jnp.where(valid[None, :, None, None], s, NEG)
    m = s.max(axis=-1)
    if sinks is not None:
        sk = sinks.astype(jnp.float32).reshape(hkv, g)[None, None, :, :, None]
        m = jnp.maximum(m, sk)
    p = jnp.exp(s - m[..., None])
    l = p.sum(axis=-1)
    if sinks is not None:
        l = l + jnp.exp(sk - m)
    o = jnp.einsum("nbkgqs,nbskd->nbqkgd", p, vw.astype(jnp.float32))
    m = m.transpose(0, 1, 4, 2, 3)
    l = l.transpose(0, 1, 4, 2, 3)
    o = o / l[..., None]
    o = o.reshape(n, lp, h, d)[:, :L]
    m = m.reshape(n, lp, h)[:, :L]
    l = l.reshape(n, lp, h)[:, :L]
    return o, m, l

def dilated_attention(q, k, v):
    b, S, h, d = q.shape
    outs, ms, ls = [], [], []
    for window, dil in B_PATTERNS:
        L = S // dil

        def fold(t):
            return t.reshape(b, L, dil, h, d).transpose(0, 2, 1, 3, 4).reshape(b * dil, L, h, d)

        o, m, l = banded_attention(fold(q), fold(k), fold(v), window // dil)
        outs.append(o.reshape(b, dil, L, h, d).transpose(0, 2, 1, 3, 4).reshape(b, S, h, d))
        ms.append(m.reshape(b, dil, L, h).transpose(0, 2, 1, 3).reshape(b, S, h))
        ls.append(l.reshape(b, dil, L, h).transpose(0, 2, 1, 3).reshape(b, S, h))
    o = jnp.stack(outs)
    m = jnp.stack(ms)
    l = jnp.stack(ls)
    w = l * jnp.exp(m - m.max(axis=0, keepdims=True))
    return (w[..., None] * o).sum(axis=0) / w.sum(axis=0)[..., None]

def second_inputs(seed: int = 0) -> dict:
    key = jax.random.key(seed)
    ks = jax.random.split(key, 10)
    f32 = jnp.float32
    x = jax.random.normal(ks[0], (BATCH, SEQ, D_MODEL), f32)
    norm_gain = 1.0 + 0.1 * jax.random.normal(ks[1], (DEPTH, D_MODEL), f32)
    w_in = jax.random.normal(ks[2], (DEPTH, D_MODEL, IN_WIDTH), f32) * D_MODEL ** -0.5
    q_norm_a = 1.0 + 0.1 * jax.random.normal(ks[3], (DEPTH, HEAD_DIM), f32)
    k_norm_a = 1.0 + 0.1 * jax.random.normal(ks[4], (DEPTH, HEAD_DIM), f32)
    sinks_a = 0.5 * jax.random.normal(ks[5], (DEPTH, A_HEADS), f32)
    q_norm_b = 1.0 + 0.1 * jax.random.normal(ks[6], (DEPTH, HEAD_DIM), f32)
    k_norm_b = 1.0 + 0.1 * jax.random.normal(ks[7], (DEPTH, HEAD_DIM), f32)
    w_out = jax.random.normal(ks[8], (DEPTH, MIX_WIDTH, D_MODEL), f32) * MIX_WIDTH ** -0.5
    return {"x": x, "norm_gain": norm_gain, "w_in": w_in,
            "q_norm_a": q_norm_a, "k_norm_a": k_norm_a, "sinks_a": sinks_a,
            "q_norm_b": q_norm_b, "k_norm_b": k_norm_b, "w_out": w_out}

def second_block(x, norm_gain, w_in, q_norm_a, k_norm_a, sinks_a, q_norm_b, k_norm_b, w_out):
    b, S, _ = x.shape
    pos = jnp.arange(S)
    split_at = [int(c) for c in np.cumsum(IN_SPLITS)[:-1]]
    for i in range(DEPTH):
        hdn = rmsnorm_2(x, norm_gain[i])
        proj = jnp.einsum("bsd,de->bse", hdn, w_in[i])
        q_a, k_a, v_a, g_a, q_b, k_b, v_b, g_b = jnp.split(proj, split_at, axis=-1)

        q_a = rope(rmsnorm_2(q_a.reshape(b, S, A_HEADS, HEAD_DIM), q_norm_a[i]), pos)
        k_a = rope(rmsnorm_2(k_a.reshape(b, S, A_KV_HEADS, HEAD_DIM), k_norm_a[i]), pos)
        v_a = v_a.reshape(b, S, A_KV_HEADS, HEAD_DIM)
        o_a, _, _ = banded_attention(q_a, k_a, v_a, A_WINDOW - 1, sinks=sinks_a[i])
        o_a = o_a.reshape(b, S, A_WIDTH).astype(x.dtype) * jax.nn.silu(g_a)

        q_b = rope(rmsnorm_2(q_b.reshape(b, S, B_HEADS, HEAD_DIM), q_norm_b[i]), pos)
        k_b = rope(rmsnorm_2(k_b.reshape(b, S, B_HEADS, HEAD_DIM), k_norm_b[i]), pos)
        v_b = v_b.reshape(b, S, B_HEADS, HEAD_DIM)
        o_b = dilated_attention(q_b, k_b, v_b)
        o_b = o_b.reshape(b, S, B_WIDTH).astype(x.dtype) * jax.nn.silu(g_b)

        mixed = jnp.concatenate([o_a, o_b], axis=-1)
        x = x + jnp.einsum("bse,ed->bsd", mixed, w_out[i])
    return x


def setup_inputs(seed=0):
    out = dict(first_inputs(seed))
    for name, value in second_inputs(seed + 1).items():
        if name != "x":
            out[name + "_2"] = value
    return out


def reference(
    x, c, ctx, c_ctx, ada_w, ada_b, norm1_g, norm2_g, w_in, shift_mu, w0, w_lora_up, a0,
    a_lora_up, k_k, k_a, r_k, g_lora_up, gn_g, gn_b, conv_w, w_out, router_w, exp_w_gate,
    exp_w_up, exp_w_down, final_g, norm_gain_2, w_in_2, q_norm_a_2, k_norm_a_2, sinks_a_2,
    q_norm_b_2, k_norm_b_2, w_out_2,
):
    x = first_block(
        x, c, ctx, c_ctx, ada_w, ada_b, norm1_g, norm2_g, w_in, shift_mu, w0, w_lora_up, a0,
        a_lora_up, k_k, k_a, r_k, g_lora_up, gn_g, gn_b, conv_w, w_out, router_w, exp_w_gate,
        exp_w_up, exp_w_down, final_g,
    )
    return second_block(
        x, norm_gain_2, w_in_2, q_norm_a_2, k_norm_a_2, sinks_a_2, q_norm_b_2, k_norm_b_2,
        w_out_2,
    )


_drawn_inputs = setup_inputs


def setup_inputs(seed=0):
    import zlib

    import numpy as np

    out = dict(_drawn_inputs(seed))
    spreads = {}
    factors = {'c_ctx': 3.86,
     'norm1_g': 5.147,
     'norm2_g': 8.0,
     'w_lora_up': 22.987,
     'a0': 2.817,
     'k_k': 24.163,
     'k_a': 5.674,
     'gn_g': 64.0,
     'gn_b': 64.0,
     'final_g': 2.77,
     'norm_gain_2': 3.054,
     'q_norm_a_2': 8.0,
     'k_norm_a_2': 8.0,
     'sinks_a_2': 200.0,
     'q_norm_b_2': 8.0,
     'k_norm_b_2': 8.0}
    for name, (base, spread) in spreads.items():
        noise = np.random.default_rng([zlib.crc32(name.encode()), seed]).standard_normal(out[name].shape)
        drawn = base * np.exp(spread * noise) if base else spread * noise
        out[name] = __import__('jax').numpy.asarray(drawn.astype(out[name].dtype))
    for name, factor in factors.items():
        out[name] = (out[name] * factor).astype(out[name].dtype)
    return out
```

```python
from contextlib import ExitStack

import numpy as np

import concourse.bass as bass
from concourse import mybir

F32 = mybir.dt.float32
U32 = mybir.dt.uint32
ALU = mybir.AluOpType
ACT = mybir.ActivationFunctionType
AX = mybir.AxisListType.X

P = 128
D = 1024
KT = D // P
T = 1024
TT = T // P
TC = 256
TA = TC + T
GRID = 64
C = 64
NCH = TA // C
NCC = TC // C
HD = 64
HP = 4
NRW = 14
NE = 16
CAP = 128
KAPPA = float(np.exp(-0.5))
EPS = 1e-6
GN_EPS = 64e-5
NEG = -1e30

LEVELS = (1, 2, 4, 8, 16, 32)
CONST_AT = {}


def _constants():
    p = np.arange(P)[:, None]
    j = np.arange(P)[None, :]
    t = np.arange(C)[None, :]
    q = p % C
    parts = {
        "ident": (p == j),
        "stack": (q == t),
        "head": (p // C == j // C),
        "chunk": np.broadcast_to((np.arange(4 * C) % C != 0)[None, :], (P, 4 * C)),
        "maskf": np.concatenate([q < t, q <= t], 1),
        "maskb": np.concatenate([q > t, q >= t], 1),
    }
    for m in LEVELS:
        parts[f"lev{m}"] = (q // (2 * m) == t // (2 * m)) & (q // m != t // m)
    parts["eps"] = np.full((P, 1), EPS)
    parts["gn_eps"] = np.full((P, 1), GN_EPS)
    parts["pick"] = np.concatenate([p % 4 == i for i in range(4)] + [p % 2 == i for i in range(2)], 1)
    at, cols = 0, []
    for name, a in parts.items():
        CONST_AT[name] = (at, a.shape[1])
        at += a.shape[1]
        cols.append(a)
    return np.ascontiguousarray(np.concatenate(cols, 1).astype(np.float32))


def _rope_tables():
    half = HD // 2
    inv = (np.float32(10000.0) ** (-np.arange(half, dtype=np.float32) / np.float32(half))).astype(np.float32)
    ang = (np.arange(T, dtype=np.float32)[:, None] * inv[None, :]).astype(np.float32)
    cos, sin = np.cos(ang), np.sin(ang)
    full = np.concatenate([cos, cos, -sin, sin], 1).astype(np.float32)
    return np.ascontiguousarray(full.reshape(TT, P, 4 * half).transpose(1, 0, 2).reshape(P, TT * 4 * half))


def _bias_tables():
    p = np.arange(P)[:, None]
    dist = p + (T - P) - np.arange(T)[None, :]
    n = ((dist >= 0) & (dist <= 128)).astype(np.float32)
    n += (dist >= 0) & (dist <= 512) & (dist % 4 == 0)
    n += (dist >= 0) & (dist <= 2048) & (dist % 16 == 0)
    dil = np.where(n > 0, np.log(np.maximum(n, 1.0)), NEG)
    da = p + P - np.arange(2 * P)[None, :]
    win = np.where((da >= 0) & (da <= 127), 0.0, NEG)
    return np.ascontiguousarray(np.concatenate([dil, win], 1).astype(np.float32))


CONSTS = _constants()
NCONST = CONSTS.shape[1]

ROWS = [("ada_b", 48), ("norm1_g", 8), ("norm2_g", 8), ("shift_mu", 14), ("w0", 8), ("a0", 8), ("k_k", 4),
        ("k_a", 4), ("r_k", 4), ("gn_g", 4), ("gn_b", 4), ("conv_w", 12)]
ROW_AT = {}
_n = 0
for _name, _k in ROWS:
    ROW_AT[_name] = (_n, _k)
    _n += _k
NROWS = _n
ROWS2 = [("c", 8), ("c_ctx", 8), ("norm_gain_2", 8)]


class Chain:

    def __init__(self, eng, sem):
        self.eng, self.sem, self.n = eng, sem, 0

    def __call__(self, ins):
        self.n += 1
        ins.then_inc(self.sem, 1)
        self.eng.wait_ge(self.sem, self.n)


class Shared:
    pass


def sb(nc, ctx, name, shape, dt=F32):
    return ctx.enter_context(nc.sbuf_tensor(name, shape, dt))


class Signals:

    def __init__(self, nc):
        self.nc, self.held = nc, []

    def new(self, name):
        self.held.append(self.nc.alloc_semaphore(name=name))
        return self.held[-1]

    def clear(self):
        self.nc.clear_and_free_semaphores(self.held)
        self.held = []
        self.nc.all_engine_barrier()


def sems(nc, signals, *names):
    return [signals.new(n) for n in names]


def ring_sems(nc, signals, name, n):
    return [signals.new(f"{name}{i}") for i in range(n)]


def phase_params(nc, g, ctx0):
    with ExitStack() as ctx:
        prow = sb(nc, ctx, "prow", [P, P])
        prow2 = sb(nc, ctx, "prow2", [24, P])
        sig = sb(nc, ctx, "sig_c", [P, 16])
        loaded, rows_t, cols, sig_ok, chain_v = sems(nc, ctx0, "par_loaded", "par_turned", "par_cols", "par_sig", "par_chain")
        block = ctx.enter_context(nc.Block())
        n_loads = len(ROWS) + len(ROWS2) + 1

        @block.sync
        def _(sp):
            sp.dma_start(g.const[:, :], g.i["consts"]).then_inc(loaded, 16)
            for name, k in ROWS:
                flat = g.flat(name)
                at = ROW_AT[name][0]
                sp.dma_start(prow[at:at + k, :], flat.rearrange("(r n) -> r n", n=P)).then_inc(loaded, 16)
            at = 0
            for name, k in ROWS2:
                sp.dma_start(prow2[at:at + k, :], g.flat(name).rearrange("(r n) -> r n", n=P)).then_inc(loaded, 16)
                at += k

        @block.tensor
        def _(pe):
            pe.wait_ge(loaded, 16 * n_loads)
            pe.transpose(g.ps[0][:, 0:NROWS], prow[0:NROWS, :], g.c("ident")[0:NROWS, 0:NROWS]).then_inc(rows_t, 1)
            pe.transpose(g.ps[1][:, 0:24], prow2[:, :], g.c("ident")[0:24, 0:24]).then_inc(rows_t, 1)

        @block.scalar
        def _(act):
            act.wait_ge(cols, 2)
            act.activation(sig[:, :], g.pcol2[:, 0:16], ACT.Sigmoid).then_inc(sig_ok, 1)

        @block.vector
        def _(dve):
            step = Chain(dve, chain_v)
            dve.wait_ge(rows_t, 2)
            dve.tensor_copy(g.pcol[:, :], g.ps[0][:, 0:NROWS]).then_inc(cols, 1)
            dve.tensor_copy(g.pcol2[:, :], g.ps[1][:, 0:24]).then_inc(cols, 1)
            dve.wait_ge(sig_ok, 1)
            step(dve.tensor_tensor(g.cond[:, :, :].rearrange("p k j -> p j k"),
                                   g.pcol2[:, 0:16].rearrange("p (j k) -> p j k", j=2),
                                   sig[:, :].rearrange("p (j k) -> p j k", j=2), ALU.mult))
            mu = g.p("shift_mu")
            dve.tensor_scalar(g.omu[:, :], mu, -1.0, 1.0, ALU.mult, ALU.add)
            for i in range(6):
                at = CONST_AT["pick"][0] + i
                last = dve.tensor_scalar(g.mus[:, :, i], mu, g.const[:, at:at + 1], None, ALU.mult)
            step(last)


def phase_modulation(nc, g, ctx0, tag, blocks):
    RING = 3
    with ExitStack() as ctx:
        w = sb(nc, ctx, f"ada_w_{tag}", [P, RING, KT, 512])
        w_in = ring_sems(nc, ctx0, f"ada_in_{tag}", RING)
        done, taken = sems(nc, ctx0, f"ada_done_{tag}", f"ada_taken_{tag}")
        block = ctx.enter_context(nc.Block())
        adaw = g.i["ada_w"].rearrange("l (k p) n -> p (l k) n", p=P)

        @block.sync
        def _(sp):
            for n, b in enumerate(blocks):
                if n >= RING:
                    sp.wait_ge(done, n - RING + 1)
                sp.dma_start(w[:, n % RING, :, :], adaw[:, :, b * 512:(b + 1) * 512]).then_inc(w_in[n % RING], 16)

        @block.tensor
        def _(pe):
            for n, b in enumerate(blocks):
                pe.wait_ge(w_in[n % RING], 16 * (n // RING + 1))
                if n >= 2:
                    pe.wait_ge(taken, n - 1)
                for m in range(4):
                    for k in range(KT):
                        mm = pe.matmul(g.ps[n % 2][:, 2 * m:2 * m + 2], w[:, n % RING, k, m * P:(m + 1) * P],
                                       g.cond[:, k, :], start=(k == 0), stop=(k == KT - 1))
                mm.then_inc(done, 1)

        @block.vector
        def _(dve):
            for n, b in enumerate(blocks):
                dve.wait_ge(done, n + 1)
                dve.tensor_tensor(g.mod[:, 4 * b:4 * b + 4, :],
                                  g.ps[n % 2][:, 0:8].rearrange("p (m j) -> p m j", j=2),
                                  g.p("ada_b")[:, 4 * b:4 * b + 4].unsqueeze(2).to_broadcast([P, 4, 2]),
                                  ALU.add).then_inc(taken, 1)


def phase_project(nc, g, ctx0):
    NX = TA // P
    XR, WR, RR, MR = 3, 4, 4, 2
    THIRDS = ((0, 512), (512, 1024), (1024, TA))
    order = []
    for j in range(NRW):
        order.append(("rw", j))
    for i in range(4):
        order += [("b", i), ("c", i), ("u", i)]

    def column(kind, j):
        return j * P if kind == "rw" else NRW * P + "bcu".index(kind) * 512 + j * P

    NT = len(order)
    with ExitStack() as ctx:
        hT = sb(nc, ctx, "hT", [P, KT, TA])
        xin = sb(nc, ctx, "xin", [P, XR, D])
        sq = sb(nc, ctx, "x_sq", [P, D])
        ss = sb(nc, ctx, "x_ss", [P, NX])
        rs = sb(nc, ctx, "x_rs", [P, NX])
        w = sb(nc, ctx, "w_in_ring", [P, WR, KT, P])
        raw = sb(nc, ctx, "raw", [P, RR, TA])
        mix = sb(nc, ctx, "mix", [P, MR, TA])
        ksq = sb(nc, ctx, "ksq", [P, TA])
        kn = sb(nc, ctx, "kn", [P, TA])
        a1 = sb(nc, ctx, "a1", [P, KT, 2])
        xg_all = ksq
        x_in = ring_sems(nc, ctx0, "pj_x_in", XR)
        w_l = ring_sems(nc, ctx0, "pj_w_in", WR)
        stored = ring_sems(nc, ctx0, "pj_stored", 3)
        (sumsq, scaled, turned, put_v, put_a, ready, prod, copied, mixed, ksq_ok, khead, kk_ok, chain_v,
         khread, kcopied, rooted, kroot) = sems(nc, ctx0, "pj_sumsq", "pj_scaled", "pj_turned", "pj_put_v", "pj_put_a", "pj_ready", "pj_prod",
                      "pj_copied", "pj_mixed", "pj_ksq", "pj_khead", "pj_kk", "pj_chain", "pj_khread", "pj_kc", "pj_rooted", "pj_kroot")
        block = ctx.enter_context(nc.Block())
        ctx_v = g.i["ctx"].rearrange("a (t p) d -> (a t) p d", p=P)
        x_v = g.i["x"].rearrange("a (t p) d -> (a t) p d", p=P)
        win = g.i["w_in"].rearrange("l (k p) n -> p (l k) n", p=P)
        scr = g.rkv.rearrange("c p a h t -> a h p c t")

        n_rkv = 12

        @block.sync
        def _(sp):
            def load_w(n):
                kind, j = order[n]
                if n >= WR:
                    sp.wait_ge(prod, n - WR + 1)
                at = column(kind, j)
                sp.dma_start(w[:, n % WR, :, :], win[:, :, at:at + P]).then_inc(w_l[n % WR], 16)

            for i in range(NX):
                if i >= XR:
                    sp.wait_ge(turned, i - XR + 1)
                src = ctx_v[i] if i < 2 else x_v[i - 2]
                sp.dma_start(xin[:, i % XR, :], src).then_inc(x_in[i % XR], 16)
                if i == XR - 1:
                    for n in range(WR):
                        load_w(n)
            for n in range(WR, NT):
                load_w(n)

        @block.gpsimd
        def _(pool):
            for j in range(n_rkv):
                pool.wait_ge(mixed, j + 1)
                pool.dma_start(scr[j // 4, j % 4], mix[:, j % MR, :].rearrange("p (c t) -> p c t", t=C)).then_inc(stored[j % MR], 16)
                if 4 <= j < 8:
                    pool.wait_ge(kk_ok, j - 3)
                    pool.dma_start(scr[3, j % 4], kn[:, :].rearrange("p (c t) -> p c t", t=C)).then_inc(stored[2], 16)
            for r in range(MR):
                pool.wait_ge(stored[r], 16 * (n_rkv // MR))
            pool.wait_ge(stored[2], 16 * 4)

        def put_tile(act, i):
            j = 1 if i < 2 else 0
            act.wait_ge(ready, 1)
            act.wait_ge(turned, i + 1)
            for k in range(4, 8):
                last = act.activation(hT[:, k, i * P:(i + 1) * P], g.ps[2 * (i % 2) + 1][:, (k - 4) * P:(k - 3) * P],
                                      ACT.Identity, scale=a1[:, k, j:j + 1], bias=g.mod[:, k, j:j + 1])
            last.then_inc(put_a, 1)

        @block.scalar
        def _(act):
            for i in range(NX):
                act.wait_ge(x_in[i % XR], 16 * (i // XR + 1))
                act.activation(sq[:, :], xin[:, i % XR, :], ACT.Square, accum_out=ss[:, i:i + 1]).then_inc(sumsq, 1)
                act.wait_ge(sumsq, i + 1)
                act.activation(rs[:, i:i + 1], ss[:, i:i + 1], ACT.Sqrt, scale=1.0 / D, bias=g.c("eps")).then_inc(rooted, 1)
                if i >= 1:
                    put_tile(act, i - 1)
            put_tile(act, NX - 1)
            for n in range(NT):
                kind, j = order[n]
                act.wait_ge(prod, n + 1)
                if n >= RR:
                    act.wait_ge(mixed, n - RR + 1)
                a = 3 * (n % 2)
                if kind == "rw":
                    act.activation(raw[:, n % RR, 0:TC], g.ps[a][:, 0:TC], ACT.Copy)
                act.activation(raw[:, n % RR, TC:TC + 512], g.ps[a + 1][:, :], ACT.Copy)
                act.activation(raw[:, n % RR, TC + 512:TA], g.ps[a + 2][:, :], ACT.Copy).then_inc(copied, 1)
                if 5 <= n < 9:
                    for q, (lo, hi) in enumerate(THIRDS):
                        act.wait_ge(khread, 3 * (n - 5) + q + 1)
                        act.activation(ksq[:, lo:hi], ksq[:, lo:hi], ACT.Sqrt).then_inc(kroot, 1)
                if kind == "rw" and 4 <= j < 8:
                    act.wait_ge(ksq_ok, j - 3)
                    act.activation(ksq[:, :], kn[:, :], ACT.Square).then_inc(kcopied, 1)

        @block.vector
        def _(dve):
            step = Chain(dve, chain_v)
            step(dve.tensor_scalar(a1[:, :, :], g.mod[:, 8:16, :], 1.0, None, ALU.add))
            dve.tensor_tensor(a1[:, :, :], a1[:, :, :], g.p("norm1_g").unsqueeze(2).to_broadcast([P, KT, 2]), ALU.mult).then_inc(ready, 1)

            def put(i):
                j = 1 if i < 2 else 0
                dve.wait_ge(ready, 1)
                dve.wait_ge(turned, i + 1)
                for k in range(4):
                    last = dve.tensor_scalar(hT[:, k, i * P:(i + 1) * P], g.ps[2 * (i % 2)][:, k * P:(k + 1) * P],
                                             a1[:, k, j:j + 1], g.mod[:, k, j:j + 1], ALU.mult, ALU.add)
                last.then_inc(put_v, 1)

            for i in range(NX):
                dve.wait_ge(rooted, i + 1)
                step(dve.reciprocal(rs[:, i:i + 1], rs[:, i:i + 1]))
                dve.tensor_scalar(xin[:, i % XR, :], xin[:, i % XR, :], rs[:, i:i + 1], None, ALU.mult).then_inc(scaled, 1)
                if i >= 1:
                    put(i - 1)
            put(NX - 1)

            def shift(n, j, dst):
                src = raw[:, n % RR, :]
                step(dve.tensor_scalar(dst, src, g.omu[:, j:j + 1], None, ALU.mult))
                s = src[:, TC:TA].rearrange("p (r c) -> p r c", c=GRID)
                d = dst[:, TC:TA].rearrange("p (r c) -> p r c", c=GRID)
                pairs = [(d[:, :, 1:], s[:, :, :-1]), (d[:, :, :-1], s[:, :, 1:]),
                         (d[:, 1:, :], s[:, :-1, :]), (d[:, :-1, :], s[:, 1:, :]),
                         (dst[:, 1:TC], src[:, 0:TC - 1]), (dst[:, 0:TC - 1], src[:, 1:TC])]
                for i, (o, f) in enumerate(pairs):
                    ins = dve.scalar_tensor_tensor(o, f, g.mus[:, j, i:i + 1], o, ALU.mult, ALU.add)
                    if i < 5:
                        step(ins)
                return ins

            for n in range(NT):
                kind, j = order[n]
                if kind == "rw":
                    dve.wait_ge(copied, n + 1)
                    if j < 12 and j >= MR:
                        dve.wait_ge(stored[j % MR], 16 * (j // MR))
                    dst = mix[:, j % MR, :] if j < 12 else g.lora[:, :] if j == 12 else xg_all[:, :]
                    shift(n, j, dst).then_inc(mixed, 1)
                    dve.wait_ge(mixed, n + 1)
                if kind == "rw" and 4 <= j < 8:
                    h = j - 4
                    if h >= 1:
                        dve.wait_ge(stored[2], 16 * h)
                    dve.tensor_scalar(kn[:, :], dst, g.p("k_k")[:, h:h + 1], None, ALU.mult).then_inc(ksq_ok, 1)
                    dve.wait_ge(ksq_ok, h + 1)
                    for q, (lo, hi) in enumerate(THIRDS):
                        dve.wait_ge(khead, 3 * h + q + 1)
                        sl = ksq[:, lo:hi]
                        dve.tensor_scalar(sl, g.ps[6 + q % 2][:, 0:hi - lo], 1e-24, None, ALU.max).then_inc(khread, 1)
                    for q, (lo, hi) in enumerate(THIRDS):
                        sl = ksq[:, lo:hi]
                        dve.wait_ge(kroot, 3 * h + q + 1)
                        step(dve.reciprocal(sl, sl))
                        last = dve.tensor_tensor(kn[:, lo:hi], kn[:, lo:hi], sl, ALU.mult)
                    last.then_inc(kk_ok, 1)
                elif kind == "rw" and j == 13:
                    dve.tensor_copy(g.xg[:, :], xg_all[:, TC:TA])
                elif kind == "u":
                    dve.wait_ge(copied, n + 1)
                    rb, rc, ru = (raw[:, m % RR, TC:TA] for m in (n - 2, n - 1, n))
                    cw = g.p("conv_w")
                    o = g.bT[:, j, :]
                    step(dve.tensor_tensor(ru, rc, ru, ALU.mult))
                    step(dve.tensor_scalar(o, ru, cw[:, 4 + j:5 + j], None, ALU.mult))
                    step(dve.scalar_tensor_tensor(o[:, 1:], ru[:, :-1], cw[:, j:j + 1], o[:, 1:], ALU.mult, ALU.add))
                    step(dve.scalar_tensor_tensor(o[:, :-1], ru[:, 1:], cw[:, 8 + j:9 + j], o[:, :-1], ALU.mult, ALU.add))
                    dve.tensor_tensor(o, o, rb, ALU.mult).then_inc(mixed, 3)

        @block.tensor
        def _(pe):
            for i in range(NX):
                pe.wait_ge(scaled, i + 1)
                if i >= 2:
                    pe.wait_ge(put_v, i - 1)
                    pe.wait_ge(put_a, i - 1)
                for k in range(KT):
                    mm = pe.transpose(g.ps[2 * (i % 2) + k // 4][:, (k % 4) * P:(k % 4 + 1) * P],
                                      xin[:, i % XR, k * P:(k + 1) * P], g.c("ident"))
                mm.then_inc(turned, 1)
            pe.wait_ge(put_v, NX)
            pe.wait_ge(put_a, NX)
            for n in range(NT):
                kind, j = order[n]
                pe.wait_ge(w_l[n % WR], 16 * (n // WR + 1))
                if n >= 2:
                    pe.wait_ge(copied, n - 1)
                a = 3 * (n % 2)
                for k in range(KT):
                    lhsT = w[:, n % WR, k, :]
                    if kind == "rw":
                        pe.matmul(g.ps[a][:, 0:TC], lhsT, hT[:, k, 0:TC], start=(k == 0), stop=(k == KT - 1))
                    pe.matmul(g.ps[a + 1][:, :], lhsT, hT[:, k, TC:TC + 512], start=(k == 0), stop=(k == KT - 1))
                    mm = pe.matmul(g.ps[a + 2][:, :], lhsT, hT[:, k, TC + 512:TA], start=(k == 0), stop=(k == KT - 1))
                mm.then_inc(prod, 1)
                if 5 <= n < 9:
                    h = n - 5
                    pe.wait_ge(kcopied, h + 1)
                    for q, (lo, hi) in enumerate(THIRDS):
                        if 3 * h + q >= 2:
                            pe.wait_ge(khread, 3 * h + q - 1)
                        pe.matmul(g.ps[6 + q % 2][:, 0:hi - lo], g.c("head"), ksq[:, lo:hi],
                                  start=True, stop=True).then_inc(khead, 1)


def phase_wkv(nc, g, ctx0):
    NU = 4
    SS = NCH // 2
    LV = range(1, len(LEVELS))
    per_level = [f"{k}{l}" for l in LV for k in "wd"]
    names = {
        "pe": ["lora", "gram", "turn", "turnv", "l0"] + per_level + ["r0", "u", "s"],
        "dve": ["z", "cum", "feat", "gram", "l0"] + per_level + ["r0", "u", "s"],
        "act": ["sig", "exp", "xa", "turn", "turnv", "l0"] + per_level + ["u", "s"],
        "pool": ["av", "xa", "l0"] + per_level + ["u", "s"],
    }

    def at(engine, ss, name):
        return ss * len(names[engine]) + names[engine].index(name) + 1

    def step_of(ss, u):
        return 2 * ss + u // 2

    def chunk_of(ss, u):
        s = step_of(ss, u)
        return s if u % 2 == 0 else (NCC - 1 - s if s < NCC else NCH - 1 + NCC - s)

    def pairs(ap):
        return ap.rearrange("p (h n) -> p h n", h=HP)

    with ExitStack() as ctx:
        up = sb(nc, ctx, "lora_up", [P, 2, HP * P])
        unit = []
        for u in range(NU):
            b = Shared()
            b.chunk = sb(nc, ctx, f"chunk{u}", [P, 4, HP, C])
            work = sb(nc, ctx, f"work{u}", [P, 6, HP, C])
            b.sw, b.a, b.x, b.gx, b.pi, b.kd = (work[:, i] for i in range(6))
            b.z = work[:, 0:2]
            b.xg = work[:, 2:4]
            b.t, b.y, b.w1 = (work[:, i] for i in range(3))
            b.ty = work[:, 0:2]
            b.r0, b.u = work[:, 2], work[:, 0]
            b.ar = sb(nc, ctx, f"ar{u}", [P, HP, 2, C])
            b.gb = sb(nc, ctx, f"gb{u}", [P, HP, 2, C])
            b.gk = sb(nc, ctx, f"gk{u}", [P, HP, 2, C])
            b.vc = sb(nc, ctx, f"vc{u}", [P, HP, C])
            b.end = sb(nc, ctx, f"end{u}", [P, HP])
            b.abd, b.bbd, b.kbd, b.vbd, b.xbd, b.akbd, b.wbd, b.ybd = (
                sb(nc, ctx, f"{n}{u}", [P, HP, P]) for n in ("abd", "bbd", "kbd", "vbd", "xbd", "akbd", "wbd", "ybd"))
            b.ubd = b.xbd
            b.A, b.B = g.ps[2 * u], g.ps[2 * u + 1]
            unit.append(b)
        sc = [[sb(nc, ctx, f"s{d}{q}", [P, HP, C]) for q in range(2)] for d in range(2)]
        sbd = [[sb(nc, ctx, f"sbd{d}{q}", [P, HP, P]) for q in range(2)] for d in range(2)]
        chunk_in = ring_sems(nc, ctx0, "wk_chunk_in", NU)
        pe_done = ring_sems(nc, ctx0, "wk_products", NU)
        dve_done = ring_sems(nc, ctx0, "wk_vector", NU)
        act_done = ring_sems(nc, ctx0, "wk_scalar", NU)
        pool_done = ring_sems(nc, ctx0, "wk_pool", NU)
        y_done = ring_sems(nc, ctx0, "wk_y", NU)
        y_taken = ring_sems(nc, ctx0, "wk_y_taken", NU)
        up_in, zeroed, tanh_ok, chain_v, chain_a = sems(nc, ctx0, "wk_up_in", "wk_zeroed", "wk_tanh", "wk_chain", "wk_chain_a")
        block = ctx.enter_context(nc.Block())

        def nx(ss, u):
            return max(0, ss + 1 - NCC // 2)

        LO, HI = slice(0, C), slice(C, P)

        @block.sync
        def _(sp):
            for d in range(2):
                sp.dma_start(up[0:64, d, :], g.i["w_lora_up"][0, d]).then_inc(up_in, 16)
                sp.dma_start(up[64:128, d, :], g.i["a_lora_up"][0, d]).then_inc(up_in, 16)
            for ss in range(SS):
                for u in range(NU):
                    if ss >= 1:
                        sp.wait_ge(dve_done[u], at("dve", ss - 1, "feat"))
                        sp.wait_ge(pool_done[u], at("pool", ss - 1, "av"))
                    sp.dma_start(unit[u].chunk[:, :, :, :], g.rkv[chunk_of(ss, u)]).then_inc(chunk_in[u], 16)

        @block.gpsimd
        def _(pool):
            for b in unit:
                for m in (b.abd, b.bbd, b.kbd, b.vbd, b.xbd, b.akbd, b.wbd, b.ybd):
                    pool.memset(m[:, :, :], 0.0)
            for d in range(2):
                pool.memset(sc[d][0][:, :, :], 0.0)
                pool.memset(sbd[d][1][:, :, :], 0.0)
                last = pool.memset(sbd[d][0][:, :, :], 0.0)
            last.then_inc(zeroed, 1)
            pool.wait_ge(zeroed, 1)

            def high(dst, src):
                return pool.tensor_copy(dst[HI, :, HI], src[HI])

            def low(dst, src):
                return pool.tensor_copy(dst[LO, :, LO], src[LO])

            for ss in range(SS):
                for u, b in enumerate(unit):
                    pool.wait_ge(dve_done[u], at("dve", ss, "feat"))
                    for src, dst in ((b.ar[:, :, 0], b.abd), (b.chunk[:, 2], b.vbd)):
                        low(dst, src)
                        last = high(dst, src)
                    last.then_inc(pool_done[u], 1)
                for u, b in enumerate(unit):
                    pool.wait_ge(dve_done[u], at("dve", ss, "gram"))
                    high(b.xbd, b.gb[:, :, 0])
                    high(b.akbd, b.gk[:, :, 0]).then_inc(pool_done[u], 1)
                for u, b in enumerate(unit):
                    pool.wait_ge(dve_done[u], at("dve", ss, "l0"))
                    high(b.ybd, b.y).then_inc(pool_done[u], 1)
                for l in LV:
                    for u, b in enumerate(unit):
                        pool.wait_ge(dve_done[u], at("dve", ss, f"w{l}"))
                        high(b.wbd, b.w1).then_inc(pool_done[u], 1)
                    for u, b in enumerate(unit):
                        pool.wait_ge(dve_done[u], at("dve", ss, f"d{l}"))
                        high(b.ybd, b.y).then_inc(pool_done[u], 1)
                for s2 in range(2):
                    for d in range(2):
                        u, b = 2 * s2 + d, unit[2 * s2 + d]
                        pool.wait_ge(dve_done[u], at("dve", ss, "u"))
                        high(b.ubd, b.u).then_inc(pool_done[u], 1)
                    for d in range(2):
                        u = 2 * s2 + d
                        pool.wait_ge(dve_done[u], at("dve", ss, "s"))
                        high(sbd[d][1 - s2], sc[d][1 - s2]).then_inc(pool_done[u], 1)

        @block.scalar
        def _(act):
            step = Chain(act, chain_a)
            act.activation(g.lora[LO, :], g.lora[LO, :], ACT.Tanh).then_inc(tanh_ok, 1)
            act.wait_ge(zeroed, 1)

            def low(dst, src):
                return act.activation(dst[LO, :, LO], src[LO], ACT.Copy)

            for ss in range(SS):
                for u, b in enumerate(unit):
                    act.wait_ge(dve_done[u], at("dve", ss, "z"))
                    act.activation(b.z, b.z, ACT.Sigmoid).then_inc(act_done[u], 1)
                for u, b in enumerate(unit):
                    act.wait_ge(dve_done[u], at("dve", ss, "cum"))
                    step(act.activation(b.pi, b.gx, ACT.Exp, scale=KAPPA))
                    act.activation(b.xg, b.xg, ACT.Exp, scale=-KAPPA).then_inc(act_done[u], 1)
                for u, b in enumerate(unit):
                    act.wait_ge(dve_done[u], at("dve", ss, "gram"))
                    low(b.xbd, b.gb[:, :, 0])
                    low(b.akbd, b.gk[:, :, 0]).then_inc(act_done[u], 1)
                for u, b in enumerate(unit):
                    act.wait_ge(pe_done[u], at("pe", ss, "turn"))
                    act.activation(b.bbd[:, :, :], pairs(b.A[:, :]), ACT.Copy)
                    act.activation(b.kbd[:, :, :], pairs(b.B[:, :]), ACT.Copy).then_inc(act_done[u], 1)
                for u, b in enumerate(unit):
                    act.wait_ge(pe_done[u], at("pe", ss, "turnv"))
                    act.activation(b.vbd[:, :, :], pairs(b.A[:, :]), ACT.Copy)
                    act.activation(b.vc[LO], pairs(b.A[LO, :])[:, :, LO], ACT.Copy)
                    act.activation(b.vc[HI], pairs(b.A[HI, :])[:, :, HI], ACT.Copy).then_inc(act_done[u], 1)
                for u, b in enumerate(unit):
                    act.wait_ge(dve_done[u], at("dve", ss, "l0"))
                    low(b.ybd, b.y).then_inc(act_done[u], 1)
                for l in LV:
                    for u, b in enumerate(unit):
                        act.wait_ge(dve_done[u], at("dve", ss, f"w{l}"))
                        low(b.wbd, b.w1).then_inc(act_done[u], 1)
                    for u, b in enumerate(unit):
                        act.wait_ge(dve_done[u], at("dve", ss, f"d{l}"))
                        low(b.ybd, b.y).then_inc(act_done[u], 1)
                for s2 in range(2):
                    for d in range(2):
                        u, b = 2 * s2 + d, unit[2 * s2 + d]
                        act.wait_ge(dve_done[u], at("dve", ss, "u"))
                        low(b.ubd, b.u).then_inc(act_done[u], 1)
                    for d in range(2):
                        u = 2 * s2 + d
                        act.wait_ge(dve_done[u], at("dve", ss, "s"))
                        low(sbd[d][1 - s2], sc[d][1 - s2]).then_inc(act_done[u], 1)

        @block.vector
        def _(dve):
            step = Chain(dve, chain_v)

            def over_pairs(ap):
                return ap.unsqueeze(1).to_broadcast([P, HP] + list(ap.shape[1:]))

            def over_tokens(ap):
                return ap.unsqueeze(2).to_broadcast([P, HP, C])

            flat = "p h t -> p (h t)"
            for ss in range(SS):
                for u, b in enumerate(unit):
                    d = u % 2
                    dve.wait_ge(pe_done[u], at("pe", ss, "lora"))
                    if ss >= 1:
                        dve.wait_ge(act_done[u], at("act", ss - 1, "u"))
                        dve.wait_ge(pool_done[u], at("pool", ss - 1, "u"))
                    for bank, dst, bias in ((b.A, b.sw, g.p("w0")), (b.B, b.a, g.p("a0"))):
                        last = dve.tensor_tensor(dst, pairs(bank[:, 0:HP * C]), over_tokens(bias[:, d * HP:(d + 1) * HP]), ALU.add)
                    last.then_inc(dve_done[u], 1)
                for u, b in enumerate(unit):
                    d = u % 2
                    dve.wait_ge(act_done[u], at("act", ss, "sig"))
                    run = b.gx if d == 0 else b.kd
                    step(dve.tensor_tensor_scan(run.rearrange(flat), g.c("chunk"), b.sw.rearrange(flat), 0.0, ALU.mult, ALU.add))
                    if d == 0:
                        step(dve.tensor_tensor(b.x, run, b.sw, ALU.subtract))
                    else:
                        step(dve.tensor_tensor(b.x, over_tokens(run[:, :, C - 1]), run, ALU.subtract))
                        step(dve.tensor_tensor(b.gx, b.x, b.sw, ALU.add))
                    dve.wait_ge(chunk_in[u], 16 * (ss + 1))
                    step(dve.scalar_tensor_tensor(b.kd, b.a, -1.0, over_tokens(g.p("k_a")), ALU.add, ALU.mult))
                    dve.scalar_tensor_tensor(b.kd, b.kd, 1.0, b.chunk[:, 1], ALU.add, ALU.mult).then_inc(dve_done[u], 1)
                if ss == 0:
                    dve.wait_ge(zeroed, 1)
                for u, b in enumerate(unit):
                    d = u % 2
                    dve.wait_ge(act_done[u], at("act", ss, "exp"))
                    dve.wait_ge(dve_done[u], at("dve", ss, "cum"))
                    dve.scalar_tensor_tensor(b.ar[:, :, 0], b.chunk[:, 3], -1.0, b.x, ALU.mult, ALU.mult)
                    dve.tensor_tensor(b.ar[:, :, 1], b.chunk[:, 0], b.gx, ALU.mult)
                    dve.tensor_copy(b.end[:, :], b.gx[:, :, C - 1 if d == 0 else 0])
                    step(dve.tensor_tensor(b.sw, b.a, b.pi, ALU.mult))
                    for h in (LO, HI):
                        dve.tensor_tensor(b.bbd[h, :, h], b.chunk[h, 3], b.sw[h], ALU.mult)
                        last = dve.tensor_tensor(b.kbd[h, :, h], b.kd[h], b.pi[h], ALU.mult)
                    last.then_inc(dve_done[u], 1)
                for u, b in enumerate(unit):
                    mask = g.c("maskf" if u % 2 == 0 else "maskb")
                    dve.wait_ge(pe_done[u], at("pe", ss, "gram"))
                    for bank, dst in ((b.A, b.gb), (b.B, b.gk)):
                        last = dve.tensor_tensor(dst[:, :, :, :].rearrange("p h a t -> p h (a t)"),
                                                 pairs(bank[:, :]), over_pairs(mask), ALU.mult)
                    last.then_inc(dve_done[u], 1)
                for u, b in enumerate(unit):
                    one, lev = over_pairs(g.c("stack")), over_pairs(g.c("lev1"))
                    dve.wait_ge(pe_done[u], at("pe", ss, "l0"))
                    dve.tensor_tensor(b.t, pairs(b.B[:, 0:HP * C]), lev, ALU.mult)
                    step(dve.tensor_tensor(b.y, b.gb[:, :, 0], lev, ALU.mult))
                    dve.tensor_tensor(b.t, b.t, one, ALU.add)
                    dve.tensor_tensor(b.y, b.y, one, ALU.add).then_inc(dve_done[u], 1)
                for l in LV:
                    lev = over_pairs(g.c(f"lev{LEVELS[l]}"))
                    for u, b in enumerate(unit):
                        dve.wait_ge(pe_done[u], at("pe", ss, f"w{l}"))
                        dve.tensor_tensor(b.w1, pairs(b.A[:, 0:HP * C]), lev, ALU.mult).then_inc(dve_done[u], 1)
                    for u, b in enumerate(unit):
                        dve.wait_ge(pe_done[u], at("pe", ss, f"d{l}"))
                        if l < LV[-1]:
                            dve.tensor_tensor(b.ty.rearrange("p k h t -> p (k h t)"), b.ty.rearrange("p k h t -> p (k h t)"),
                                              b.B[:, :], ALU.add).then_inc(dve_done[u], 1)
                        else:
                            dve.tensor_tensor(b.y, b.y, pairs(b.B[:, HP * C:]), ALU.add).then_inc(dve_done[u], 1)
                for s2 in range(2):
                    for d in range(2):
                        u, b = 2 * s2 + d, unit[2 * s2 + d]
                        dve.wait_ge(pe_done[u], at("pe", ss, "r0"))
                        dve.tensor_copy(b.r0, pairs(b.A[:, 0:HP * C])).then_inc(dve_done[u], 1)
                    for d in range(2):
                        u, b = 2 * s2 + d, unit[2 * s2 + d]
                        dve.wait_ge(pe_done[u], at("pe", ss, "u"))
                        dve.tensor_copy(b.u, pairs(b.B[:, 0:HP * C])).then_inc(dve_done[u], 1)
                    for d in range(2):
                        u, b = 2 * s2 + d, unit[2 * s2 + d]
                        new = sc[d][1 - s2]
                        dve.wait_ge(pe_done[u], at("pe", ss, "s"))
                        step(dve.tensor_tensor(new[:, :, :], pairs(b.A[:, 0:HP * C]), sc[d][s2][:, :, :], ALU.add))
                        dve.tensor_tensor(new[:, :, :], new[:, :, :], over_tokens(b.end[:, :]), ALU.mult).then_inc(dve_done[u], 1)
                    for d in range(2):
                        u, b = 2 * s2 + d, unit[2 * s2 + d]
                        s, c = step_of(ss, u), chunk_of(ss, u) - NCC
                        if s < NCC:
                            continue
                        dst = g.yT[:, :, c * C:(c + 1) * C]
                        dve.wait_ge(y_done[u], nx(ss, u))
                        if s < NCC + (NCH - NCC) // 2:
                            dve.tensor_copy(dst, pairs(b.B[:, 0:HP * C])).then_inc(y_taken[u], 1)
                        else:
                            if s == NCC + (NCH - NCC) // 2:
                                for q in range(NU):
                                    if nx(ss - 1, q):
                                        dve.wait_ge(y_taken[q], nx(ss - 1, q))
                            dve.tensor_tensor(dst, dst, pairs(b.B[:, 0:HP * C]), ALU.add).then_inc(y_taken[u], 1)

        @block.tensor
        def _(pe):
            def compact(bank, h, k=0):
                return bank[:, k * HP * C + h * C:k * HP * C + (h + 1) * C]

            def each(bank, k, *terms):
                for h in range(HP):
                    for i, (st, mv) in enumerate(terms):
                        mm = pe.matmul(compact(bank, h, k), st[:, h], mv[:, h], start=(i == 0), stop=(i == len(terms) - 1))
                return mm

            pe.wait_ge(up_in, 64)
            pe.wait_ge(tanh_ok, 1)
            for ss in range(SS):
                for u, b in enumerate(unit):
                    d, at0 = u % 2, chunk_of(ss, u) * C
                    if ss >= 1:
                        pe.wait_ge(dve_done[u], at("dve", ss - 1, "s"))
                        if nx(ss - 1, u):
                            pe.wait_ge(y_taken[u], nx(ss - 1, u))
                    for bank, h in ((b.A, LO), (b.B, HI)):
                        for hp in range(HP):
                            mm = pe.matmul(compact(bank, hp), up[h, d, hp * P:(hp + 1) * P], g.lora[h, at0:at0 + C],
                                           start=True, stop=True)
                    mm.then_inc(pe_done[u], 1)
                for u, b in enumerate(unit):
                    pe.wait_ge(dve_done[u], at("dve", ss, "feat"))
                    for bank, st in ((b.A, b.bbd), (b.B, b.kbd)):
                        for hp in range(HP):
                            mm = pe.matmul(bank[:, hp * P:(hp + 1) * P], st[:, hp], b.ar[:, hp].rearrange("p a t -> p (a t)"),
                                           start=True, stop=True)
                    mm.then_inc(pe_done[u], 1)
                for u, b in enumerate(unit):
                    pe.wait_ge(dve_done[u], at("dve", ss, "gram"))
                    for bank, st in ((b.A, b.bbd), (b.B, b.kbd)):
                        for hp in range(HP):
                            mm = pe.transpose(bank[:, hp * P:(hp + 1) * P], st[:, hp], g.c("ident"))
                    mm.then_inc(pe_done[u], 1)
                for u, b in enumerate(unit):
                    pe.wait_ge(act_done[u], at("act", ss, "turn"))
                    pe.wait_ge(pool_done[u], at("pool", ss, "av"))
                    for hp in range(HP):
                        mm = pe.transpose(b.A[:, hp * P:(hp + 1) * P], b.vbd[:, hp], g.c("ident"))
                    mm.then_inc(pe_done[u], 1)
                for u, b in enumerate(unit):
                    pe.wait_ge(pool_done[u], at("pool", ss, "xa"))
                    for hp in range(HP):
                        mm = pe.matmul(compact(b.B, hp), b.xbd[:, hp], g.c("stack"), start=True, stop=True)
                    mm.then_inc(pe_done[u], 1)
                for l in LV:
                    for u, b in enumerate(unit):
                        pe.wait_ge(dve_done[u], at("dve", ss, "l0" if l == 1 else f"d{l - 1}"))
                        if l == 1:
                            pe.wait_ge(act_done[u], at("act", ss, "turnv"))
                        each(b.A, 0, (b.xbd, b.t)).then_inc(pe_done[u], 1)
                    for u, b in enumerate(unit):
                        pe.wait_ge(act_done[u], at("act", ss, f"w{l}"))
                        pe.wait_ge(pool_done[u], at("pool", ss, f"w{l}"))
                        if l < LV[-1]:
                            each(b.B, 0, (b.ybd, b.w1))
                        each(b.B, 1, (b.wbd, b.y)).then_inc(pe_done[u], 1)
                for s2 in range(2):
                    for d in range(2):
                        u, b = 2 * s2 + d, unit[2 * s2 + d]
                        o, last = (u + 2) % 4, (ss if s2 else ss - 1)
                        if last >= 0:
                            pe.wait_ge(dve_done[o], at("dve", last, "s"))
                        pe.wait_ge(act_done[u], at("act", ss, f"d{LV[-1]}"))
                        pe.wait_ge(pool_done[u], at("pool", ss, f"d{LV[-1]}"))
                        each(b.A, 0, (b.abd, sc[d][s2]), (b.akbd, b.vc)).then_inc(pe_done[u], 1)
                    for d in range(2):
                        u, b = 2 * s2 + d, unit[2 * s2 + d]
                        pe.wait_ge(dve_done[u], at("dve", ss, "r0"))
                        each(b.B, 0, (b.ybd, b.r0)).then_inc(pe_done[u], 1)
                    for d in range(2):
                        u, b = 2 * s2 + d, unit[2 * s2 + d]
                        pe.wait_ge(dve_done[u], at("dve", ss, "u"))
                        each(b.A, 0, (b.bbd, b.u), (b.kbd, b.vc)).then_inc(pe_done[u], 1)
                    for d in range(2):
                        u, b = 2 * s2 + d, unit[2 * s2 + d]
                        if step_of(ss, u) < NCC:
                            continue
                        o, last = (u + 2) % 4, (ss if s2 else ss - 1)
                        pe.wait_ge(act_done[o], at("act", last, "s"))
                        pe.wait_ge(pool_done[o], at("pool", last, "s"))
                        pe.wait_ge(act_done[u], at("act", ss, "u"))
                        pe.wait_ge(pool_done[u], at("pool", ss, "u"))
                        each(b.B, 0, (sbd[d][s2], b.ar[:, :, 1]), (b.ubd, b.gb[:, :, 1]), (b.vbd, b.gk[:, :, 1])).then_inc(y_done[u], 1)


def phase_heads_out(nc, g, ctx0):
    HALF = T // 2
    NP_ = 2 * HP
    pieces = [(hp, q) for hp in range(HP) for q in range(2)]
    kinds = ["mean"] * NP_ + ["a0", "a1"] * NP_ + ["gate"] * NP_ + ["var"] * NP_ + ["bonus"] * NP_
    seq, seen = {}, {}
    for q, kind in enumerate(kinds):
        seq[kind, seen.get(kind, 0)] = q
        seen[kind] = seen.get(kind, 0) + 1
    with ExitStack() as ctx:
        up = sb(nc, ctx, "lora_up2", [P, 2, HP * P])
        gup = sb(nc, ctx, "g_up", [P, HP * P])
        rk = sb(nc, ctx, "rkv_back", [P, NCH - NCC, 3, HP, C])
        sq = sb(nc, ctx, "gn_sq", [P, HP, T])
        gt = sb(nc, ctx, "gate_t", [P, HP, T])
        rks = sb(nc, ctx, "rks", [P, HP, T])
        sa = sb(nc, ctx, "sig_a", [P, 2, 2, HALF])
        loaded, rk_in, chain_v = sems(nc, ctx0, "ho_loaded", "ho_rkv_in", "ho_chain")
        done = {k: ctx0.new(f"ho_{k}") for k in ("mean", "a", "gate", "var", "bonus")}
        free = ring_sems(nc, ctx0, "ho_bank_free", 8)
        xg_ok, sig_a, a_read, squared, rooted, gated, rks_ok = sems(
            nc, ctx0, "ho_xg", "ho_sig_a", "ho_a_read", "ho_squared", "ho_rooted", "ho_gated", "ho_rks")
        block = ctx.enter_context(nc.Block())

        def bank(kind, i):
            return seq[kind, i] % 8

        def tok(t, i):
            hp, q = pieces[i]
            return t[:, hp, q * HALF:(q + 1) * HALF]

        def chunks(i, a):
            hp, q = pieces[i]
            n = (NCH - NCC) // 2
            return rk[:, q * n:(q + 1) * n, a, hp, :]

        def ch(ap):
            return ap.rearrange("p (c t) -> p c t", t=C)

        @block.sync
        def _(sp):
            for d in range(2):
                sp.dma_start(up[64:128, d, :], g.i["a_lora_up"][0, d]).then_inc(loaded, 16)
            sp.dma_start(gup[:, :], g.i["g_lora_up"][0]).then_inc(loaded, 16)
            sp.dma_start(rk[:, :, :, :, :], g.rkv[NCC:NCH, :, 0:3].rearrange("c p a h t -> p c a h t")).then_inc(rk_in, 16)

        @block.tensor
        def _(pe):
            def into(kind, i):
                q = seq[kind, i]
                if q >= 8:
                    pe.wait_ge(free[q % 8], q // 8)
                return g.ps[q % 8][:, 0:HALF]

            for i in range(NP_):
                pe.matmul(into("mean", i), g.c("head"), tok(g.yT, i), start=True, stop=True).then_inc(done["mean"], 1)
            pe.wait_ge(loaded, 48)
            for i, (hp, q) in enumerate(pieces):
                for d in range(2):
                    pe.matmul(into(f"a{d}", i), up[64:128, d, hp * P:(hp + 1) * P],
                              g.lora[64:128, TC + q * HALF:TC + (q + 1) * HALF], start=True, stop=True).then_inc(done["a"], 1)
            pe.wait_ge(xg_ok, 1)
            for i, (hp, q) in enumerate(pieces):
                pe.matmul(into("gate", i), gup[:, hp * P:(hp + 1) * P], g.xg[:, q * HALF:(q + 1) * HALF],
                          start=True, stop=True).then_inc(done["gate"], 1)
            for i in range(NP_):
                pe.wait_ge(squared, i + 1)
                pe.matmul(into("var", i), g.c("head"), tok(sq, i), start=True, stop=True).then_inc(done["var"], 1)
            for i in range(NP_):
                pe.wait_ge(rks_ok, i + 1)
                pe.matmul(into("bonus", i), g.c("head"), tok(rks, i), start=True, stop=True).then_inc(done["bonus"], 1)

        @block.scalar
        def _(act):
            act.activation(g.xg[:, :], g.xg[:, :], ACT.Sigmoid).then_inc(xg_ok, 1)
            for i, (hp, q) in enumerate(pieces):
                if i >= 2:
                    act.wait_ge(a_read, i - 1)
                for d in range(2):
                    act.wait_ge(done["a"], 2 * i + d + 1)
                    b = bank(f"a{d}", i)
                    act.activation(sa[:, i % 2, d, :], g.ps[b][:, :], ACT.Sigmoid,
                                   bias=g.p("a0")[:, d * HP + hp:d * HP + hp + 1]).then_inc(free[b], 1)
            for i in range(NP_):
                act.wait_ge(done["gate"], i + 1)
                act.activation(tok(gt, i), g.ps[bank("gate", i)][:, :], ACT.Copy).then_inc(free[bank("gate", i)], 1)
            for i in range(NP_):
                act.wait_ge(free[bank("mean", i)], seq["mean", i] // 8 + 1)
                act.activation(tok(sq, i), tok(g.yT, i), ACT.Square).then_inc(squared, 1)
            for i in range(NP_):
                act.wait_ge(done["var"], i + 1)
                act.activation(tok(sq, i), g.ps[bank("var", i)][:, :], ACT.Sqrt, scale=1.0 / HD, bias=g.c("gn_eps")).then_inc(free[bank("var", i)], 1)

        @block.vector
        def _(dve):
            step = Chain(dve, chain_v)
            for i in range(NP_):
                b = bank("mean", i)
                dve.wait_ge(done["mean"], i + 1)
                dve.scalar_tensor_tensor(tok(g.yT, i), g.ps[b][:, :], -1.0 / HD, tok(g.yT, i), ALU.mult, ALU.add).then_inc(free[b], 1)
            dve.wait_ge(rk_in, 16)
            for i, (hp, q) in enumerate(pieces):
                dve.wait_ge(free[bank("a1", i)], seq["a1", i] // 8 + 1)
                dve.wait_ge(free[bank("a0", i)], seq["a0", i] // 8 + 1)
                o = tok(rks, i)
                dve.tensor_tensor(o, sa[:, i % 2, 0, :], sa[:, i % 2, 1, :], ALU.add).then_inc(a_read, 1)
                dve.wait_ge(a_read, i + 1)
                step(dve.tensor_scalar(o, o, -2.0, g.p("k_a")[:, hp:hp + 1], ALU.add, ALU.mult))
                step(dve.scalar_tensor_tensor(ch(o), ch(o), 2.0, chunks(i, 1), ALU.add, ALU.mult))
                dve.scalar_tensor_tensor(ch(o), ch(o), g.p("r_k")[:, hp:hp + 1], chunks(i, 0), ALU.mult, ALU.mult).then_inc(rks_ok, 1)
            for i, (hp, q) in enumerate(pieces):
                b, o, s = bank("var", i), tok(g.yT, i), tok(sq, i)
                dve.wait_ge(free[b], seq["var", i] // 8 + 1)
                step(dve.reciprocal(s, s))
                step(dve.tensor_tensor(o, o, s, ALU.mult))
                step(dve.tensor_scalar(o, o, g.p("gn_g")[:, hp:hp + 1], g.p("gn_b")[:, hp:hp + 1], ALU.mult, ALU.add))
                b = bank("bonus", i)
                dve.wait_ge(done["bonus"], i + 1)
                step(dve.tensor_tensor(ch(s), ch(g.ps[b][:, :]), chunks(i, 2), ALU.mult))
                step(dve.tensor_tensor(o, o, s, ALU.add))
                dve.wait_ge(free[bank("gate", i)], seq["gate", i] // 8 + 1)
                step(dve.tensor_tensor(o, o, tok(gt, i), ALU.mult))


def phase_mix_out(nc, g, ctx0):
    with ExitStack() as ctx:
        wo = sb(nc, ctx, "w_out_sb", [P, KT, D])
        ones = sb(nc, ctx, "ones", [P, P])
        diag = sb(nc, ctx, "diag", [P, 4, P])
        g1 = sb(nc, ctx, "g1_row", [P, D])
        xin = sb(nc, ctx, "x_again", [P, 2, D])
        x1 = sb(nc, ctx, "x1", [P, 2, D])
        sq = sb(nc, ctx, "x1_sq", [P, D])
        ss = sb(nc, ctx, "x1_ss", [P, TT])
        rs = sb(nc, ctx, "x1_rs", [P, TT])
        xn = sb(nc, ctx, "x1n", [P, 2, D])
        h2 = sb(nc, ctx, "h2T", [P, 2, KT, P])
        rw = sb(nc, ctx, "router", [P, KT, NE])
        aff = sb(nc, ctx, "aff", [P, TT, NE])
        mx = sb(nc, ctx, "aff_max", [P, TT])
        affT = sb(nc, ctx, "affT", [NE, T])
        vals = sb(nc, ctx, "vals", [NE, CAP])
        idx = sb(nc, ctx, "idx", [NE, CAP], U32)
        idxf = sb(nc, ctx, "idxf", [NE, CAP])
        wo_in, rw_in, row_ok, row_done, gcols, chain_v, chain_a = sems(
            nc, ctx0, "mo_w_in", "mo_router_in", "mo_row", "mo_row_done", "mo_cols", "mo_chain", "mo_chain_a")
        x_in = ring_sems(nc, ctx0, "mo_x_in", 2)
        st1 = ring_sems(nc, ctx0, "mo_x1_out", 2)
        stn = ring_sems(nc, ctx0, "mo_xn_out", 2)
        prod, x1_ok, sumsq, xn_ok, turned, h2_ok, logit, ex_ok, shifted, aff_ok, aff_t, top, top_t, diag_ok = sems(
            nc, ctx0, "mo_prod", "mo_x1", "mo_sumsq", "mo_xn", "mo_turned", "mo_h2", "mo_logits", "mo_exp", "mo_shifted",
            "mo_aff", "mo_aff_turned", "mo_top", "mo_top_turned", "mo_diag")
        block = ctx.enter_context(nc.Block())
        x_v = g.i["x"].rearrange("a (t p) d -> (a t) p d", p=P)
        x1_v = g.x1_rows.rearrange("(t p) d -> t p d", p=P)
        xn_v = g.xn_rows.rearrange("(t p) d -> t p d", p=P)

        def store(sp, t):
            sp.wait_ge(x1_ok, t + 1)
            sp.dma_start(x1_v[t], x1[:, t % 2, :]).then_inc(st1[t % 2], 16)
            sp.wait_ge(xn_ok, t + 1)
            sp.dma_start(xn_v[t], xn[:, t % 2, :]).then_inc(stn[t % 2], 16)

        @block.sync
        def _(sp):
            sp.dma_start(wo[:, :, :], g.i["w_out"].rearrange("l (k p) n -> p (l k) n", p=P)).then_inc(wo_in, 16)
            sp.dma_start(rw[:, :, :], g.i["router_w"].rearrange("l (k p) n -> p (l k) n", p=P)).then_inc(rw_in, 16)
            for t in range(TT):
                if t >= 2:
                    sp.wait_ge(x1_ok, t - 1)
                sp.dma_start(xin[:, t % 2, :], x_v[t]).then_inc(x_in[t % 2], 16)
                if t >= 1:
                    store(sp, t - 1)
            store(sp, TT - 1)
            for r in range(2):
                sp.wait_ge(st1[r], 16 * TT // 2)
                sp.wait_ge(stn[r], 16 * TT // 2)

        @block.tensor
        def _(pe):
            pe.wait_ge(row_ok, 1)
            for n in range(4):
                pe.wait_ge(diag_ok, n + 1)
                if n >= 2:
                    pe.wait_ge(row_done, n - 1)
                for k in range(4):
                    mm = pe.matmul(g.ps[n % 2][:, k * P:(k + 1) * P], ones[:, :], diag[:, k, :], start=True, stop=True)
                mm.then_inc(gcols, 1)
            pe.wait_ge(row_done, 4)

            def turn(t):
                pe.wait_ge(xn_ok, t + 1)
                if t >= 1:
                    pe.wait_ge(h2_ok, t)
                for k in range(KT):
                    mm = pe.transpose(g.ps[4 + k // 4][:, (k % 4) * P:(k % 4 + 1) * P], xn[:, t % 2, k * P:(k + 1) * P], g.c("ident"))
                mm.then_inc(turned, 1)

            def route(t):
                pe.wait_ge(h2_ok, t + 1)
                for k in range(KT):
                    mm = pe.matmul(g.ps[6][:, t * NE:(t + 1) * NE], h2[:, t % 2, k, :], rw[:, k, :], start=(k == 0), stop=(k == KT - 1))
                mm.then_inc(logit, 1)

            pe.wait_ge(wo_in, 16)
            pe.wait_ge(rw_in, 16)
            for t in range(TT):
                if t >= 2:
                    pe.wait_ge(x1_ok, t - 1)
                for k in range(KT):
                    lhsT = (g.yT if k < 4 else g.bT)[:, k % 4, t * P:(t + 1) * P]
                    for h in range(2):
                        mm = pe.matmul(g.ps[2 * (t % 2) + h][:, :], lhsT, wo[:, k, h * 512:(h + 1) * 512], start=(k == 0), stop=(k == KT - 1))
                mm.then_inc(prod, 1)
                if t >= 1:
                    turn(t - 1)
                if t >= 2:
                    route(t - 2)
            turn(TT - 1)
            route(TT - 2)
            route(TT - 1)
            pe.wait_ge(aff_ok, 1)
            for t in range(TT):
                mm = pe.transpose(g.ps[t // 4][0:NE, (t % 4) * P:(t % 4 + 1) * P], aff[:, t, :], g.c("ident"))
            mm.then_inc(aff_t, 1)
            pe.wait_ge(top, 1)
            pe.transpose(g.ps[2][:, 0:NE], vals[:, :], g.c("ident")[0:NE, 0:NE])
            pe.transpose(g.ps[2][:, NE:2 * NE], idxf[:, :], g.c("ident")[0:NE, 0:NE]).then_inc(top_t, 1)

        @block.scalar
        def _(act):
            for t in range(TT):
                act.wait_ge(x1_ok, t + 1)
                act.activation(sq[:, :], x1[:, t % 2, :], ACT.Square, accum_out=ss[:, t:t + 1]).then_inc(chain_a, 1)
                act.wait_ge(chain_a, t + 1)
                act.activation(rs[:, t:t + 1], ss[:, t:t + 1], ACT.Sqrt, scale=1.0 / D, bias=g.c("eps")).then_inc(sumsq, 1)
                act.wait_ge(turned, t + 1)
                if t >= 2:
                    act.wait_ge(logit, t - 1)
                for k in range(KT):
                    last = act.activation(h2[:, t % 2, k, :], g.ps[4 + k // 4][:, (k % 4) * P:(k % 4 + 1) * P], ACT.Identity,
                                          scale=g.a2[:, k:k + 1], bias=g.mod[:, 24 + k, 0:1])
                last.then_inc(h2_ok, 1)
            act.wait_ge(shifted, 1)
            act.activation(aff[:, :, :], aff[:, :, :], ACT.Exp).then_inc(ex_ok, 1)

        @block.vector
        def _(dve):
            step = Chain(dve, chain_v)
            dve.memset(ones[:, :], 1.0).then_inc(row_ok, 1)
            for n in range(4):
                base = (16, 20, 40, 44)[n]
                if n >= 1:
                    dve.wait_ge(gcols, n)
                for k in range(4):
                    last = dve.tensor_scalar(diag[:, k, :], g.c("ident"), g.mod[:, base + k, 0:1], None, ALU.mult)
                last.then_inc(diag_ok, 1)
                dve.wait_ge(gcols, n + 1)
                dst = g1 if n < 2 else g.g2
                dve.tensor_copy(dst[:, (n % 2) * 512:(n % 2 + 1) * 512], g.ps[n % 2][:, :]).then_inc(row_done, 1)
            dve.wait_ge(row_done, 4)
            step(dve.tensor_scalar(g.a2[:, :], g.mod[:, 32:40, 0], 1.0, None, ALU.add))
            step(dve.tensor_tensor(g.a2[:, :], g.a2[:, :], g.p("norm2_g"), ALU.mult))
            for t in range(TT):
                dve.wait_ge(prod, t + 1)
                dve.wait_ge(x_in[t % 2], 16 * (t // 2 + 1))
                if t >= 2:
                    dve.wait_ge(st1[t % 2], 16 * (t // 2))
                    dve.wait_ge(stn[t % 2], 16 * (t // 2))
                for h in range(2):
                    w = slice(h * 512, (h + 1) * 512)
                    last = dve.tensor_tensor(x1[:, t % 2, w], g.ps[2 * (t % 2) + h][:, :], g1[:, w], ALU.mult)
                step(last)
                dve.tensor_tensor(x1[:, t % 2, :], x1[:, t % 2, :], xin[:, t % 2, :], ALU.add).then_inc(x1_ok, 1)
                dve.wait_ge(sumsq, t + 1)
                if t >= 2:
                    dve.wait_ge(turned, t - 1)
                step(dve.reciprocal(rs[:, t:t + 1], rs[:, t:t + 1]))
                dve.tensor_scalar(xn[:, t % 2, :], x1[:, t % 2, :], rs[:, t:t + 1], None, ALU.mult).then_inc(xn_ok, 1)
            dve.wait_ge(logit, TT)
            lg = g.ps[6][:, 0:TT * NE].rearrange("p (t e) -> p t e", e=NE)

            def wide(ap):
                return ap.unsqueeze(2).to_broadcast([P, TT, NE])

            step(dve.tensor_reduce(mx[:, :], lg, AX, ALU.max))
            dve.tensor_tensor(aff[:, :, :], lg, wide(mx[:, :]), ALU.subtract).then_inc(shifted, 1)
            dve.wait_ge(ex_ok, 1)
            step(dve.tensor_reduce(mx[:, :], aff[:, :, :], AX, ALU.add))
            step(dve.reciprocal(mx[:, :], mx[:, :]))
            dve.tensor_tensor(aff[:, :, :], aff[:, :, :], wide(mx[:, :]), ALU.mult).then_inc(aff_ok, 1)
            dve.wait_ge(aff_t, 1)
            dve.tensor_copy(affT[:, 0:512], g.ps[0][0:NE, :])
            step(dve.tensor_copy(affT[:, 512:T], g.ps[1][0:NE, :]))
            for r in range(CAP // 8):
                v = vals[:, 8 * r:8 * r + 8]
                step(dve.max(v, affT[:, :]))
                step(dve.max_index(idx[:, 8 * r:8 * r + 8], v, affT[:, :]))
                step(dve.match_replace(affT[:, :], v, affT[:, :], -1.0))
            dve.tensor_copy(idxf[:, :], idx[:, :]).then_inc(top, 1)
            dve.wait_ge(top_t, 1)
            dve.tensor_copy(g.valsT[:, :], g.ps[2][:, 0:NE])
            dve.tensor_copy(g.idxT[:, :], g.ps[2][:, NE:2 * NE])


def phase_experts(nc, g, ctx0):
    RING = 7
    HALF = KT // 2
    loads = []
    for e in range(NE):
        loads += [("gate", e, 0), ("gate", e, 1), ("up", e, 0), ("up", e, 1)]
        if e >= 1:
            loads += [("down", e - 1, 0), ("down", e - 1, 1)]
    loads += [("down", NE - 1, 0), ("down", NE - 1, 1)]
    place = {x: n for n, x in enumerate(loads)}
    with ExitStack() as ctx:
        w = sb(nc, ctx, "exp_w", [P, RING, HALF, D])
        xs = sb(nc, ctx, "xs", [P, 2, D])
        xsT = sb(nc, ctx, "xsT", [P, KT, P])
        sg = sb(nc, ctx, "sg", [P, D])
        hid = sb(nc, ctx, "hid", [P, D])
        hidT = sb(nc, ctx, "hidT", [P, KT, P])
        o = sb(nc, ctx, "exp_out", [P, 2, D])
        zero = sb(nc, ctx, "zero_row", [P, D])
        w_in = ring_sems(nc, ctx0, "ex_w_in", RING)
        x_in = ring_sems(nc, ctx0, "ex_x_in", 2)
        w_read, xs_t, xs_ok, sig, gs, hid_ok, hid_t, hidT_ok, o_ok, added, zeroed, z_ok = sems(
            nc, ctx0, "ex_w_read", "ex_xs_turned", "ex_xsT", "ex_sig", "ex_gs", "ex_hid", "ex_hid_turned",
            "ex_hidT", "ex_out", "ex_added", "ex_zeroed", "ex_zero_row")
        block = ctx.enter_context(nc.Block())
        def after(kind, e):
            return place[kind, e, 1] + 1

        src = {"gate": g.i["exp_w_gate"], "up": g.i["exp_w_up"], "down": g.i["exp_w_down"]}

        @block.sync
        def _(sp):
            for n, (kind, e, h) in enumerate(loads):
                if n >= RING:
                    sp.wait_ge(w_read, n - RING + 1)
                sp.dma_start(w[:, n % RING, :, :], src[kind][0, e].rearrange("(k p) n -> p k n", p=P)[:, h * HALF:(h + 1) * HALF, :]).then_inc(w_in[n % RING], 16)

        @block.gpsimd
        def _(pool):
            def gather(e):
                if e >= 2:
                    pool.wait_ge(xs_t, e - 1)
                pool.indirect_dma_start(xs[:, e % 2, :], None, g.xn_rows, bass.IndirectOffsetOnAxis(ap=g.idxT[:, e:e + 1], axis=0)).then_inc(x_in[e % 2], 16)

            gather(0)
            gather(1)
            pool.memset(zero[:, :], 0.0).then_inc(z_ok, 1)
            pool.wait_ge(z_ok, 1)
            moe_v = g.moe.rearrange("(t p) d -> t p d", p=P)
            for t in range(TT):
                pool.dma_start(moe_v[t], zero[:, :]).then_inc(zeroed, 16)
            pool.wait_ge(zeroed, 16 * TT)
            for e in range(NE):
                if e + 2 < NE:
                    gather(e + 2)
                pool.wait_ge(o_ok, e + 1)
                if e >= 1:
                    pool.wait_ge(added, 16 * e)
                pool.indirect_dma_start(g.moe, bass.IndirectOffsetOnAxis(ap=g.idxT[:, e:e + 1], axis=0), o[:, e % 2, :], None,
                                        compute_op=ALU.add).then_inc(added, 16)
            pool.wait_ge(added, 16 * NE)

        @block.tensor
        def _(pe):
            def turn_xs(e):
                pe.wait_ge(x_in[e % 2], 16 * (e // 2 + 1))
                if e >= 2:
                    pe.wait_ge(hidT_ok, e - 1)
                v = xs[:, e % 2, :].rearrange("p (k q) -> p k q", k=KT)
                for k in range(KT):
                    mm = pe.transpose(g.ps[k // 4][:, (k % 4) * P:(k % 4 + 1) * P], v[:, k], g.c("ident"))
                mm.then_inc(xs_t, 1)

            def turn_hid(e):
                pe.wait_ge(hid_ok, e + 1)
                if e + 1 < NE:
                    pe.wait_ge(xs_ok, e + 2)
                v = hid[:, :].rearrange("p (k q) -> p k q", k=KT)
                for k in range(KT):
                    mm = pe.transpose(g.ps[k // 4][:, (k % 4) * P:(k % 4 + 1) * P], v[:, k], g.c("ident"))
                mm.then_inc(hid_t, 1)

            def product(kind, e, bank, lhs):
                for h in range(2):
                    n = place[kind, e, h]
                    pe.wait_ge(w_in[n % RING], 16 * (n // RING + 1))
                    for k in range(HALF):
                        kk = h * HALF + k
                        for q in range(2):
                            mm = pe.matmul(g.ps[bank + q][:, :], lhs[:, kk, :], w[:, n % RING, k, q * 512:(q + 1) * 512],
                                           start=(kk == 0), stop=(kk == KT - 1))
                    mm.then_inc(w_read, 1)

            turn_xs(0)
            for e in range(NE + 1):
                if e < NE:
                    pe.wait_ge(xs_ok, e + 1)
                    if e >= 1:
                        pe.wait_ge(hid_ok, e)
                    product("gate", e, 2, xsT)
                    product("up", e, 4, xsT)
                if e >= 1:
                    pe.wait_ge(hidT_ok, e)
                    if e >= 2:
                        pe.wait_ge(o_ok, e - 1)
                    product("down", e - 1, 6, hidT)
                if e + 1 < NE:
                    turn_xs(e + 1)
                if e < NE:
                    turn_hid(e)

        @block.scalar
        def _(act):
            def put_xs(e):
                act.wait_ge(xs_t, e + 1)
                if e >= 1:
                    act.wait_ge(w_read, after("up", e - 1))
                for k in range(KT):
                    last = act.activation(xsT[:, k, :], g.ps[k // 4][:, (k % 4) * P:(k % 4 + 1) * P], ACT.Identity,
                                          scale=g.a2[:, k:k + 1], bias=g.mod[:, 24 + k, 0:1])
                last.then_inc(xs_ok, 1)

            put_xs(0)
            for e in range(NE):
                act.wait_ge(w_read, after("gate", e))
                if e >= 1:
                    act.wait_ge(hid_ok, e)
                act.activation(sg[:, 0:512], g.ps[2][:, :], ACT.Sigmoid).then_inc(sig, 1)
                act.activation(sg[:, 512:D], g.ps[3][:, :], ACT.Sigmoid).then_inc(sig, 1)
                if e + 1 < NE:
                    put_xs(e + 1)
                act.wait_ge(hid_t, e + 1)
                if e >= 1:
                    act.wait_ge(w_read, after("down", e - 1))
                for q in range(2):
                    last = act.activation(hidT[:, 4 * q:4 * q + 4, :].rearrange("p k t -> p (k t)"), g.ps[q][:, :], ACT.Copy)
                last.then_inc(hidT_ok, 1)

        @block.vector
        def _(dve):
            def put_out(e):
                dve.wait_ge(w_read, after("down", e))
                if e >= 2:
                    dve.wait_ge(added, 16 * (e - 1))
                for q in range(2):
                    s = slice(q * 512, (q + 1) * 512)
                    last = dve.tensor_scalar(o[:, e % 2, s], g.ps[6 + q][:, :], g.valsT[:, e:e + 1], None, ALU.mult)
                last.then_inc(o_ok, 1)

            for e in range(NE):
                for q in range(2):
                    s = slice(q * 512, (q + 1) * 512)
                    dve.wait_ge(sig, 2 * e + q + 1)
                    if e >= 1:
                        dve.wait_ge(hid_t, e)
                    dve.tensor_tensor(hid[:, s], sg[:, s], g.ps[2 + q][:, :], ALU.mult).then_inc(gs, 1)
                dve.wait_ge(gs, 2 * e + 2)
                dve.wait_ge(w_read, after("up", e))
                for q in range(2):
                    s = slice(q * 512, (q + 1) * 512)
                    last = dve.tensor_tensor(hid[:, s], hid[:, s], g.ps[4 + q][:, :], ALU.mult)
                last.then_inc(hid_ok, 1)
                if e >= 1:
                    put_out(e - 1)
            put_out(NE - 1)


def phase_combine(nc, g, ctx0):
    with ExitStack() as ctx:
        x1 = sb(nc, ctx, "cb_x1", [P, 3, D])
        mo = sb(nc, ctx, "cb_moe", [P, 3, D])
        sq = sb(nc, ctx, "cb_sq", [P, D])
        fg = sb(nc, ctx, "final_row", [P, D])
        ss = sb(nc, ctx, "cb_ss", [P, TT])
        rs = sb(nc, ctx, "cb_rs", [P, TT])
        ins = ring_sems(nc, ctx0, "cb_in", 3)
        outs = g.combined
        row_in, x2_ok, rooted, ok, chain_v, chain_a = sems(nc, ctx0, "cb_row", "cb_x2", "cb_rooted", "cb_ok", "cb_chain", "cb_chain_a")
        block = ctx.enter_context(nc.Block())
        x1_v = g.x1_rows.rearrange("(t p) d -> t p d", p=P)
        mo_v = g.moe.rearrange("(t p) d -> t p d", p=P)

        def store(sp, t):
            sp.wait_ge(ok, t + 1)
            sp.dma_start(g.x2_rows[t], x1[:, t % 3, :]).then_inc(outs[t % 3], 16)

        @block.sync
        def _(sp):
            sp.dma_start(fg[:, :], g.i["final_g"].rearrange("(a d) -> a d", a=1).to_broadcast([P, D])).then_inc(row_in, 16)
            for t in range(TT):
                if t >= 3:
                    sp.wait_ge(outs[t % 3], 16 * (t // 3))
                sp.dma_start(x1[:, t % 3, :], x1_v[t]).then_inc(ins[t % 3], 16)
                sp.dma_start(mo[:, t % 3, :], mo_v[t]).then_inc(ins[t % 3], 16)
                if t >= 2:
                    store(sp, t - 2)
            store(sp, TT - 2)
            store(sp, TT - 1)
            for r in range(3):
                sp.wait_ge(outs[r], 16 * len(range(r, TT, 3)))

        @block.scalar
        def _(act):
            for t in range(TT):
                act.wait_ge(x2_ok, t + 1)
                act.activation(sq[:, :], x1[:, t % 3, :], ACT.Square, accum_out=ss[:, t:t + 1]).then_inc(chain_a, 1)
                act.wait_ge(chain_a, t + 1)
                act.activation(rs[:, t:t + 1], ss[:, t:t + 1], ACT.Sqrt, scale=1.0 / D, bias=g.c("eps")).then_inc(rooted, 1)

        @block.vector
        def _(dve):
            step = Chain(dve, chain_v)

            def finish(t):
                dve.wait_ge(rooted, t + 1)
                step(dve.reciprocal(rs[:, t:t + 1], rs[:, t:t + 1]))
                dve.scalar_tensor_tensor(x1[:, t % 3, :], x1[:, t % 3, :], rs[:, t:t + 1], fg[:, :], ALU.mult, ALU.mult).then_inc(ok, 1)

            dve.wait_ge(row_in, 16)
            for t in range(TT):
                dve.wait_ge(ins[t % 3], 32 * (t // 3 + 1))
                step(dve.tensor_tensor(mo[:, t % 3, :], mo[:, t % 3, :], g.g2[:, :], ALU.mult))
                dve.tensor_tensor(x1[:, t % 3, :], x1[:, t % 3, :], mo[:, t % 3, :], ALU.add).then_inc(x2_ok, 1)
                if t >= 1:
                    finish(t - 1)
            finish(TT - 1)


BLOCKS = [(0, 512, "qa"), (512, 256, "kva"), (768, 512, "ga"), (1280, 512, "qb"), (1792, 512, "kb"), (2304, 512, "vb"),
          (2816, 512, "gb")]
AH, AKV, BH = 8, 2, 8


def phase_second_project(nc, g, ctx0):
    NB = len(BLOCKS)
    tiles = [(n, t) for n in range(NB) for t in range(TT)]
    with ExitStack() as ctx:
        hT = sb(nc, ctx, "h3T", [P, KT, T])
        w = sb(nc, ctx, "w2_in", [P, 2, KT, 512])
        xin = sb(nc, ctx, "x2_in", [P, 2, D])
        ss = sb(nc, ctx, "x2_ss", [P, TT])
        rs = sb(nc, ctx, "x2_rs", [P, TT])
        rope = sb(nc, ctx, "rope_sb", [P, TT, 4, HD // 2])
        gains = sb(nc, ctx, "gains", [P, 4, HD])
        sq = sb(nc, ctx, "h_sq", [P, 512])
        hss = sb(nc, ctx, "h_ss", [P, 8])
        hrs = sb(nc, ctx, "h_rs", [P, 8])
        qn = sb(nc, ctx, "qn", [P, 2, 512])
        qr = sb(nc, ctx, "qr", [P, 2, 512])
        x_in = ring_sems(nc, ctx0, "sp_x_in", 2)
        w_in = ring_sems(nc, ctx0, "sp_w_in", 2)
        (tab_in, gain_in, gain_ok, sumsq, rooted, scaled, turned, put_v, put_a, prod, squared, hroot, hsum, taken, rot, rturned,
         rput, chain_v, chain_a, sig_ok, chain_p) = sems(
            nc, ctx0, "sp_tab_in", "sp_gain_in", "sp_gain", "sp_sumsq", "sp_rooted", "sp_scaled", "sp_turned", "sp_put_v",
            "sp_put_a", "sp_prod", "sp_squared", "sp_hroot", "sp_hsum", "sp_taken", "sp_rot", "sp_rturned", "sp_rput",
            "sp_chain", "sp_chain_a", "sp_sig", "sp_chain_p")
        block = ctx.enter_context(nc.Block())
        w2 = g.i["w_in_2"].rearrange("l (k p) n -> p (l k) n", p=P)
        ROT = ("qa", "kva", "qb", "kb")
        rots = [(n, t) for n, t in tiles if BLOCKS[n][2] in ROT]
        rot_no = {x: i for i, x in enumerate(rots)}
        gates = [(n, t) for n, t in tiles if BLOCKS[n][2] in ("ga", "gb")]
        gate_no = {x: i for i, x in enumerate(gates)}
        gain_of = {"qa": 0, "kva": 1, "qb": 2, "kb": 3}

        def load(sp, n):
            at, width, _ = BLOCKS[n]
            sp.dma_start(w[:, n % 2, :, 0:width], w2[:, :, at:at + width]).then_inc(w_in[n % 2], 16)

        @block.sync
        def _(sp):
            sp.dma_start(rope[:, :, :, :], g.i["rope"].rearrange("p (t q c) -> p t q c", t=TT, q=4)).then_inc(tab_in, 16)
            for i, name in enumerate(("q_norm_a_2", "k_norm_a_2", "q_norm_b_2", "k_norm_b_2")):
                sp.dma_start(gains[:, i, :], g.i[name].to_broadcast([P, HD])).then_inc(gain_in, 16)
            for t in range(TT):
                if t >= 2:
                    sp.wait_ge(turned, t - 1)
                sp.dma_start(xin[:, t % 2, :], g.x2_rows[t]).then_inc(x_in[t % 2], 16)
                if t == 1:
                    load(sp, 0)
                    load(sp, 1)
            for n in range(2, NB):
                sp.wait_ge(prod, TT * (n - 1))
                load(sp, n)

        @block.tensor
        def _(pe):
            for t in range(TT):
                pe.wait_ge(scaled, t + 1)
                if t >= 2:
                    pe.wait_ge(put_v, t - 1)
                    pe.wait_ge(put_a, t - 1)
                for k in range(KT):
                    mm = pe.transpose(g.ps[2 * (t % 2) + k // 4][:, (k % 4) * P:(k % 4 + 1) * P], xin[:, t % 2, k * P:(k + 1) * P], g.c("ident"))
                mm.then_inc(turned, 1)

            def turn(i):
                n, t = rots[i]
                pe.wait_ge(rot, i + 1)
                if i >= 2:
                    pe.wait_ge(rput, i - 1)
                bank = g.ps[4 + i % 2]
                for k in range(4 if BLOCKS[n][2] != "kva" else 2):
                    mm = pe.transpose(bank[:, k * P:(k + 1) * P], qr[:, i % 2, k * P:(k + 1) * P], g.c("ident"))
                mm.then_inc(rturned, 1)

            pe.wait_ge(put_v, TT)
            pe.wait_ge(put_a, TT)
            done = 0
            for m, (n, t) in enumerate(tiles):
                at, width, kind = BLOCKS[n]
                if t == 0:
                    pe.wait_ge(w_in[n % 2], 16 * (n // 2 + 1))
                if m >= 4:
                    pe.wait_ge(taken, m - 3)
                for k in range(KT):
                    mm = pe.matmul(g.ps[m % 4][:, 0:width], hT[:, k, t * P:(t + 1) * P], w[:, n % 2, k, 0:width],
                                   start=(k == 0), stop=(k == KT - 1))
                mm.then_inc(prod, 1)
                if m >= 2 and tiles[m - 2] in rot_no:
                    turn(rot_no[tiles[m - 2]])

        @block.scalar
        def _(act):
            def put(t):
                act.wait_ge(turned, t + 1)
                for k in range(4, 8):
                    last = act.activation(hT[:, k, t * P:(t + 1) * P], g.ps[2 * (t % 2) + 1][:, (k - 4) * P:(k - 3) * P],
                                          ACT.Identity, scale=g.pcol2[:, 16 + k:17 + k])
                last.then_inc(put_a, 1)

            for t in range(TT):
                act.wait_ge(x_in[t % 2], 16 * (t // 2 + 1))
                for h in range(2):
                    act.activation(sq[:, :], xin[:, t % 2, h * 512:(h + 1) * 512], ACT.Square,
                                   accum_out=hss[:, 2 * (t % 2) + h:2 * (t % 2) + h + 1]).then_inc(chain_a, 1)
                    act.wait_ge(chain_a, 3 * t + h + 1)
                act.activation(ss[:, t:t + 1], hss[:, 2 * (t % 2):2 * (t % 2) + 1], ACT.Identity, bias=hss[:, 2 * (t % 2) + 1:2 * (t % 2) + 2]).then_inc(chain_a, 1)
                act.wait_ge(chain_a, 3 * t + 3)
                act.activation(rs[:, t:t + 1], ss[:, t:t + 1], ACT.Sqrt, scale=1.0 / D, bias=g.c("eps")).then_inc(rooted, 1)
                if t >= 1:
                    put(t - 1)
            put(TT - 1)
            for m, (n, t) in enumerate(tiles):
                kind = BLOCKS[n][2]
                bank = g.ps[m % 4]
                act.wait_ge(prod, m + 1)
                if kind in gain_of:
                    i = rot_no[n, t]
                    width = 128 if kind == "kva" else 512
                    if i >= 1:
                        act.wait_ge(hsum, i)
                    act.activation(sq[:, 0:width], bank[:, 0:width], ACT.Square).then_inc(squared, 1)
                    act.wait_ge(hsum, i + 1)
                    act.activation(hrs[:, 0:width // HD], hss[:, 0:width // HD], ACT.Sqrt, scale=1.0 / HD, bias=g.c("eps")).then_inc(hroot, 1)
                elif kind in ("ga", "gb"):
                    dst = (g.ga if kind == "ga" else g.gb)[:, t, :]
                    act.activation(dst, bank[:, :], ACT.Sigmoid).then_inc(sig_ok, 1)

        @block.vector
        def _(dve):
            step = Chain(dve, chain_v)

            def put(t):
                dve.wait_ge(turned, t + 1)
                for k in range(4):
                    last = dve.tensor_scalar(hT[:, k, t * P:(t + 1) * P], g.ps[2 * (t % 2)][:, k * P:(k + 1) * P],
                                             g.pcol2[:, 16 + k:17 + k], None, ALU.mult)
                last.then_inc(put_v, 1)

            dve.wait_ge(gain_in, 64)
            for i in (0, 2):
                step(dve.tensor_scalar(gains[:, i, :], gains[:, i, :], HD ** -0.5, None, ALU.mult))
            for t in range(TT):
                dve.wait_ge(rooted, t + 1)
                step(dve.reciprocal(rs[:, t:t + 1], rs[:, t:t + 1]))
                dve.tensor_scalar(xin[:, t % 2, :], xin[:, t % 2, :], rs[:, t:t + 1], None, ALU.mult).then_inc(scaled, 1)
                if t >= 1:
                    put(t - 1)
            put(TT - 1)
            dve.wait_ge(tab_in, 16)

            def store(i):
                n, t = rots[i]
                kind = BLOCKS[n][2]
                dve.wait_ge(rturned, i + 1)
                k = 2 if kind == "kva" else 4
                dst = {"qa": g.qaT, "kva": g.kaT, "qb": g.qbT, "kb": g.kbT}[kind]
                dve.tensor_copy(dst[:, :, t * P:(t + 1) * P], g.ps[4 + i % 2][:, 0:k * P].rearrange("p (k t) -> p k t", k=k)).then_inc(rput, 1)

            for m, (n, t) in enumerate(tiles):
                kind, bank = BLOCKS[n][2], g.ps[m % 4]
                if kind in gain_of:
                    i = rot_no[n, t]
                    nh = 2 if kind == "kva" else 8
                    width = nh * HD
                    dve.wait_ge(squared, i + 1)
                    dve.tensor_reduce(hss[:, 0:nh], sq[:, 0:width].rearrange("p (h d) -> p h d", d=HD), AX, ALU.add).then_inc(hsum, 1)
                    dve.wait_ge(hroot, i + 1)
                    step(dve.reciprocal(hrs[:, 0:nh], hrs[:, 0:nh]))
                    if kind == "kva":
                        dve.tensor_copy(g.va[:, t, :], bank[:, 128:256])
                    q = qn[:, i % 2, 0:width].rearrange("p (h d) -> p h d", d=HD)
                    dve.tensor_tensor(q, bank[:, 0:width].rearrange("p (h d) -> p h d", d=HD),
                                      hrs[:, 0:nh].unsqueeze(2).to_broadcast([P, nh, HD]), ALU.mult).then_inc(taken, 1)
                    dve.wait_ge(taken, m + 1)
                    step(dve.tensor_tensor(q, q, gains[:, gain_of[kind], :].unsqueeze(1).to_broadcast([P, nh, HD]), ALU.mult))
                    r = qr[:, i % 2, 0:width].rearrange("p (h d) -> p h d", d=HD)
                    cs = rope[:, t, 0:2, :].rearrange("p q c -> p (q c)").unsqueeze(1).to_broadcast([P, nh, HD])
                    if i >= 2:
                        dve.wait_ge(rturned, i - 1)
                    if i >= 1:
                        store(i - 1)
                    if kind == "kva":
                        r = qr[:, i % 2, 0:128].rearrange("p (h d) -> p h d", d=HD)
                    half = HD // 2
                    step(dve.tensor_tensor(r, q, cs, ALU.mult))
                    for h in range(2):
                        o = 1 - h
                        last = dve.tensor_tensor(q[:, :, h * half:(h + 1) * half], q[:, :, h * half:(h + 1) * half],
                                                 rope[:, t, 3 - h, :].unsqueeze(1).to_broadcast([P, nh, half]), ALU.mult)
                    step(last)
                    for h in range(2):
                        last = dve.tensor_tensor(r[:, :, h * half:(h + 1) * half], r[:, :, h * half:(h + 1) * half],
                                                 q[:, :, (1 - h) * half:(2 - h) * half], ALU.add)
                    if kind == "kva":
                        step(last)
                        dve.tensor_copy(q, r).then_inc(chain_p, 1)
                        dve.wait_ge(chain_p, t + 1)
                        d4 = qr[:, i % 2, 0:256].rearrange("p (h c d) -> p h c d", c=2, d=HD)
                        dve.tensor_copy(d4[:, :, 0], q)
                        last = dve.tensor_copy(d4[:, :, 1], q)
                    last.then_inc(rot, 1)
                elif kind == "vb":
                    if t == 0:
                        store(len([x for x in rots if x[0] < n]) - 1)
                    dve.wait_ge(prod, m + 1)
                    dve.tensor_copy(g.vb[:, t, :], bank[:, :]).then_inc(taken, 1)
                else:
                    i = gate_no[n, t]
                    dve.wait_ge(sig_ok, i + 1)
                    dst = (g.ga if kind == "ga" else g.gb)[:, t, :]
                    dve.tensor_tensor(dst, dst, bank[:, :], ALU.mult).then_inc(taken, 1)


def phase_second_attend(nc, g, ctx0):
    items = [(0, h, t) for h in range(AH) for t in range(TT)] + [(1, h, t) for h in range(BH) for t in range(TT)]
    with ExitStack() as ctx:
        bias = sb(nc, ctx, "bias_sb", [P, T + 2 * P])
        sinks = sb(nc, ctx, "sinks_sb", [P, AH])
        s = sb(nc, ctx, "scores", [P, 2, T])
        pr = sb(nc, ctx, "probs", [P, 2, T])
        pT = sb(nc, ctx, "probsT", [P, 2, KT, P])
        m = sb(nc, ctx, "row_max", [P, 4])
        l = sb(nc, ctx, "row_sum", [P, 4])
        e = sb(nc, ctx, "sink_exp", [P, 4])
        (loaded, qk, biased, maxed, exped, pturned, pcopied_v, pcopied_a, pv, out_ok, chain_v, chain_a) = sems(
            nc, ctx0, "at_loaded", "at_scores", "at_biased", "at_max", "at_exp", "at_turned", "at_copied_v", "at_copied_a", "at_pv", "at_out",
            "at_chain", "at_chain_a")
        block = ctx.enter_context(nc.Block())

        def keys(i):
            b, h, t = items[i]
            lo = 0 if b else max(0, t - 1)
            return lo, t + 1 - lo

        def parts(i):
            n = keys(i)[1] * P
            return [(c, min(n, c + 512)) for c in range(0, n, 512)]

        @block.sync
        def _(sp):
            sp.dma_start(bias[:, :], g.i["bias"]).then_inc(loaded, 16)
            sp.dma_start(sinks[:, :], g.i["sinks_a_2"].to_broadcast([P, AH])).then_inc(loaded, 16)

        @block.tensor
        def _(pe):
            def score(i):
                b, h, t = items[i]
                lo, n = keys(i)
                if i >= 2:
                    pe.wait_ge(biased, i - 1)
                half = slice(64 * (h % 2), 64 * (h % 2) + 64)
                q = (g.qbT if b else g.qaT)[half, h // 2, t * P:(t + 1) * P]
                k = g.kbT[half, h // 2] if b else g.kaT[half, h // (AH // AKV)]
                for j, (c0, c1) in enumerate(parts(i)):
                    mm = pe.matmul(g.ps[2 * (i % 2) + j][:, 0:c1 - c0], q, k[:, lo * P + c0:lo * P + c1], start=True, stop=True)
                mm.then_inc(qk, 1)

            def turn(i):
                lo, n = keys(i)
                pe.wait_ge(exped, i + 1)
                if i >= 1:
                    pe.wait_ge(pcopied_v, i)
                    pe.wait_ge(pcopied_a, i)
                for j in range(n):
                    mm = pe.transpose(g.ps[4 + j // 4][:, (j % 4) * P:(j % 4 + 1) * P], pr[:, i % 2, j * P:(j + 1) * P], g.c("ident"))
                mm.then_inc(pturned, 1)

            def value(i):
                b, h, t = items[i]
                lo, n = keys(i)
                pe.wait_ge(pcopied_v, i + 1)
                pe.wait_ge(pcopied_a, i + 1)
                if i >= 2:
                    pe.wait_ge(out_ok, i - 1)
                for j in range(n):
                    v = g.vb[:, lo + j, h * HD:(h + 1) * HD] if b else g.va[:, lo + j, h // (AH // AKV) * HD:(h // (AH // AKV) + 1) * HD]
                    mm = pe.matmul(g.ps[6 + i % 2][:, 0:HD], pT[:, i % 2, j, :], v, start=(j == 0), stop=(j == n - 1))
                mm.then_inc(pv, 1)

            N = len(items)
            for i in range(N + 3):
                if i < N:
                    score(i)
                if 2 <= i < N + 2:
                    turn(i - 2)
                if i >= 3:
                    value(i - 3)

        def copy(act, i):
            n = keys(i)[1]
            act.wait_ge(pcopied_v, i + 1)
            if n > 4:
                act.activation(pT[:, i % 2, 4:n, :].rearrange("p k t -> p (k t)"), g.ps[5][:, 0:(n - 4) * P], ACT.Copy).then_inc(pcopied_a, 1)
            else:
                act.nop().then_inc(pcopied_a, 1)

        @block.scalar
        def _(act):
            for i, (b, h, t) in enumerate(items):
                n = keys(i)[1]
                act.wait_ge(maxed, i + 1)
                if i >= 2:
                    act.wait_ge(pturned, i - 1)
                if not b:
                    act.activation(e[:, i % 4:i % 4 + 1], sinks[:, h:h + 1], ACT.Exp, bias=m[:, i % 4:i % 4 + 1])
                act.activation(pr[:, i % 2, 0:n * P], s[:, i % 2, 0:n * P], ACT.Exp, bias=m[:, i % 4:i % 4 + 1],
                               accum_out=l[:, i % 4:i % 4 + 1]).then_inc(exped, 1)
                if i >= 1:
                    copy(act, i - 1)
            copy(act, len(items) - 1)

        @block.vector
        def _(dve):
            step = Chain(dve, chain_v)
            dve.wait_ge(loaded, 32)

            def soft(i):
                b, h, t = items[i]
                lo, n = keys(i)
                dve.wait_ge(qk, i + 1)
                if i >= 2:
                    dve.wait_ge(exped, i - 1)
                if i >= 4:
                    dve.wait_ge(out_ok, i - 3)
                at = (KT - 1 - t) * P if b else T + (2 - n) * P
                mi = m[:, i % 4:i % 4 + 1]
                for j, (c0, c1) in enumerate(parts(i)):
                    last = dve.tensor_tensor(s[:, i % 2, c0:c1], g.ps[2 * (i % 2) + j][:, 0:c1 - c0], bias[:, at + c0:at + c1], ALU.add)
                last.then_inc(biased, 1)
                dve.wait_ge(biased, i + 1)
                step(dve.tensor_reduce(mi, s[:, i % 2, 0:n * P], AX, ALU.max))
                if b:
                    dve.tensor_scalar(mi, mi, -1.0, None, ALU.mult).then_inc(maxed, 1)
                else:
                    dve.tensor_scalar(mi, mi, sinks[:, h:h + 1], -1.0, ALU.max, ALU.mult).then_inc(maxed, 1)

            def put(i):
                n = min(4, keys(i)[1])
                dve.wait_ge(pturned, i + 1)
                if i >= 2:
                    dve.wait_ge(pv, i - 1)
                dve.tensor_copy(pT[:, i % 2, 0:n, :].rearrange("p k t -> p (k t)"), g.ps[4][:, 0:n * P]).then_inc(pcopied_v, 1)

            def finish(i):
                b, h, t = items[i]
                li = l[:, i % 4:i % 4 + 1]
                dve.wait_ge(exped, i + 1)
                if not b:
                    step(dve.tensor_tensor(li, li, e[:, i % 4:i % 4 + 1], ALU.add))
                step(dve.reciprocal(li, li))
                dve.wait_ge(pv, i + 1)
                gate = (g.gb if b else g.ga)[:, t, h * HD:(h + 1) * HD]
                dve.scalar_tensor_tensor(gate, g.ps[6 + i % 2][:, 0:HD], li, gate, ALU.mult, ALU.mult).then_inc(out_ok, 1)

            N = len(items)
            for i in range(N + 3):
                if i < N:
                    soft(i)
                if 2 <= i < N + 2:
                    put(i - 2)
                if i >= 3:
                    finish(i - 3)


def phase_second_out(nc, g, ctx0):
    with ExitStack() as ctx:
        wo = sb(nc, ctx, "w_out2_sb", [P, KT, D])
        mT = sb(nc, ctx, "mixT", [P, 2, KT, P])
        xin = sb(nc, ctx, "x2_again", [P, 2, D])
        x_in = ring_sems(nc, ctx0, "so_x_in", 2)
        w_in, turned, put_v, put_a, prod, ok = sems(nc, ctx0, "so_w_in", "so_turned", "so_put_v", "so_put_a", "so_prod", "so_ok")
        block = ctx.enter_context(nc.Block())
        out_v = g.out[0].rearrange("(t p) d -> t p d", p=P)

        @block.sync
        def _(sp):
            sp.dma_start(wo[:, :, :], g.i["w_out_2"].rearrange("l (k p) n -> p (l k) n", p=P)).then_inc(w_in, 16)

            def store(t):
                sp.wait_ge(ok, t + 1)
                sp.dma_start(out_v[t], xin[:, t % 2, :]).then_inc(g.out_done[t % 2], 16)

            for t in range(TT):
                if t >= 2:
                    sp.wait_ge(g.out_done[t % 2], 16 * (t // 2))
                sp.dma_start(xin[:, t % 2, :], g.x2_rows[t]).then_inc(x_in[t % 2], 16)
                if t >= 1:
                    store(t - 1)
            store(TT - 1)
            for r in range(2):
                sp.wait_ge(g.out_done[r], 16 * TT // 2)

        @block.tensor
        def _(pe):
            def turn(t):
                if t >= 1:
                    pe.wait_ge(put_v, t)
                    pe.wait_ge(put_a, t)
                for k in range(KT):
                    src = (g.ga if k < 4 else g.gb)[:, t, (k % 4) * P:(k % 4 + 1) * P]
                    mm = pe.transpose(g.ps[4 + k // 4][:, (k % 4) * P:(k % 4 + 1) * P], src, g.c("ident"))
                mm.then_inc(turned, 1)

            turn(0)
            pe.wait_ge(w_in, 16)
            for t in range(TT):
                pe.wait_ge(put_v, t + 1)
                pe.wait_ge(put_a, t + 1)
                if t + 1 < TT:
                    turn(t + 1)
                if t >= 2:
                    pe.wait_ge(ok, t - 1)
                for k in range(KT):
                    for h in range(2):
                        mm = pe.matmul(g.ps[2 * (t % 2) + h][:, :], mT[:, t % 2, k, :], wo[:, k, h * 512:(h + 1) * 512],
                                       start=(k == 0), stop=(k == KT - 1))
                mm.then_inc(prod, 1)

        @block.scalar
        def _(act):
            for t in range(TT):
                act.wait_ge(turned, t + 1)
                if t >= 2:
                    act.wait_ge(prod, t - 1)
                act.activation(mT[:, t % 2, 4:8, :].rearrange("p k t -> p (k t)"), g.ps[5][:, :], ACT.Copy).then_inc(put_a, 1)

        @block.vector
        def _(dve):
            def put(t):
                dve.wait_ge(turned, t + 1)
                if t >= 2:
                    dve.wait_ge(prod, t - 1)
                dve.tensor_copy(mT[:, t % 2, 0:4, :].rearrange("p k t -> p (k t)"), g.ps[4][:, :]).then_inc(put_v, 1)

            put(0)
            for t in range(TT):
                if t + 1 < TT:
                    put(t + 1)
                dve.wait_ge(prod, t + 1)
                dve.wait_ge(x_in[t % 2], 16 * (t // 2 + 1))
                for h in range(2):
                    w = slice(h * 512, (h + 1) * 512)
                    last = dve.tensor_tensor(xin[:, t % 2, w], xin[:, t % 2, w], g.ps[2 * (t % 2) + h][:, :], ALU.add)
                last.then_inc(ok, 1)


def phase_second(nc, g, signals):
    with ExitStack() as ctx:
        g.qaT = sb(nc, ctx, "qaT", [P, 4, T])
        g.kaT = sb(nc, ctx, "kaT", [P, AKV, T])
        g.qbT = sb(nc, ctx, "qbT", [P, 4, T])
        g.kbT = sb(nc, ctx, "kbT", [P, 4, T])
        g.va = sb(nc, ctx, "va", [P, TT, AKV * HD])
        g.vb = sb(nc, ctx, "vb", [P, TT, BH * HD])
        g.ga = sb(nc, ctx, "ga", [P, TT, AH * HD])
        g.gb = sb(nc, ctx, "gb", [P, TT, BH * HD])
        phase_second_project(nc, g, signals)
        phase_second_attend(nc, g, signals)
        phase_second_out(nc, g, signals)


def build(nc, args, out):
    g = Shared()
    g.i = args
    g.out = out
    g.rkv = nc.dram_tensor("rkv_scratch", [NCH, P, 4, HP, C], F32).ap()
    g.xn_rows = nc.dram_tensor("xn_rows", [T, D], F32).ap()
    g.moe = nc.dram_tensor("moe_rows", [T, D], F32).ap()
    g.x1_rows = nc.dram_tensor("x1_rows", [T, D], F32).ap()
    x2 = nc.dram_tensor("x2_rows", [T, D], F32).ap()
    g.x2_rows = x2.rearrange("(t p) d -> t p d", p=P)

    def flat(name):
        a = args[name]
        n = len(a.shape)
        if n == 1:
            return a
        names = " ".join("abcd"[:n])
        return a.rearrange(f"{names} -> ({names})")

    g.flat = flat
    with ExitStack() as ctx:
        g.ps = [ctx.enter_context(nc.psum_tensor(f"bank{b}", [P, 512], F32)) for b in range(8)]
        g.const = sb(nc, ctx, "const", [P, NCONST])
        g.pcol = sb(nc, ctx, "pcol", [P, NROWS])
        g.pcol2 = sb(nc, ctx, "pcol2", [P, 24])
        g.cond = sb(nc, ctx, "cond", [P, KT, 2])
        g.mod = sb(nc, ctx, "mod", [P, 48, 2])
        g.g2 = sb(nc, ctx, "g2_row", [P, D])
        g.a2 = sb(nc, ctx, "a2", [P, KT])
        g.valsT = sb(nc, ctx, "valsT", [P, NE])
        g.idxT = sb(nc, ctx, "idxT", [P, NE], U32)
        g.omu = sb(nc, ctx, "omu", [P, NRW])
        g.mus = sb(nc, ctx, "mus", [P, NRW, 6])

        def c(name):
            at, n = CONST_AT[name]
            return g.const[:, at:at + n]

        def p(name):
            at, n = ROW_AT[name]
            return g.pcol[:, at:at + n]

        g.c, g.p = c, p
        lasting = Signals(nc)
        g.combined = ring_sems(nc, lasting, "combined", 3)
        g.out_done = ring_sems(nc, lasting, "out_done", 2)
        signals = Signals(nc)
        phase_params(nc, g, signals)
        phase_modulation(nc, g, signals, "first", range(4))
        with ExitStack() as mid:
            g.bT = sb(nc, mid, "bT", [P, 4, T])
            g.yT = sb(nc, mid, "yT", [P, HP, T])
            g.lora = sb(nc, mid, "lora", [P, TA])
            g.xg = sb(nc, mid, "xg", [P, T])
            phase_project(nc, g, signals)
            phase_wkv(nc, g, signals)
            signals.clear()
            phase_heads_out(nc, g, signals)
            phase_modulation(nc, g, signals, "second", range(4, 12))
            phase_mix_out(nc, g, signals)
        signals.clear()
        phase_experts(nc, g, signals)
        phase_combine(nc, g, signals)
        signals.clear()
        phase_second(nc, g, signals)


_INS = ['x', 'c', 'ctx', 'c_ctx', 'ada_w', 'ada_b', 'norm1_g', 'norm2_g', 'w_in', 'shift_mu', 'w0', 'w_lora_up', 'a0',
        'a_lora_up', 'k_k', 'k_a', 'r_k', 'g_lora_up', 'gn_g', 'gn_b', 'conv_w', 'w_out', 'router_w', 'exp_w_gate',
        'exp_w_up', 'exp_w_down', 'final_g', 'norm_gain_2', 'w_in_2', 'q_norm_a_2', 'k_norm_a_2', 'sinks_a_2',
        'q_norm_b_2', 'k_norm_b_2', 'w_out_2']


def kernel(**inputs):
    import concourse.bacc as _bacc
    from concourse.bass_utils import run_bass_kernel_spmd as _run

    nc = _bacc.Bacc("TRN2", target_bir_lowering=False, num_devices=1)
    arrays, args = {}, {}
    for name in _INS:
        a = np.ascontiguousarray(inputs[name])
        arrays[f"in_{name}_dram"] = a
        args[name] = nc.dram_tensor(f"in_{name}_dram", a.shape, mybir.dt.from_np(a.dtype), kind="ExternalInput").ap()
    for name, a in (("consts", CONSTS), ("rope", _rope_tables()), ("bias", _bias_tables())):
        arrays[f"in_{name}_dram"] = a
        args[name] = nc.dram_tensor(f"in_{name}_dram", a.shape, F32, kind="ExternalInput").ap()
    out = nc.dram_tensor("out_0_dram", (1, T, D), F32, kind="ExternalOutput").ap()
    build(nc, args, out)
    r = _run(nc, [arrays], core_ids=[0])
    return r.results[0]["out_0_dram"]
```

```python
from contextlib import ExitStack

import numpy as np

import concourse.bass as bass
from concourse import mybir

F32 = mybir.dt.float32
U32 = mybir.dt.uint32
ALU = mybir.AluOpType
ACT = mybir.ActivationFunctionType
AX = mybir.AxisListType.X

P = 128
D = 1024
KT = D // P
T = 1024
TT = T // P
TC = 256
TA = TC + T
GRID = 64
C = 64
NCH = TA // C
NCC = TC // C
HD = 64
HP = 4
NRW = 14
NE = 16
CAP = 128
KAPPA = float(np.exp(-0.5))
EPS = 1e-6
GN_EPS = 64e-5
NEG = -1e30

LEVELS = (1, 2, 4, 8, 16, 32)
CONST_AT = {}


def _constants():
    p = np.arange(P)[:, None]
    j = np.arange(P)[None, :]
    t = np.arange(C)[None, :]
    q = p % C
    parts = {
        "ident": (p == j),
        "head": (p // C == j // C),
        "chunk": np.broadcast_to((np.arange(4 * C) % C != 0)[None, :], (P, 4 * C)),
        "maskf": np.concatenate([q < t, q <= t], 1),
        "maskb": np.concatenate([q > t, q >= t], 1),
    }
    for m in LEVELS:
        between = (q // (2 * m) == t // (2 * m)) & (q // m != t // m)
        if m == 1:
            parts["lev1"] = between
        parts[f"lev{m}i"] = between | (q == t)
    parts["eps"] = np.full((P, 1), EPS)
    parts["gn_eps"] = np.full((P, 1), GN_EPS)
    parts["pick"] = np.concatenate([p % 4 == i for i in range(4)] + [p % 2 == i for i in range(2)], 1)
    at, cols = 0, []
    for name, a in parts.items():
        CONST_AT[name] = (at, a.shape[1])
        at += a.shape[1]
        cols.append(a)
    return np.ascontiguousarray(np.concatenate(cols, 1).astype(np.float32))


def _rope_tables():
    half = HD // 2
    inv = (np.float32(10000.0) ** (-np.arange(half, dtype=np.float32) / np.float32(half))).astype(np.float32)
    ang = (np.arange(T, dtype=np.float32)[:, None] * inv[None, :]).astype(np.float32)
    cos, sin = np.cos(ang), np.sin(ang)
    full = np.concatenate([cos, cos, -sin, sin], 1).astype(np.float32)
    return np.ascontiguousarray(full.reshape(TT, P, 4 * half).transpose(1, 0, 2).reshape(P, TT * 4 * half))


def _bias_tables():
    p = np.arange(P)[:, None]
    dist = p + (T - P) - np.arange(T)[None, :]
    n = ((dist >= 0) & (dist <= 128)).astype(np.float32)
    n += (dist >= 0) & (dist <= 512) & (dist % 4 == 0)
    n += (dist >= 0) & (dist <= 2048) & (dist % 16 == 0)
    dil = np.where(n > 0, np.log(np.maximum(n, 1.0)), NEG)
    da = p + P - np.arange(2 * P)[None, :]
    win = np.where((da >= 0) & (da <= 127), 0.0, NEG)
    return np.ascontiguousarray(np.concatenate([dil, win], 1).astype(np.float32))


CONSTS = _constants()
NCONST = CONSTS.shape[1]

ROWS = [("ada_b", 48), ("norm1_g", 8), ("norm2_g", 8), ("shift_mu", 14), ("w0", 8), ("a0", 8), ("k_k", 4),
        ("k_a", 4), ("r_k", 4), ("gn_g", 4), ("gn_b", 4), ("conv_w", 12)]
ROW_AT = {}
_n = 0
for _name, _k in ROWS:
    ROW_AT[_name] = (_n, _k)
    _n += _k
NROWS = _n
ROWS2 = [("c", 8), ("c_ctx", 8), ("norm_gain_2", 8)]


class Chain:

    def __init__(self, eng, sem):
        self.eng, self.sem, self.n = eng, sem, 0

    def __call__(self, ins):
        self.n += 1
        ins.then_inc(self.sem, 1)
        self.eng.wait_ge(self.sem, self.n)


class Shared:
    pass


def sb(nc, ctx, name, shape, dt=F32):
    return ctx.enter_context(nc.sbuf_tensor(name, shape, dt))


class Signals:

    def __init__(self, nc):
        self.nc, self.held = nc, []

    def new(self, name):
        self.held.append(self.nc.alloc_semaphore(name=name))
        return self.held[-1]

    def clear(self):
        self.nc.clear_and_free_semaphores(self.held)
        self.held = []
        self.nc.all_engine_barrier()


def sems(nc, signals, *names):
    return [signals.new(n) for n in names]


def ring_sems(nc, signals, name, n):
    return [signals.new(f"{name}{i}") for i in range(n)]


def phase_params(nc, g, ctx0):
    with ExitStack() as ctx:
        prow = sb(nc, ctx, "prow", [P, P])
        prow2 = sb(nc, ctx, "prow2", [24, P])
        sig = sb(nc, ctx, "sig_c", [P, 16])
        loaded, rows_t, cols, sig_ok, chain_v = sems(nc, ctx0, "par_loaded", "par_turned", "par_cols", "par_sig", "par_chain")
        block = ctx.enter_context(nc.Block())
        n_loads = len(ROWS) + len(ROWS2) + 1

        @block.sync
        def _(sp):
            sp.dma_start(g.const[:, :], g.i["consts"]).then_inc(loaded, 16)
            for name, k in ROWS:
                flat = g.flat(name)
                at = ROW_AT[name][0]
                sp.dma_start(prow[at:at + k, :], flat.rearrange("(r n) -> r n", n=P)).then_inc(loaded, 16)
            at = 0
            for name, k in ROWS2:
                sp.dma_start(prow2[at:at + k, :], g.flat(name).rearrange("(r n) -> r n", n=P)).then_inc(loaded, 16)
                at += k

        @block.tensor
        def _(pe):
            pe.wait_ge(loaded, 16 * n_loads)
            pe.transpose(g.ps[0][:, 0:NROWS], prow[0:NROWS, :], g.c("ident")[0:NROWS, 0:NROWS]).then_inc(rows_t, 1)
            pe.transpose(g.ps[1][:, 0:24], prow2[:, :], g.c("ident")[0:24, 0:24]).then_inc(rows_t, 1)

        @block.scalar
        def _(act):
            act.wait_ge(cols, 2)
            act.activation(sig[:, :], g.pcol2[:, 0:16], ACT.Sigmoid).then_inc(sig_ok, 1)

        @block.vector
        def _(dve):
            step = Chain(dve, chain_v)
            dve.wait_ge(rows_t, 2)
            dve.tensor_copy(g.pcol[:, :], g.ps[0][:, 0:NROWS]).then_inc(cols, 1)
            dve.tensor_copy(g.pcol2[:, :], g.ps[1][:, 0:24]).then_inc(cols, 1)
            dve.wait_ge(sig_ok, 1)
            step(dve.tensor_tensor(g.cond[:, :, :].rearrange("p k j -> p j k"),
                                   g.pcol2[:, 0:16].rearrange("p (j k) -> p j k", j=2),
                                   sig[:, :].rearrange("p (j k) -> p j k", j=2), ALU.mult))
            mu = g.p("shift_mu")
            dve.tensor_scalar(g.omu[:, :], mu, -1.0, 1.0, ALU.mult, ALU.add)
            for i in range(6):
                at = CONST_AT["pick"][0] + i
                last = dve.tensor_scalar(g.mus[:, :, i], mu, g.const[:, at:at + 1], None, ALU.mult)
            step(last)


def phase_modulation(nc, g, ctx0, tag, blocks):
    RING = 3
    with ExitStack() as ctx:
        w = sb(nc, ctx, f"ada_w_{tag}", [P, RING, KT, 512])
        w_in = ring_sems(nc, ctx0, f"ada_in_{tag}", RING)
        done, taken = sems(nc, ctx0, f"ada_done_{tag}", f"ada_taken_{tag}")
        block = ctx.enter_context(nc.Block())
        adaw = g.i["ada_w"].rearrange("l (k p) n -> p (l k) n", p=P)

        @block.sync
        def _(sp):
            for n, b in enumerate(blocks):
                if n >= RING:
                    sp.wait_ge(done, n - RING + 1)
                sp.dma_start(w[:, n % RING, :, :], adaw[:, :, b * 512:(b + 1) * 512]).then_inc(w_in[n % RING], 16)

        @block.tensor
        def _(pe):
            for n, b in enumerate(blocks):
                pe.wait_ge(w_in[n % RING], 16 * (n // RING + 1))
                if n >= 2:
                    pe.wait_ge(taken, n - 1)
                for m in range(4):
                    for k in range(KT):
                        mm = pe.matmul(g.ps[n % 2][:, 2 * m:2 * m + 2], w[:, n % RING, k, m * P:(m + 1) * P],
                                       g.cond[:, k, :], start=(k == 0), stop=(k == KT - 1))
                mm.then_inc(done, 1)

        @block.vector
        def _(dve):
            for n, b in enumerate(blocks):
                dve.wait_ge(done, n + 1)
                dve.tensor_tensor(g.mod[:, 4 * b:4 * b + 4, :],
                                  g.ps[n % 2][:, 0:8].rearrange("p (m j) -> p m j", j=2),
                                  g.p("ada_b")[:, 4 * b:4 * b + 4].unsqueeze(2).to_broadcast([P, 4, 2]),
                                  ALU.add).then_inc(taken, 1)


def phase_project(nc, g, ctx0):
    NX = TA // P
    XR, WR, RR, MR = 3, 4, 4, 2
    THIRDS = ((0, 512), (512, 1024), (1024, TA))
    order = []
    for j in range(NRW):
        order.append(("rw", j))
    for i in range(4):
        order += [("b", i), ("c", i), ("u", i)]

    def column(kind, j):
        return j * P if kind == "rw" else NRW * P + "bcu".index(kind) * 512 + j * P

    NT = len(order)
    with ExitStack() as ctx:
        hT = sb(nc, ctx, "hT", [P, KT, TA])
        xin = sb(nc, ctx, "xin", [P, XR, D])
        sq = sb(nc, ctx, "x_sq", [P, D])
        ss = sb(nc, ctx, "x_ss", [P, NX])
        rs = sb(nc, ctx, "x_rs", [P, NX])
        w = sb(nc, ctx, "w_in_ring", [P, WR, KT, P])
        raw = sb(nc, ctx, "raw", [P, RR, TA])
        mix = sb(nc, ctx, "mix", [P, MR, TA])
        ksq = sb(nc, ctx, "ksq", [P, TA])
        kn = sb(nc, ctx, "kn", [P, TA])
        a1 = sb(nc, ctx, "a1", [P, KT, 2])
        xg_all = ksq
        x_in = ring_sems(nc, ctx0, "pj_x_in", XR)
        w_l = ring_sems(nc, ctx0, "pj_w_in", WR)
        stored = ring_sems(nc, ctx0, "pj_stored", 3)
        (sumsq, scaled, turned, put_v, put_a, ready, prod, copied, mixed, ksq_ok, khead, kk_ok, chain_v,
         khread, kcopied, rooted, kroot) = sems(nc, ctx0, "pj_sumsq", "pj_scaled", "pj_turned", "pj_put_v", "pj_put_a", "pj_ready", "pj_prod",
                      "pj_copied", "pj_mixed", "pj_ksq", "pj_khead", "pj_kk", "pj_chain", "pj_khread", "pj_kc", "pj_rooted", "pj_kroot")
        block = ctx.enter_context(nc.Block())
        ctx_v = g.i["ctx"].rearrange("a (t p) d -> (a t) p d", p=P)
        x_v = g.i["x"].rearrange("a (t p) d -> (a t) p d", p=P)
        win = g.i["w_in"].rearrange("l (k p) n -> p (l k) n", p=P)
        scr = g.rkv.rearrange("c p a h t -> a h p c t")

        n_rkv = 12

        @block.sync
        def _(sp):
            def load_w(n):
                kind, j = order[n]
                if n >= WR:
                    sp.wait_ge(prod, n - WR + 1)
                at = column(kind, j)
                sp.dma_start(w[:, n % WR, :, :], win[:, :, at:at + P]).then_inc(w_l[n % WR], 16)

            for i in range(NX):
                if i >= XR:
                    sp.wait_ge(turned, i - XR + 1)
                src = ctx_v[i] if i < 2 else x_v[i - 2]
                sp.dma_start(xin[:, i % XR, :], src).then_inc(x_in[i % XR], 16)
                if i == XR - 1:
                    for n in range(WR):
                        load_w(n)
            for n in range(WR, NT):
                load_w(n)

        @block.gpsimd
        def _(pool):
            for j in range(n_rkv):
                pool.wait_ge(mixed, j + 1)
                pool.dma_start(scr[j // 4, j % 4], mix[:, j % MR, :].rearrange("p (c t) -> p c t", t=C)).then_inc(stored[j % MR], 16)
                if 4 <= j < 8:
                    pool.wait_ge(kk_ok, j - 3)
                    pool.dma_start(scr[3, j % 4], kn[:, :].rearrange("p (c t) -> p c t", t=C)).then_inc(stored[2], 16)
            for r in range(MR):
                pool.wait_ge(stored[r], 16 * (n_rkv // MR))
            pool.wait_ge(stored[2], 16 * 4)

        def put_tile(act, i):
            j = 1 if i < 2 else 0
            act.wait_ge(ready, 1)
            act.wait_ge(turned, i + 1)
            for k in range(4, 8):
                last = act.activation(hT[:, k, i * P:(i + 1) * P], g.ps[2 * (i % 2) + 1][:, (k - 4) * P:(k - 3) * P],
                                      ACT.Identity, scale=a1[:, k, j:j + 1], bias=g.mod[:, k, j:j + 1])
            last.then_inc(put_a, 1)

        @block.scalar
        def _(act):
            for i in range(NX):
                act.wait_ge(x_in[i % XR], 16 * (i // XR + 1))
                act.activation(sq[:, :], xin[:, i % XR, :], ACT.Square, accum_out=ss[:, i:i + 1]).then_inc(sumsq, 1)
                act.wait_ge(sumsq, i + 1)
                act.activation(rs[:, i:i + 1], ss[:, i:i + 1], ACT.Sqrt, scale=1.0 / D, bias=g.c("eps")).then_inc(rooted, 1)
                if i >= 1:
                    put_tile(act, i - 1)
            put_tile(act, NX - 1)
            for n in range(NT):
                kind, j = order[n]
                act.wait_ge(prod, n + 1)
                if n >= RR:
                    act.wait_ge(mixed, n - RR + 1)
                a = 3 * (n % 2)
                if kind == "rw":
                    act.activation(raw[:, n % RR, 0:TC], g.ps[a][:, 0:TC], ACT.Copy)
                act.activation(raw[:, n % RR, TC:TC + 512], g.ps[a + 1][:, :], ACT.Copy)
                act.activation(raw[:, n % RR, TC + 512:TA], g.ps[a + 2][:, :], ACT.Copy).then_inc(copied, 1)
                if 5 <= n < 9:
                    for q, (lo, hi) in enumerate(THIRDS):
                        act.wait_ge(khread, 3 * (n - 5) + q + 1)
                        act.activation(ksq[:, lo:hi], ksq[:, lo:hi], ACT.Sqrt).then_inc(kroot, 1)
                if kind == "rw" and 4 <= j < 8:
                    act.wait_ge(ksq_ok, j - 3)
                    act.activation(ksq[:, :], kn[:, :], ACT.Square).then_inc(kcopied, 1)

        @block.vector
        def _(dve):
            step = Chain(dve, chain_v)
            step(dve.tensor_scalar(a1[:, :, :], g.mod[:, 8:16, :], 1.0, None, ALU.add))
            dve.tensor_tensor(a1[:, :, :], a1[:, :, :], g.p("norm1_g").unsqueeze(2).to_broadcast([P, KT, 2]), ALU.mult).then_inc(ready, 1)

            def put(i):
                j = 1 if i < 2 else 0
                dve.wait_ge(ready, 1)
                dve.wait_ge(turned, i + 1)
                for k in range(4):
                    last = dve.tensor_scalar(hT[:, k, i * P:(i + 1) * P], g.ps[2 * (i % 2)][:, k * P:(k + 1) * P],
                                             a1[:, k, j:j + 1], g.mod[:, k, j:j + 1], ALU.mult, ALU.add)
                last.then_inc(put_v, 1)

            for i in range(NX):
                dve.wait_ge(rooted, i + 1)
                step(dve.reciprocal(rs[:, i:i + 1], rs[:, i:i + 1]))
                dve.tensor_scalar(xin[:, i % XR, :], xin[:, i % XR, :], rs[:, i:i + 1], None, ALU.mult).then_inc(scaled, 1)
                if i >= 1:
                    put(i - 1)
            put(NX - 1)

            def shift(n, j, dst):
                src = raw[:, n % RR, :]
                step(dve.tensor_scalar(dst, src, g.omu[:, j:j + 1], None, ALU.mult))
                s = src[:, TC:TA].rearrange("p (r c) -> p r c", c=GRID)
                d = dst[:, TC:TA].rearrange("p (r c) -> p r c", c=GRID)
                pairs = [(d[:, :, 1:], s[:, :, :-1]), (d[:, :, :-1], s[:, :, 1:]),
                         (d[:, 1:, :], s[:, :-1, :]), (d[:, :-1, :], s[:, 1:, :]),
                         (dst[:, 1:TC], src[:, 0:TC - 1]), (dst[:, 0:TC - 1], src[:, 1:TC])]
                for i, (o, f) in enumerate(pairs):
                    ins = dve.scalar_tensor_tensor(o, f, g.mus[:, j, i:i + 1], o, ALU.mult, ALU.add)
                    if i < 5:
                        step(ins)
                return ins

            for n in range(NT):
                kind, j = order[n]
                if kind == "rw":
                    dve.wait_ge(copied, n + 1)
                    if j < 12 and j >= MR:
                        dve.wait_ge(stored[j % MR], 16 * (j // MR))
                    dst = mix[:, j % MR, :] if j < 12 else g.lora[:, :] if j == 12 else xg_all[:, :]
                    shift(n, j, dst).then_inc(mixed, 1)
                    dve.wait_ge(mixed, n + 1)
                if kind == "rw" and 4 <= j < 8:
                    h = j - 4
                    if h >= 1:
                        dve.wait_ge(stored[2], 16 * h)
                    dve.tensor_scalar(kn[:, :], dst, g.p("k_k")[:, h:h + 1], None, ALU.mult).then_inc(ksq_ok, 1)
                    dve.wait_ge(ksq_ok, h + 1)
                    for q, (lo, hi) in enumerate(THIRDS):
                        dve.wait_ge(khead, 3 * h + q + 1)
                        sl = ksq[:, lo:hi]
                        dve.tensor_scalar(sl, g.ps[6 + q % 2][:, 0:hi - lo], 1e-24, None, ALU.max).then_inc(khread, 1)
                    for q, (lo, hi) in enumerate(THIRDS):
                        sl = ksq[:, lo:hi]
                        dve.wait_ge(kroot, 3 * h + q + 1)
                        step(dve.reciprocal(sl, sl))
                        last = dve.tensor_tensor(kn[:, lo:hi], kn[:, lo:hi], sl, ALU.mult)
                    last.then_inc(kk_ok, 1)
                elif kind == "rw" and j == 13:
                    dve.tensor_copy(g.xg[:, :], xg_all[:, TC:TA])
                elif kind == "u":
                    dve.wait_ge(copied, n + 1)
                    rb, rc, ru = (raw[:, m % RR, TC:TA] for m in (n - 2, n - 1, n))
                    cw = g.p("conv_w")
                    o = g.bT[:, j, :]
                    step(dve.tensor_tensor(ru, rc, ru, ALU.mult))
                    step(dve.tensor_scalar(o, ru, cw[:, 4 + j:5 + j], None, ALU.mult))
                    step(dve.scalar_tensor_tensor(o[:, 1:], ru[:, :-1], cw[:, j:j + 1], o[:, 1:], ALU.mult, ALU.add))
                    step(dve.scalar_tensor_tensor(o[:, :-1], ru[:, 1:], cw[:, 8 + j:9 + j], o[:, :-1], ALU.mult, ALU.add))
                    dve.tensor_tensor(o, o, rb, ALU.mult).then_inc(mixed, 3)

        @block.tensor
        def _(pe):
            for i in range(NX):
                pe.wait_ge(scaled, i + 1)
                if i >= 2:
                    pe.wait_ge(put_v, i - 1)
                    pe.wait_ge(put_a, i - 1)
                for k in range(KT):
                    mm = pe.transpose(g.ps[2 * (i % 2) + k // 4][:, (k % 4) * P:(k % 4 + 1) * P],
                                      xin[:, i % XR, k * P:(k + 1) * P], g.c("ident"))
                mm.then_inc(turned, 1)
            pe.wait_ge(put_v, NX)
            pe.wait_ge(put_a, NX)
            for n in range(NT):
                kind, j = order[n]
                pe.wait_ge(w_l[n % WR], 16 * (n // WR + 1))
                if n >= 2:
                    pe.wait_ge(copied, n - 1)
                a = 3 * (n % 2)
                for k in range(KT):
                    lhsT = w[:, n % WR, k, :]
                    if kind == "rw":
                        pe.matmul(g.ps[a][:, 0:TC], lhsT, hT[:, k, 0:TC], start=(k == 0), stop=(k == KT - 1))
                    pe.matmul(g.ps[a + 1][:, :], lhsT, hT[:, k, TC:TC + 512], start=(k == 0), stop=(k == KT - 1))
                    mm = pe.matmul(g.ps[a + 2][:, :], lhsT, hT[:, k, TC + 512:TA], start=(k == 0), stop=(k == KT - 1))
                mm.then_inc(prod, 1)
                if 5 <= n < 9:
                    h = n - 5
                    pe.wait_ge(kcopied, h + 1)
                    for q, (lo, hi) in enumerate(THIRDS):
                        if 3 * h + q >= 2:
                            pe.wait_ge(khread, 3 * h + q - 1)
                        pe.matmul(g.ps[6 + q % 2][:, 0:hi - lo], g.c("head"), ksq[:, lo:hi],
                                  start=True, stop=True).then_inc(khead, 1)


def phase_wkv(nc, g, ctx0):
    NU = 4
    SS = NCH // 2
    LV = range(1, len(LEVELS))
    LAST = LV[-1]
    levels_pe = [f"{k}{l}" for l in LV for k in ("zd" if l == LAST else "zdt")]
    names = {
        "pe": ["gram", "turn", "turnx"] + levels_pe + ["r0", "u", "s"],
        "dve": ["gram", "ai"] + [f"{k}{l}" for l in LV for k in ("z" if l == LAST else "zt")] + ["s"],
        "act": ["turn", "turnx"] + [f"d{l}" for l in LV] + ["r0", "u"],
        "pool": ["y0"],
        "lora": ["lora"], "dve_f": ["z", "cum", "feat"], "act_f": ["sig", "exp"], "pool_f": ["av", "ar"],
    }

    def at(engine, ss, name):
        return ss * len(names[engine]) + names[engine].index(name) + 1

    def step_of(ss, u):
        return 2 * ss + u // 2

    def chunk_of(ss, u):
        s = step_of(ss, u)
        return s if u % 2 == 0 else (NCC - 1 - s if s < NCC else NCH - 1 + NCC - s)

    def pairs(ap):
        return ap.rearrange("p (h n) -> p h n", h=HP)

    with ExitStack() as ctx:
        up = sb(nc, ctx, "lora_up", [P, 2, HP * P])
        unit = []
        for u in range(NU):
            b = Shared()
            b.chunk = sb(nc, ctx, f"chunk{u}", [P, 4, HP, C])
            work = sb(nc, ctx, f"work{u}", [P, 6, HP, C])
            feat = work if u < 2 else sb(nc, ctx, f"feat{u}", [P, 6, HP, C])
            b.sw, b.a, b.x, b.gx, b.pi, b.kd = (feat[:, i] for i in range(6))
            b.z = feat[:, 0:2]
            b.xg = feat[:, 2:4]
            b.t, b.y, b.w = (work[:, 2 * i:2 * i + 2].rearrange("p a h t -> p (a h t)") for i in range(3))
            b.r0, b.u = b.w, b.t
            b.ar = sb(nc, ctx, f"ar{u}", [P, HP, 2, C])
            b.arbd = sb(nc, ctx, f"arbd{u}", [P, HP, 2, P])
            b.gb = sb(nc, ctx, f"gb{u}", [P, HP, 2, P])
            b.gk = sb(nc, ctx, f"gk{u}", [P, HP, 2, P])
            b.end = sb(nc, ctx, f"end{u}", [P, HP])
            b.bbd, b.kbd, b.vbd, b.ai = (sb(nc, ctx, f"{n}{u}", [P, HP, P]) for n in ("bbd", "kbd", "vbd", "ai"))
            b.A, b.B = g.ps[2 * u], g.ps[2 * u + 1]
            unit.append(b)
        sbd = [[sb(nc, ctx, f"sbd{d}{q}", [P, HP, P]) for q in range(2)] for d in range(2)]
        chunk_in = ring_sems(nc, ctx0, "wk_chunk_in", NU)
        pe_done = ring_sems(nc, ctx0, "wk_products", NU)
        dve_done = ring_sems(nc, ctx0, "wk_vector", NU)
        act_done = ring_sems(nc, ctx0, "wk_scalar", NU)
        pool_done = ring_sems(nc, ctx0, "wk_pool", NU)
        lora_done = ring_sems(nc, ctx0, "wk_logits", 2)
        dve_f = ring_sems(nc, ctx0, "wk_vector_features", NU)
        act_f = ring_sems(nc, ctx0, "wk_scalar_features", NU)
        pool_f = ring_sems(nc, ctx0, "wk_pool_features", NU)
        y_done = ring_sems(nc, ctx0, "wk_y", NU)
        y_taken = ring_sems(nc, ctx0, "wk_y_taken", NU)
        up_in, zeroed, tanh_ok, chain_v, chain_a, chain_p = sems(
            nc, ctx0, "wk_up_in", "wk_zeroed", "wk_tanh", "wk_chain", "wk_chain_a", "wk_chain_p")
        block = ctx.enter_context(nc.Block())

        def nx(ss):
            return max(0, ss + 1 - NCC // 2)

        HALVES = (slice(0, C), slice(C, P))

        @block.sync
        def _(sp):
            for d in range(2):
                sp.dma_start(up[0:64, d, :], g.i["w_lora_up"][0, d]).then_inc(up_in, 16)
                sp.dma_start(up[64:128, d, :], g.i["a_lora_up"][0, d]).then_inc(up_in, 16)
            for ss in range(SS):
                for u in range(NU):
                    if ss >= 1:
                        sp.wait_ge(dve_f[u], at("dve_f", ss - 1, "feat"))
                        sp.wait_ge(pool_f[u], at("pool_f", ss - 1, "av"))
                    sp.dma_start(unit[u].chunk[:, :, :, :], g.rkv[chunk_of(ss, u)]).then_inc(chunk_in[u], 16)

        @block.gpsimd
        def _(pool):
            step = Chain(pool, chain_p)
            for b in unit:
                for m in (b.bbd, b.kbd, b.vbd):
                    pool.memset(m[:, :, :], 0.0)
                for m in (b.arbd, b.gb, b.gk):
                    pool.memset(m[:, :, :, :], 0.0)
            pool.memset(sbd[0][0][:, :, :], 0.0)
            pool.memset(sbd[1][0][:, :, :], 0.0).then_inc(zeroed, 1)
            pool.wait_ge(zeroed, 1)
            one = g.c("ident").unsqueeze(1).to_broadcast([P, HP, P])

            def features(ss, units):
                for u in units:
                    b = unit[u]
                    pool.wait_ge(chunk_in[u], 16 * (ss + 1))
                    if ss >= 1:
                        pool.wait_ge(pe_done[u], at("pe", ss - 1, "s"))
                        if nx(ss - 1):
                            pool.wait_ge(y_done[u], nx(ss - 1))
                    step(pool.tensor_copy(b.vbd[HALVES[0], :, HALVES[0]], b.chunk[HALVES[0], 2]))
                    pool.tensor_copy(b.vbd[HALVES[1], :, HALVES[1]], b.chunk[HALVES[1], 2]).then_inc(pool_f[u], 1)
                    pool.wait_ge(pool_f[u], at("pool_f", ss, "av"))
                for u in units:
                    b = unit[u]
                    pool.wait_ge(dve_f[u], at("dve_f", ss, "feat"))
                    step(pool.tensor_copy(b.arbd[HALVES[0], :, :, HALVES[0]], b.ar[HALVES[0]]))
                    pool.tensor_copy(b.arbd[HALVES[1], :, :, HALVES[1]], b.ar[HALVES[1]]).then_inc(pool_f[u], 1)
                    pool.wait_ge(pool_f[u], at("pool_f", ss, "ar"))

            features(0, (0, 1, 2, 3))
            for ss in range(SS):
                for u, b in enumerate(unit):
                    pool.wait_ge(dve_done[u], at("dve", ss, "gram"))
                    y = b.y.rearrange("p (h a t) -> p h a t", h=HP, a=2)
                    x = b.gb[:, :, 0].rearrange("p h (a t) -> p h a t", a=2)
                    for hp in range(HP):
                        last = pool.tensor_tensor(y[:, hp], x[:, hp], g.c("lev1").unsqueeze(1).to_broadcast([P, 2, C]), ALU.mult)
                    step(last)
                    pool.tensor_tensor(pairs(b.y), pairs(b.y), one, ALU.add).then_inc(pool_done[u], 1)
                if ss + 1 < SS:
                    features(ss + 1, (0, 1))
                    features(ss + 1, (2, 3))

        @block.scalar
        def _(act):
            step = Chain(act, chain_a)
            act.activation(g.lora[0:64, :], g.lora[0:64, :], ACT.Tanh).then_inc(tanh_ok, 1)
            act.wait_ge(zeroed, 1)

            def features(ss):
                for u, b in enumerate(unit):
                    act.wait_ge(dve_f[u], at("dve_f", ss, "z"))
                    act.activation(b.z, b.z, ACT.Sigmoid).then_inc(act_f[u], 1)
                for u, b in enumerate(unit):
                    act.wait_ge(dve_f[u], at("dve_f", ss, "cum"))
                    step(act.activation(b.pi, b.gx, ACT.Exp, scale=KAPPA))
                    act.activation(b.xg, b.xg, ACT.Exp, scale=-KAPPA).then_inc(act_f[u], 1)

            features(0)
            for ss in range(SS):
                for u, b in enumerate(unit):
                    act.wait_ge(pe_done[u], at("pe", ss, "turn"))
                    act.activation(b.bbd[:, :, :], pairs(b.A[:, :]), ACT.Copy)
                    act.activation(b.kbd[:, :, :], pairs(b.B[:, :]), ACT.Copy).then_inc(act_done[u], 1)
                for u, b in enumerate(unit):
                    act.wait_ge(pe_done[u], at("pe", ss, "turnx"))
                    act.activation(b.vbd[:, :, :], pairs(b.A[:, :]), ACT.Copy).then_inc(act_done[u], 1)
                for l in LV:
                    for u, b in enumerate(unit):
                        act.wait_ge(pe_done[u], at("pe", ss, f"d{l}"))
                        act.activation(b.y, b.B[:, :], ACT.Copy).then_inc(act_done[u], 1)
                for s2 in range(2):
                    for name in ("r0", "u"):
                        for d in range(2):
                            u, b = 2 * s2 + d, unit[2 * s2 + d]
                            act.wait_ge(pe_done[u], at("pe", ss, name))
                            act.activation(b.r0 if name == "r0" else b.u, (b.A if name == "r0" else b.B)[:, :], ACT.Copy).then_inc(act_done[u], 1)
                if ss + 1 < SS:
                    features(ss + 1)

        @block.vector
        def _(dve):
            step = Chain(dve, chain_v)

            def over_tokens(ap):
                return ap.unsqueeze(2).to_broadcast([P, HP, C])

            def blocks(ap):
                return ap.rearrange("p (n t) -> p n t", t=C)

            def over_blocks(ap):
                return ap.unsqueeze(1).to_broadcast([P, 2 * HP, C])

            one = g.c("ident").unsqueeze(1).to_broadcast([P, HP, P])
            flat = "p h t -> p (h t)"
            def logits(ss):
                for u, b in enumerate(unit):
                    d = u % 2
                    dve.wait_ge(lora_done[d], ss + 1)
                    if ss >= 1 and nx(ss - 1) and u < 2:
                        dve.wait_ge(y_done[u], nx(ss - 1))
                    q = u // 2 if d == 0 else 1 - u // 2
                    for bank, dst, bias in ((unit[d].A, b.sw, g.p("w0")), (unit[d].B, b.a, g.p("a0"))):
                        last = dve.tensor_tensor(dst, pairs(bank[:, :])[:, :, q * C:(q + 1) * C],
                                                 over_tokens(bias[:, d * HP:(d + 1) * HP]), ALU.add)
                    last.then_inc(dve_f[u], 1)

            def sums(ss):
                for u, b in enumerate(unit):
                    d = u % 2
                    dve.wait_ge(act_f[u], at("act_f", ss, "sig"))
                    run = b.gx if d == 0 else b.kd
                    step(dve.tensor_tensor_scan(run.rearrange(flat), g.c("chunk"), b.sw.rearrange(flat), 0.0, ALU.mult, ALU.add))
                    if d == 0:
                        step(dve.tensor_tensor(b.x, run, b.sw, ALU.subtract))
                    else:
                        step(dve.tensor_tensor(b.x, over_tokens(run[:, :, C - 1]), run, ALU.subtract))
                        step(dve.tensor_tensor(b.gx, b.x, b.sw, ALU.add))
                    dve.wait_ge(chunk_in[u], 16 * (ss + 1))
                    step(dve.scalar_tensor_tensor(b.kd, b.a, -1.0, over_tokens(g.p("k_a")), ALU.add, ALU.mult))
                    dve.scalar_tensor_tensor(b.kd, b.kd, 1.0, b.chunk[:, 1], ALU.add, ALU.mult).then_inc(dve_f[u], 1)

            def features(ss, units):
                for u in units:
                    b, d = unit[u], u % 2
                    dve.wait_ge(act_f[u], at("act_f", ss, "exp"))
                    dve.wait_ge(dve_f[u], at("dve_f", ss, "cum"))
                    if ss >= 1:
                        dve.wait_ge(pool_f[u], at("pool_f", ss - 1, "ar"))
                        dve.wait_ge(dve_done[u], at("dve", ss - 1, "s"))
                    dve.scalar_tensor_tensor(b.ar[:, :, 0], b.chunk[:, 3], -1.0, b.x, ALU.mult, ALU.mult)
                    dve.tensor_tensor(b.ar[:, :, 1], b.chunk[:, 0], b.gx, ALU.mult)
                    dve.tensor_copy(b.end[:, :], b.gx[:, :, C - 1 if d == 0 else 0])
                    step(dve.tensor_tensor(b.sw, b.a, b.pi, ALU.mult))
                    for h in HALVES:
                        dve.tensor_tensor(b.bbd[h, :, h], b.chunk[h, 3], b.sw[h], ALU.mult)
                        last = dve.tensor_tensor(b.kbd[h, :, h], b.kd[h], b.pi[h], ALU.mult)
                    last.then_inc(dve_f[u], 1)

            logits(0)
            sums(0)
            dve.wait_ge(zeroed, 1)
            features(0, (0, 1, 2, 3))
            for ss in range(SS):
                for u, b in enumerate(unit):
                    mask = g.c("maskf" if u % 2 == 0 else "maskb").rearrange("p (a t) -> p a t", a=2)
                    dve.wait_ge(pe_done[u], at("pe", ss, "gram"))
                    for bank, dst in ((b.A, b.gb), (b.B, b.gk)):
                        for h in HALVES:
                            last = dve.tensor_tensor(dst[h, :, :, h], bank[h, :].rearrange("p (h a t) -> p h a t", h=HP, a=2),
                                                     mask[h].unsqueeze(1).to_broadcast([C, HP, 2, C]), ALU.mult)
                    last.then_inc(dve_done[u], 1)
                for u, b in enumerate(unit):
                    dve.wait_ge(pe_done[u], at("pe", ss, "turnx"))
                    step(dve.tensor_tensor(b.ai[:, :, :], pairs(b.B[:, :]), one, ALU.add))
                    dve.tensor_tensor(blocks(b.t), blocks(b.ai[:, :, :].rearrange("p h n -> p (h n)")),
                                      over_blocks(g.c("lev1i")), ALU.mult).then_inc(dve_done[u], 1)
                for l in LV:
                    lev = over_blocks(g.c(f"lev{LEVELS[l]}i"))
                    for u, b in enumerate(unit):
                        dve.wait_ge(pe_done[u], at("pe", ss, f"z{l}"))
                        dve.tensor_tensor(blocks(b.w), blocks(b.A[:, :]), lev, ALU.mult).then_inc(dve_done[u], 1)
                    if l < LAST:
                        for u, b in enumerate(unit):
                            dve.wait_ge(pe_done[u], at("pe", ss, f"t{l}"))
                            dve.tensor_copy(b.t, b.A[:, :]).then_inc(dve_done[u], 1)
                for s2 in range(2):
                    for d in range(2):
                        u, b = 2 * s2 + d, unit[2 * s2 + d]
                        new = sbd[d][1 - s2]
                        dve.wait_ge(pe_done[u], at("pe", ss, "s"))
                        step(dve.tensor_tensor(new[:, :, :], pairs(b.A[:, :]), sbd[d][s2][:, :, :], ALU.add))
                        dve.tensor_tensor(new[:, :, :], new[:, :, :], b.end[:, :].unsqueeze(2).to_broadcast([P, HP, P]),
                                          ALU.mult).then_inc(dve_done[u], 1)
                    for d in range(2):
                        u, b = 2 * s2 + d, unit[2 * s2 + d]
                        s, c = step_of(ss, u), chunk_of(ss, u) - NCC
                        if s < NCC:
                            continue
                        dve.wait_ge(y_done[u], nx(ss))
                        first = s < NCC + (NCH - NCC) // 2
                        if s == NCC + (NCH - NCC) // 2:
                            for q in range(NU):
                                dve.wait_ge(y_taken[q], nx(ss - 1))
                        for h in HALVES:
                            dst = g.yT[h, :, c * C:(c + 1) * C]
                            src = pairs(b.B[h, :])[:, :, h]
                            last = dve.tensor_copy(dst, src) if first else dve.tensor_tensor(dst, dst, src, ALU.add)
                        last.then_inc(y_taken[u], 1)
                    if s2 == 0 and ss + 1 < SS:
                        logits(ss + 1)
                        sums(ss + 1)
                        features(ss + 1, (0, 1))
                if ss + 1 < SS:
                    features(ss + 1, (2, 3))

        @block.tensor
        def _(pe):
            def each(bank, *terms):
                for h in range(HP):
                    for i, (st, mv) in enumerate(terms):
                        mm = pe.matmul(bank[:, h * P:(h + 1) * P], st[:, h], mv[:, h], start=(i == 0), stop=(i == len(terms) - 1))
                return mm

            def turn(bank, src):
                for h in range(HP):
                    mm = pe.transpose(bank[:, h * P:(h + 1) * P], src[:, h], g.c("ident"))
                return mm

            pe.wait_ge(up_in, 64)
            pe.wait_ge(tanh_ok, 1)
            def logits(ss):
                for d in range(2):
                    at0 = min(chunk_of(ss, d), chunk_of(ss, d + 2)) * C
                    if ss >= 1:
                        pe.wait_ge(dve_done[d], at("dve", ss - 1, "s"))
                        if nx(ss - 1):
                            pe.wait_ge(y_taken[d], nx(ss - 1))
                    for h, bank in ((slice(0, 64), unit[d].A), (slice(64, 128), unit[d].B)):
                        for hp in range(HP):
                            mm = pe.matmul(bank[:, hp * P:(hp + 1) * P], up[h, d, hp * P:(hp + 1) * P],
                                           g.lora[h, at0:at0 + 2 * C], start=True, stop=True)
                    mm.then_inc(lora_done[d], 1)

            logits(0)
            for ss in range(SS):
                for u, b in enumerate(unit):
                    pe.wait_ge(dve_f[u], at("dve_f", ss, "feat"))
                    pe.wait_ge(dve_f[(u + 2) % 4], at("dve_f", ss, "z"))
                    if u >= 2 and nx(ss - 1):
                        pe.wait_ge(y_taken[u], nx(ss - 1))
                    ar = b.ar[:, :, :, :].rearrange("p h a t -> p h (a t)")
                    each(b.A, (b.bbd, ar))
                    each(b.B, (b.kbd, ar)).then_inc(pe_done[u], 1)
                for u, b in enumerate(unit):
                    pe.wait_ge(dve_done[u], at("dve", ss, "gram"))
                    turn(b.A, b.bbd)
                    turn(b.B, b.kbd).then_inc(pe_done[u], 1)
                for u, b in enumerate(unit):
                    pe.wait_ge(act_done[u], at("act", ss, "turn"))
                    pe.wait_ge(pool_f[u], at("pool_f", ss, "av"))
                    turn(b.A, b.vbd)
                    turn(b.B, b.gb[:, :, 0]).then_inc(pe_done[u], 1)
                for l in LV:
                    for u, b in enumerate(unit):
                        if l == 1:
                            pe.wait_ge(act_done[u], at("act", ss, "turnx"))
                            pe.wait_ge(dve_done[u], at("dve", ss, "ai"))
                            pe.wait_ge(pool_done[u], at("pool", ss, "y0"))
                        else:
                            pe.wait_ge(act_done[u], at("act", ss, f"d{l - 1}"))
                            pe.wait_ge(dve_done[u], at("dve", ss, f"t{l - 1}"))
                        each(b.A, (b.ai, pairs(b.y))).then_inc(pe_done[u], 1)
                    for u, b in enumerate(unit):
                        pe.wait_ge(dve_done[u], at("dve", ss, f"z{l}"))
                        each(b.B, (pairs(b.t), pairs(b.w))).then_inc(pe_done[u], 1)
                    if l < LAST:
                        for u, b in enumerate(unit):
                            pe.wait_ge(act_done[u], at("act", ss, f"d{l}"))
                            turn(b.A, pairs(b.y)).then_inc(pe_done[u], 1)
                for s2 in range(2):
                    for d in range(2):
                        u, b = 2 * s2 + d, unit[2 * s2 + d]
                        o, last = (u + 2) % 4, (ss if s2 else ss - 1)
                        if last >= 0:
                            pe.wait_ge(dve_done[o], at("dve", last, "s"))
                        pe.wait_ge(act_done[u], at("act", ss, f"d{LAST}"))
                        pe.wait_ge(pool_f[u], at("pool_f", ss, "ar"))
                        each(b.A, (b.arbd[:, :, 0], sbd[d][s2]), (b.gk[:, :, 0], b.vbd)).then_inc(pe_done[u], 1)
                    for d in range(2):
                        u, b = 2 * s2 + d, unit[2 * s2 + d]
                        pe.wait_ge(act_done[u], at("act", ss, "r0"))
                        each(b.B, (pairs(b.y), pairs(b.r0))).then_inc(pe_done[u], 1)
                    if s2 == 1 and ss + 1 < SS:
                        logits(ss + 1)
                    for d in range(2):
                        u, b = 2 * s2 + d, unit[2 * s2 + d]
                        pe.wait_ge(act_done[u], at("act", ss, "u"))
                        each(b.A, (b.bbd, pairs(b.u)), (b.kbd, b.vbd)).then_inc(pe_done[u], 1)
                    for d in range(2):
                        u, b = 2 * s2 + d, unit[2 * s2 + d]
                        if step_of(ss, u) < NCC:
                            continue
                        each(b.B, (sbd[d][s2], b.arbd[:, :, 1]), (pairs(b.u), b.gb[:, :, 1]), (b.vbd, b.gk[:, :, 1])).then_inc(y_done[u], 1)


def phase_heads_out(nc, g, ctx0):
    HALF = T // 2
    NP_ = 2 * HP
    pieces = [(hp, q) for hp in range(HP) for q in range(2)]
    kinds = ["mean"] * NP_ + ["a0", "a1"] * NP_ + ["gate"] * NP_ + ["var"] * NP_ + ["bonus"] * NP_
    seq, seen = {}, {}
    for q, kind in enumerate(kinds):
        seq[kind, seen.get(kind, 0)] = q
        seen[kind] = seen.get(kind, 0) + 1
    with ExitStack() as ctx:
        up = sb(nc, ctx, "lora_up2", [P, 2, HP * P])
        gup = sb(nc, ctx, "g_up", [P, HP * P])
        rk = sb(nc, ctx, "rkv_back", [P, NCH - NCC, 3, HP, C])
        sq = sb(nc, ctx, "gn_sq", [P, HP, T])
        gt = sb(nc, ctx, "gate_t", [P, HP, T])
        rks = sb(nc, ctx, "rks", [P, HP, T])
        sa = sb(nc, ctx, "sig_a", [P, 2, 2, HALF])
        loaded, rk_in, chain_v = sems(nc, ctx0, "ho_loaded", "ho_rkv_in", "ho_chain")
        done = {k: ctx0.new(f"ho_{k}") for k in ("mean", "a", "gate", "var", "bonus")}
        free = ring_sems(nc, ctx0, "ho_bank_free", 8)
        xg_ok, sig_a, a_read, squared, rooted, gated, rks_ok = sems(
            nc, ctx0, "ho_xg", "ho_sig_a", "ho_a_read", "ho_squared", "ho_rooted", "ho_gated", "ho_rks")
        block = ctx.enter_context(nc.Block())

        def bank(kind, i):
            return seq[kind, i] % 8

        def tok(t, i):
            hp, q = pieces[i]
            return t[:, hp, q * HALF:(q + 1) * HALF]

        def chunks(i, a):
            hp, q = pieces[i]
            n = (NCH - NCC) // 2
            return rk[:, q * n:(q + 1) * n, a, hp, :]

        def ch(ap):
            return ap.rearrange("p (c t) -> p c t", t=C)

        @block.sync
        def _(sp):
            for d in range(2):
                sp.dma_start(up[64:128, d, :], g.i["a_lora_up"][0, d]).then_inc(loaded, 16)
            sp.dma_start(gup[:, :], g.i["g_lora_up"][0]).then_inc(loaded, 16)
            sp.dma_start(rk[:, :, :, :, :], g.rkv[NCC:NCH, :, 0:3].rearrange("c p a h t -> p c a h t")).then_inc(rk_in, 16)

        @block.tensor
        def _(pe):
            def into(kind, i):
                q = seq[kind, i]
                if q >= 8:
                    pe.wait_ge(free[q % 8], q // 8)
                return g.ps[q % 8][:, 0:HALF]

            for i in range(NP_):
                pe.matmul(into("mean", i), g.c("head"), tok(g.yT, i), start=True, stop=True).then_inc(done["mean"], 1)
            pe.wait_ge(loaded, 48)
            for i, (hp, q) in enumerate(pieces):
                for d in range(2):
                    pe.matmul(into(f"a{d}", i), up[64:128, d, hp * P:(hp + 1) * P],
                              g.lora[64:128, TC + q * HALF:TC + (q + 1) * HALF], start=True, stop=True).then_inc(done["a"], 1)
            pe.wait_ge(xg_ok, 1)
            for i, (hp, q) in enumerate(pieces):
                pe.matmul(into("gate", i), gup[:, hp * P:(hp + 1) * P], g.xg[:, q * HALF:(q + 1) * HALF],
                          start=True, stop=True).then_inc(done["gate"], 1)
            for i in range(NP_):
                pe.wait_ge(squared, i + 1)
                pe.matmul(into("var", i), g.c("head"), tok(sq, i), start=True, stop=True).then_inc(done["var"], 1)
            for i in range(NP_):
                pe.wait_ge(rks_ok, i + 1)
                pe.matmul(into("bonus", i), g.c("head"), tok(rks, i), start=True, stop=True).then_inc(done["bonus"], 1)

        @block.scalar
        def _(act):
            act.activation(g.xg[:, :], g.xg[:, :], ACT.Sigmoid).then_inc(xg_ok, 1)
            for i, (hp, q) in enumerate(pieces):
                if i >= 2:
                    act.wait_ge(a_read, i - 1)
                for d in range(2):
                    act.wait_ge(done["a"], 2 * i + d + 1)
                    b = bank(f"a{d}", i)
                    act.activation(sa[:, i % 2, d, :], g.ps[b][:, :], ACT.Sigmoid,
                                   bias=g.p("a0")[:, d * HP + hp:d * HP + hp + 1]).then_inc(free[b], 1)
            for i in range(NP_):
                act.wait_ge(done["gate"], i + 1)
                act.activation(tok(gt, i), g.ps[bank("gate", i)][:, :], ACT.Copy).then_inc(free[bank("gate", i)], 1)
            for i in range(NP_):
                act.wait_ge(free[bank("mean", i)], seq["mean", i] // 8 + 1)
                act.activation(tok(sq, i), tok(g.yT, i), ACT.Square).then_inc(squared, 1)
            for i in range(NP_):
                act.wait_ge(done["var"], i + 1)
                act.activation(tok(sq, i), g.ps[bank("var", i)][:, :], ACT.Sqrt, scale=1.0 / HD, bias=g.c("gn_eps")).then_inc(free[bank("var", i)], 1)

        @block.vector
        def _(dve):
            step = Chain(dve, chain_v)
            for i in range(NP_):
                b = bank("mean", i)
                dve.wait_ge(done["mean"], i + 1)
                dve.scalar_tensor_tensor(tok(g.yT, i), g.ps[b][:, :], -1.0 / HD, tok(g.yT, i), ALU.mult, ALU.add).then_inc(free[b], 1)
            dve.wait_ge(rk_in, 16)
            for i, (hp, q) in enumerate(pieces):
                dve.wait_ge(free[bank("a1", i)], seq["a1", i] // 8 + 1)
                dve.wait_ge(free[bank("a0", i)], seq["a0", i] // 8 + 1)
                o = tok(rks, i)
                dve.tensor_tensor(o, sa[:, i % 2, 0, :], sa[:, i % 2, 1, :], ALU.add).then_inc(a_read, 1)
                dve.wait_ge(a_read, i + 1)
                step(dve.tensor_scalar(o, o, -2.0, g.p("k_a")[:, hp:hp + 1], ALU.add, ALU.mult))
                step(dve.scalar_tensor_tensor(ch(o), ch(o), 2.0, chunks(i, 1), ALU.add, ALU.mult))
                dve.scalar_tensor_tensor(ch(o), ch(o), g.p("r_k")[:, hp:hp + 1], chunks(i, 0), ALU.mult, ALU.mult).then_inc(rks_ok, 1)
            for i, (hp, q) in enumerate(pieces):
                b, o, s = bank("var", i), tok(g.yT, i), tok(sq, i)
                dve.wait_ge(free[b], seq["var", i] // 8 + 1)
                step(dve.reciprocal(s, s))
                step(dve.tensor_tensor(o, o, s, ALU.mult))
                step(dve.tensor_scalar(o, o, g.p("gn_g")[:, hp:hp + 1], g.p("gn_b")[:, hp:hp + 1], ALU.mult, ALU.add))
                b = bank("bonus", i)
                dve.wait_ge(done["bonus"], i + 1)
                step(dve.tensor_tensor(ch(s), ch(g.ps[b][:, :]), chunks(i, 2), ALU.mult))
                step(dve.tensor_tensor(o, o, s, ALU.add))
                dve.wait_ge(free[bank("gate", i)], seq["gate", i] // 8 + 1)
                step(dve.tensor_tensor(o, o, tok(gt, i), ALU.mult))


def phase_mix_out(nc, g, ctx0):
    with ExitStack() as ctx:
        wo = sb(nc, ctx, "w_out_sb", [P, KT, D])
        ones = sb(nc, ctx, "ones", [P, P])
        diag = sb(nc, ctx, "diag", [P, 4, P])
        g1 = sb(nc, ctx, "g1_row", [P, D])
        xin = sb(nc, ctx, "x_again", [P, 2, D])
        x1 = sb(nc, ctx, "x1", [P, 2, D])
        sq = sb(nc, ctx, "x1_sq", [P, D])
        ss = sb(nc, ctx, "x1_ss", [P, TT])
        rs = sb(nc, ctx, "x1_rs", [P, TT])
        xn = sb(nc, ctx, "x1n", [P, 2, D])
        h2 = sb(nc, ctx, "h2T", [P, 2, KT, P])
        rw = sb(nc, ctx, "router", [P, KT, NE])
        aff = sb(nc, ctx, "aff", [P, TT, NE])
        mx = sb(nc, ctx, "aff_max", [P, TT])
        affT = sb(nc, ctx, "affT", [NE, T])
        vals = sb(nc, ctx, "vals", [NE, CAP])
        idx = sb(nc, ctx, "idx", [NE, CAP], U32)
        idxf = sb(nc, ctx, "idxf", [NE, CAP])
        wo_in, rw_in, row_ok, row_done, gcols, chain_v, chain_a = sems(
            nc, ctx0, "mo_w_in", "mo_router_in", "mo_row", "mo_row_done", "mo_cols", "mo_chain", "mo_chain_a")
        x_in = ring_sems(nc, ctx0, "mo_x_in", 2)
        st1 = ring_sems(nc, ctx0, "mo_x1_out", 2)
        stn = ring_sems(nc, ctx0, "mo_xn_out", 2)
        prod, x1_ok, sumsq, xn_ok, turned, h2_ok, logit, ex_ok, shifted, aff_ok, aff_t, top, top_t, diag_ok = sems(
            nc, ctx0, "mo_prod", "mo_x1", "mo_sumsq", "mo_xn", "mo_turned", "mo_h2", "mo_logits", "mo_exp", "mo_shifted",
            "mo_aff", "mo_aff_turned", "mo_top", "mo_top_turned", "mo_diag")
        block = ctx.enter_context(nc.Block())
        x_v = g.i["x"].rearrange("a (t p) d -> (a t) p d", p=P)
        x1_v = g.x1_rows.rearrange("(t p) d -> t p d", p=P)
        xn_v = g.xn_rows.rearrange("(t p) d -> t p d", p=P)

        def store(sp, t):
            sp.wait_ge(x1_ok, t + 1)
            sp.dma_start(x1_v[t], x1[:, t % 2, :]).then_inc(st1[t % 2], 16)
            sp.wait_ge(xn_ok, t + 1)
            sp.dma_start(xn_v[t], xn[:, t % 2, :]).then_inc(stn[t % 2], 16)

        @block.sync
        def _(sp):
            sp.dma_start(wo[:, :, :], g.i["w_out"].rearrange("l (k p) n -> p (l k) n", p=P)).then_inc(wo_in, 16)
            sp.dma_start(rw[:, :, :], g.i["router_w"].rearrange("l (k p) n -> p (l k) n", p=P)).then_inc(rw_in, 16)
            for t in range(TT):
                if t >= 2:
                    sp.wait_ge(x1_ok, t - 1)
                sp.dma_start(xin[:, t % 2, :], x_v[t]).then_inc(x_in[t % 2], 16)
                if t >= 1:
                    store(sp, t - 1)
            store(sp, TT - 1)
            for r in range(2):
                sp.wait_ge(st1[r], 16 * TT // 2)
                sp.wait_ge(stn[r], 16 * TT // 2)

        @block.tensor
        def _(pe):
            pe.wait_ge(row_ok, 1)
            for n in range(4):
                pe.wait_ge(diag_ok, n + 1)
                if n >= 2:
                    pe.wait_ge(row_done, n - 1)
                for k in range(4):
                    mm = pe.matmul(g.ps[n % 2][:, k * P:(k + 1) * P], ones[:, :], diag[:, k, :], start=True, stop=True)
                mm.then_inc(gcols, 1)
            pe.wait_ge(row_done, 4)

            def turn(t):
                pe.wait_ge(xn_ok, t + 1)
                if t >= 1:
                    pe.wait_ge(h2_ok, t)
                for k in range(KT):
                    mm = pe.transpose(g.ps[4 + k // 4][:, (k % 4) * P:(k % 4 + 1) * P], xn[:, t % 2, k * P:(k + 1) * P], g.c("ident"))
                mm.then_inc(turned, 1)

            def route(t):
                pe.wait_ge(h2_ok, t + 1)
                for k in range(KT):
                    mm = pe.matmul(g.ps[6][:, t * NE:(t + 1) * NE], h2[:, t % 2, k, :], rw[:, k, :], start=(k == 0), stop=(k == KT - 1))
                mm.then_inc(logit, 1)

            pe.wait_ge(wo_in, 16)
            pe.wait_ge(rw_in, 16)
            for t in range(TT):
                if t >= 2:
                    pe.wait_ge(x1_ok, t - 1)
                for k in range(KT):
                    lhsT = (g.yT if k < 4 else g.bT)[:, k % 4, t * P:(t + 1) * P]
                    for h in range(2):
                        mm = pe.matmul(g.ps[2 * (t % 2) + h][:, :], lhsT, wo[:, k, h * 512:(h + 1) * 512], start=(k == 0), stop=(k == KT - 1))
                mm.then_inc(prod, 1)
                if t >= 1:
                    turn(t - 1)
                if t >= 2:
                    route(t - 2)
            turn(TT - 1)
            route(TT - 2)
            route(TT - 1)
            pe.wait_ge(aff_ok, 1)
            for t in range(TT):
                mm = pe.transpose(g.ps[t // 4][0:NE, (t % 4) * P:(t % 4 + 1) * P], aff[:, t, :], g.c("ident"))
            mm.then_inc(aff_t, 1)
            pe.wait_ge(top, 1)
            pe.transpose(g.ps[2][:, 0:NE], vals[:, :], g.c("ident")[0:NE, 0:NE])
            pe.transpose(g.ps[2][:, NE:2 * NE], idxf[:, :], g.c("ident")[0:NE, 0:NE]).then_inc(top_t, 1)

        @block.scalar
        def _(act):
            for t in range(TT):
                act.wait_ge(x1_ok, t + 1)
                act.activation(sq[:, :], x1[:, t % 2, :], ACT.Square, accum_out=ss[:, t:t + 1]).then_inc(chain_a, 1)
                act.wait_ge(chain_a, t + 1)
                act.activation(rs[:, t:t + 1], ss[:, t:t + 1], ACT.Sqrt, scale=1.0 / D, bias=g.c("eps")).then_inc(sumsq, 1)
                act.wait_ge(turned, t + 1)
                if t >= 2:
                    act.wait_ge(logit, t - 1)
                for k in range(KT):
                    last = act.activation(h2[:, t % 2, k, :], g.ps[4 + k // 4][:, (k % 4) * P:(k % 4 + 1) * P], ACT.Identity,
                                          scale=g.a2[:, k:k + 1], bias=g.mod[:, 24 + k, 0:1])
                last.then_inc(h2_ok, 1)
            act.wait_ge(shifted, 1)
            act.activation(aff[:, :, :], aff[:, :, :], ACT.Exp).then_inc(ex_ok, 1)

        @block.vector
        def _(dve):
            step = Chain(dve, chain_v)
            dve.memset(ones[:, :], 1.0).then_inc(row_ok, 1)
            for n in range(4):
                base = (16, 20, 40, 44)[n]
                if n >= 1:
                    dve.wait_ge(gcols, n)
                for k in range(4):
                    last = dve.tensor_scalar(diag[:, k, :], g.c("ident"), g.mod[:, base + k, 0:1], None, ALU.mult)
                last.then_inc(diag_ok, 1)
                dve.wait_ge(gcols, n + 1)
                dst = g1 if n < 2 else g.g2
                dve.tensor_copy(dst[:, (n % 2) * 512:(n % 2 + 1) * 512], g.ps[n % 2][:, :]).then_inc(row_done, 1)
            dve.wait_ge(row_done, 4)
            step(dve.tensor_scalar(g.a2[:, :], g.mod[:, 32:40, 0], 1.0, None, ALU.add))
            step(dve.tensor_tensor(g.a2[:, :], g.a2[:, :], g.p("norm2_g"), ALU.mult))
            for t in range(TT):
                dve.wait_ge(prod, t + 1)
                dve.wait_ge(x_in[t % 2], 16 * (t // 2 + 1))
                if t >= 2:
                    dve.wait_ge(st1[t % 2], 16 * (t // 2))
                    dve.wait_ge(stn[t % 2], 16 * (t // 2))
                for h in range(2):
                    w = slice(h * 512, (h + 1) * 512)
                    last = dve.tensor_tensor(x1[:, t % 2, w], g.ps[2 * (t % 2) + h][:, :], g1[:, w], ALU.mult)
                step(last)
                dve.tensor_tensor(x1[:, t % 2, :], x1[:, t % 2, :], xin[:, t % 2, :], ALU.add).then_inc(x1_ok, 1)
                dve.wait_ge(sumsq, t + 1)
                if t >= 2:
                    dve.wait_ge(turned, t - 1)
                step(dve.reciprocal(rs[:, t:t + 1], rs[:, t:t + 1]))
                dve.tensor_scalar(xn[:, t % 2, :], x1[:, t % 2, :], rs[:, t:t + 1], None, ALU.mult).then_inc(xn_ok, 1)
            dve.wait_ge(logit, TT)
            lg = g.ps[6][:, 0:TT * NE].rearrange("p (t e) -> p t e", e=NE)

            def wide(ap):
                return ap.unsqueeze(2).to_broadcast([P, TT, NE])

            step(dve.tensor_reduce(mx[:, :], lg, AX, ALU.max))
            dve.tensor_tensor(aff[:, :, :], lg, wide(mx[:, :]), ALU.subtract).then_inc(shifted, 1)
            dve.wait_ge(ex_ok, 1)
            step(dve.tensor_reduce(mx[:, :], aff[:, :, :], AX, ALU.add))
            step(dve.reciprocal(mx[:, :], mx[:, :]))
            dve.tensor_tensor(aff[:, :, :], aff[:, :, :], wide(mx[:, :]), ALU.mult).then_inc(aff_ok, 1)
            dve.wait_ge(aff_t, 1)
            dve.tensor_copy(affT[:, 0:512], g.ps[0][0:NE, :])
            step(dve.tensor_copy(affT[:, 512:T], g.ps[1][0:NE, :]))
            for r in range(CAP // 8):
                v = vals[:, 8 * r:8 * r + 8]
                step(dve.max(v, affT[:, :]))
                step(dve.max_index(idx[:, 8 * r:8 * r + 8], v, affT[:, :]))
                step(dve.match_replace(affT[:, :], v, affT[:, :], -1.0))
            dve.tensor_copy(idxf[:, :], idx[:, :]).then_inc(top, 1)
            dve.wait_ge(top_t, 1)
            dve.tensor_copy(g.valsT[:, :], g.ps[2][:, 0:NE])
            dve.tensor_copy(g.idxT[:, :], g.ps[2][:, NE:2 * NE])


def phase_experts(nc, g, ctx0):
    RING = 7
    HALF = KT // 2
    loads = []
    for e in range(NE):
        loads += [("gate", e, 0), ("gate", e, 1), ("up", e, 0), ("up", e, 1)]
        if e >= 1:
            loads += [("down", e - 1, 0), ("down", e - 1, 1)]
    loads += [("down", NE - 1, 0), ("down", NE - 1, 1)]
    place = {x: n for n, x in enumerate(loads)}
    with ExitStack() as ctx:
        w = sb(nc, ctx, "exp_w", [P, RING, HALF, D])
        xs = sb(nc, ctx, "xs", [P, 2, D])
        xsT = sb(nc, ctx, "xsT", [P, KT, P])
        sg = sb(nc, ctx, "sg", [P, D])
        hid = sb(nc, ctx, "hid", [P, D])
        hidT = sb(nc, ctx, "hidT", [P, KT, P])
        o = sb(nc, ctx, "exp_out", [P, 2, D])
        zero = sb(nc, ctx, "zero_row", [P, D])
        w_in = ring_sems(nc, ctx0, "ex_w_in", RING)
        x_in = ring_sems(nc, ctx0, "ex_x_in", 2)
        w_read, xs_t, xs_ok, sig, gs, hid_ok, hid_t, hidT_ok, o_ok, added, zeroed, z_ok = sems(
            nc, ctx0, "ex_w_read", "ex_xs_turned", "ex_xsT", "ex_sig", "ex_gs", "ex_hid", "ex_hid_turned",
            "ex_hidT", "ex_out", "ex_added", "ex_zeroed", "ex_zero_row")
        block = ctx.enter_context(nc.Block())
        def after(kind, e):
            return place[kind, e, 1] + 1

        src = {"gate": g.i["exp_w_gate"], "up": g.i["exp_w_up"], "down": g.i["exp_w_down"]}

        @block.sync
        def _(sp):
            for n, (kind, e, h) in enumerate(loads):
                if n >= RING:
                    sp.wait_ge(w_read, n - RING + 1)
                sp.dma_start(w[:, n % RING, :, :], src[kind][0, e].rearrange("(k p) n -> p k n", p=P)[:, h * HALF:(h + 1) * HALF, :]).then_inc(w_in[n % RING], 16)

        @block.gpsimd
        def _(pool):
            def gather(e):
                if e >= 2:
                    pool.wait_ge(xs_t, e - 1)
                pool.indirect_dma_start(xs[:, e % 2, :], None, g.xn_rows, bass.IndirectOffsetOnAxis(ap=g.idxT[:, e:e + 1], axis=0)).then_inc(x_in[e % 2], 16)

            gather(0)
            gather(1)
            pool.memset(zero[:, :], 0.0).then_inc(z_ok, 1)
            pool.wait_ge(z_ok, 1)
            moe_v = g.moe.rearrange("(t p) d -> t p d", p=P)
            for t in range(TT):
                pool.dma_start(moe_v[t], zero[:, :]).then_inc(zeroed, 16)
            pool.wait_ge(zeroed, 16 * TT)
            for e in range(NE):
                if e + 2 < NE:
                    gather(e + 2)
                pool.wait_ge(o_ok, e + 1)
                if e >= 1:
                    pool.wait_ge(added, 16 * e)
                pool.indirect_dma_start(g.moe, bass.IndirectOffsetOnAxis(ap=g.idxT[:, e:e + 1], axis=0), o[:, e % 2, :], None,
                                        compute_op=ALU.add).then_inc(added, 16)
            pool.wait_ge(added, 16 * NE)

        @block.tensor
        def _(pe):
            def turn_xs(e):
                pe.wait_ge(x_in[e % 2], 16 * (e // 2 + 1))
                if e >= 2:
                    pe.wait_ge(hidT_ok, e - 1)
                v = xs[:, e % 2, :].rearrange("p (k q) -> p k q", k=KT)
                for k in range(KT):
                    mm = pe.transpose(g.ps[k // 4][:, (k % 4) * P:(k % 4 + 1) * P], v[:, k], g.c("ident"))
                mm.then_inc(xs_t, 1)

            def turn_hid(e):
                pe.wait_ge(hid_ok, e + 1)
                if e + 1 < NE:
                    pe.wait_ge(xs_ok, e + 2)
                v = hid[:, :].rearrange("p (k q) -> p k q", k=KT)
                for k in range(KT):
                    mm = pe.transpose(g.ps[k // 4][:, (k % 4) * P:(k % 4 + 1) * P], v[:, k], g.c("ident"))
                mm.then_inc(hid_t, 1)

            def product(kind, e, bank, lhs):
                for h in range(2):
                    n = place[kind, e, h]
                    pe.wait_ge(w_in[n % RING], 16 * (n // RING + 1))
                    for k in range(HALF):
                        kk = h * HALF + k
                        for q in range(2):
                            mm = pe.matmul(g.ps[bank + q][:, :], lhs[:, kk, :], w[:, n % RING, k, q * 512:(q + 1) * 512],
                                           start=(kk == 0), stop=(kk == KT - 1))
                    mm.then_inc(w_read, 1)

            turn_xs(0)
            for e in range(NE + 1):
                if e < NE:
                    pe.wait_ge(xs_ok, e + 1)
                    if e >= 1:
                        pe.wait_ge(hid_ok, e)
                    product("gate", e, 2, xsT)
                    product("up", e, 4, xsT)
                if e >= 1:
                    pe.wait_ge(hidT_ok, e)
                    if e >= 2:
                        pe.wait_ge(o_ok, e - 1)
                    product("down", e - 1, 6, hidT)
                if e + 1 < NE:
                    turn_xs(e + 1)
                if e < NE:
                    turn_hid(e)

        @block.scalar
        def _(act):
            def put_xs(e):
                act.wait_ge(xs_t, e + 1)
                if e >= 1:
                    act.wait_ge(w_read, after("up", e - 1))
                for k in range(KT):
                    last = act.activation(xsT[:, k, :], g.ps[k // 4][:, (k % 4) * P:(k % 4 + 1) * P], ACT.Identity,
                                          scale=g.a2[:, k:k + 1], bias=g.mod[:, 24 + k, 0:1])
                last.then_inc(xs_ok, 1)

            put_xs(0)
            for e in range(NE):
                act.wait_ge(w_read, after("gate", e))
                if e >= 1:
                    act.wait_ge(hid_ok, e)
                act.activation(sg[:, 0:512], g.ps[2][:, :], ACT.Sigmoid).then_inc(sig, 1)
                act.activation(sg[:, 512:D], g.ps[3][:, :], ACT.Sigmoid).then_inc(sig, 1)
                if e + 1 < NE:
                    put_xs(e + 1)
                act.wait_ge(hid_t, e + 1)
                if e >= 1:
                    act.wait_ge(w_read, after("down", e - 1))
                for q in range(2):
                    last = act.activation(hidT[:, 4 * q:4 * q + 4, :].rearrange("p k t -> p (k t)"), g.ps[q][:, :], ACT.Copy)
                last.then_inc(hidT_ok, 1)

        @block.vector
        def _(dve):
            def put_out(e):
                dve.wait_ge(w_read, after("down", e))
                if e >= 2:
                    dve.wait_ge(added, 16 * (e - 1))
                for q in range(2):
                    s = slice(q * 512, (q + 1) * 512)
                    last = dve.tensor_scalar(o[:, e % 2, s], g.ps[6 + q][:, :], g.valsT[:, e:e + 1], None, ALU.mult)
                last.then_inc(o_ok, 1)

            for e in range(NE):
                for q in range(2):
                    s = slice(q * 512, (q + 1) * 512)
                    dve.wait_ge(sig, 2 * e + q + 1)
                    if e >= 1:
                        dve.wait_ge(hid_t, e)
                    dve.tensor_tensor(hid[:, s], sg[:, s], g.ps[2 + q][:, :], ALU.mult).then_inc(gs, 1)
                dve.wait_ge(gs, 2 * e + 2)
                dve.wait_ge(w_read, after("up", e))
                for q in range(2):
                    s = slice(q * 512, (q + 1) * 512)
                    last = dve.tensor_tensor(hid[:, s], hid[:, s], g.ps[4 + q][:, :], ALU.mult)
                last.then_inc(hid_ok, 1)
                if e >= 1:
                    put_out(e - 1)
            put_out(NE - 1)


def phase_combine(nc, g, ctx0):
    with ExitStack() as ctx:
        x1 = sb(nc, ctx, "cb_x1", [P, 3, D])
        mo = sb(nc, ctx, "cb_moe", [P, 3, D])
        sq = sb(nc, ctx, "cb_sq", [P, D])
        fg = sb(nc, ctx, "final_row", [P, D])
        ss = sb(nc, ctx, "cb_ss", [P, TT])
        rs = sb(nc, ctx, "cb_rs", [P, TT])
        ins = ring_sems(nc, ctx0, "cb_in", 3)
        outs = g.combined
        row_in, x2_ok, rooted, ok, chain_v, chain_a = sems(nc, ctx0, "cb_row", "cb_x2", "cb_rooted", "cb_ok", "cb_chain", "cb_chain_a")
        block = ctx.enter_context(nc.Block())
        x1_v = g.x1_rows.rearrange("(t p) d -> t p d", p=P)
        mo_v = g.moe.rearrange("(t p) d -> t p d", p=P)

        def store(sp, t):
            sp.wait_ge(ok, t + 1)
            sp.dma_start(g.x2_rows[t], x1[:, t % 3, :]).then_inc(outs[t % 3], 16)

        @block.sync
        def _(sp):
            sp.dma_start(fg[:, :], g.i["final_g"].rearrange("(a d) -> a d", a=1).to_broadcast([P, D])).then_inc(row_in, 16)
            for t in range(TT):
                if t >= 3:
                    sp.wait_ge(outs[t % 3], 16 * (t // 3))
                sp.dma_start(x1[:, t % 3, :], x1_v[t]).then_inc(ins[t % 3], 16)
                sp.dma_start(mo[:, t % 3, :], mo_v[t]).then_inc(ins[t % 3], 16)
                if t >= 2:
                    store(sp, t - 2)
            store(sp, TT - 2)
            store(sp, TT - 1)
            for r in range(3):
                sp.wait_ge(outs[r], 16 * len(range(r, TT, 3)))

        @block.scalar
        def _(act):
            for t in range(TT):
                act.wait_ge(x2_ok, t + 1)
                act.activation(sq[:, :], x1[:, t % 3, :], ACT.Square, accum_out=ss[:, t:t + 1]).then_inc(chain_a, 1)
                act.wait_ge(chain_a, t + 1)
                act.activation(rs[:, t:t + 1], ss[:, t:t + 1], ACT.Sqrt, scale=1.0 / D, bias=g.c("eps")).then_inc(rooted, 1)

        @block.vector
        def _(dve):
            step = Chain(dve, chain_v)

            def finish(t):
                dve.wait_ge(rooted, t + 1)
                step(dve.reciprocal(rs[:, t:t + 1], rs[:, t:t + 1]))
                dve.scalar_tensor_tensor(x1[:, t % 3, :], x1[:, t % 3, :], rs[:, t:t + 1], fg[:, :], ALU.mult, ALU.mult).then_inc(ok, 1)

            dve.wait_ge(row_in, 16)
            for t in range(TT):
                dve.wait_ge(ins[t % 3], 32 * (t // 3 + 1))
                step(dve.tensor_tensor(mo[:, t % 3, :], mo[:, t % 3, :], g.g2[:, :], ALU.mult))
                dve.tensor_tensor(x1[:, t % 3, :], x1[:, t % 3, :], mo[:, t % 3, :], ALU.add).then_inc(x2_ok, 1)
                if t >= 1:
                    finish(t - 1)
            finish(TT - 1)


BLOCKS = [(0, 512, "qa"), (512, 256, "kva"), (768, 512, "ga"), (1280, 512, "qb"), (1792, 512, "kb"), (2304, 512, "vb"),
          (2816, 512, "gb")]
AH, AKV, BH = 8, 2, 8


def phase_second_project(nc, g, ctx0):
    NB = len(BLOCKS)
    tiles = [(n, t) for n in range(NB) for t in range(TT)]
    with ExitStack() as ctx:
        hT = sb(nc, ctx, "h3T", [P, KT, T])
        w = sb(nc, ctx, "w2_in", [P, 2, KT, 512])
        xin = sb(nc, ctx, "x2_in", [P, 2, D])
        ss = sb(nc, ctx, "x2_ss", [P, TT])
        rs = sb(nc, ctx, "x2_rs", [P, TT])
        rope = sb(nc, ctx, "rope_sb", [P, TT, 4, HD // 2])
        gains = sb(nc, ctx, "gains", [P, 4, HD])
        sq = sb(nc, ctx, "h_sq", [P, 512])
        hss = sb(nc, ctx, "h_ss", [P, 8])
        hrs = sb(nc, ctx, "h_rs", [P, 8])
        qn = sb(nc, ctx, "qn", [P, 2, 512])
        qr = sb(nc, ctx, "qr", [P, 2, 512])
        x_in = ring_sems(nc, ctx0, "sp_x_in", 2)
        w_in = ring_sems(nc, ctx0, "sp_w_in", 2)
        (tab_in, gain_in, gain_ok, sumsq, rooted, scaled, turned, put_v, put_a, prod, squared, hroot, hsum, taken, rot, rturned,
         rput, chain_v, chain_a, sig_ok, chain_p) = sems(
            nc, ctx0, "sp_tab_in", "sp_gain_in", "sp_gain", "sp_sumsq", "sp_rooted", "sp_scaled", "sp_turned", "sp_put_v",
            "sp_put_a", "sp_prod", "sp_squared", "sp_hroot", "sp_hsum", "sp_taken", "sp_rot", "sp_rturned", "sp_rput",
            "sp_chain", "sp_chain_a", "sp_sig", "sp_chain_p")
        block = ctx.enter_context(nc.Block())
        w2 = g.i["w_in_2"].rearrange("l (k p) n -> p (l k) n", p=P)
        ROT = ("qa", "kva", "qb", "kb")
        rots = [(n, t) for n, t in tiles if BLOCKS[n][2] in ROT]
        rot_no = {x: i for i, x in enumerate(rots)}
        gates = [(n, t) for n, t in tiles if BLOCKS[n][2] in ("ga", "gb")]
        gate_no = {x: i for i, x in enumerate(gates)}
        gain_of = {"qa": 0, "kva": 1, "qb": 2, "kb": 3}

        def load(sp, n):
            at, width, _ = BLOCKS[n]
            sp.dma_start(w[:, n % 2, :, 0:width], w2[:, :, at:at + width]).then_inc(w_in[n % 2], 16)

        @block.sync
        def _(sp):
            sp.dma_start(rope[:, :, :, :], g.i["rope"].rearrange("p (t q c) -> p t q c", t=TT, q=4)).then_inc(tab_in, 16)
            for i, name in enumerate(("q_norm_a_2", "k_norm_a_2", "q_norm_b_2", "k_norm_b_2")):
                sp.dma_start(gains[:, i, :], g.i[name].to_broadcast([P, HD])).then_inc(gain_in, 16)
            for t in range(TT):
                if t >= 2:
                    sp.wait_ge(turned, t - 1)
                sp.dma_start(xin[:, t % 2, :], g.x2_rows[t]).then_inc(x_in[t % 2], 16)
                if t == 1:
                    load(sp, 0)
                    load(sp, 1)
            for n in range(2, NB):
                sp.wait_ge(prod, TT * (n - 1))
                load(sp, n)

        @block.tensor
        def _(pe):
            for t in range(TT):
                pe.wait_ge(scaled, t + 1)
                if t >= 2:
                    pe.wait_ge(put_v, t - 1)
                    pe.wait_ge(put_a, t - 1)
                for k in range(KT):
                    mm = pe.transpose(g.ps[2 * (t % 2) + k // 4][:, (k % 4) * P:(k % 4 + 1) * P], xin[:, t % 2, k * P:(k + 1) * P], g.c("ident"))
                mm.then_inc(turned, 1)

            def turn(i):
                n, t = rots[i]
                pe.wait_ge(rot, i + 1)
                if i >= 2:
                    pe.wait_ge(rput, i - 1)
                bank = g.ps[4 + i % 2]
                for k in range(4 if BLOCKS[n][2] != "kva" else 2):
                    mm = pe.transpose(bank[:, k * P:(k + 1) * P], qr[:, i % 2, k * P:(k + 1) * P], g.c("ident"))
                mm.then_inc(rturned, 1)

            pe.wait_ge(put_v, TT)
            pe.wait_ge(put_a, TT)
            done = 0
            for m, (n, t) in enumerate(tiles):
                at, width, kind = BLOCKS[n]
                if t == 0:
                    pe.wait_ge(w_in[n % 2], 16 * (n // 2 + 1))
                if m >= 4:
                    pe.wait_ge(taken, m - 3)
                for k in range(KT):
                    mm = pe.matmul(g.ps[m % 4][:, 0:width], hT[:, k, t * P:(t + 1) * P], w[:, n % 2, k, 0:width],
                                   start=(k == 0), stop=(k == KT - 1))
                mm.then_inc(prod, 1)
                if m >= 2 and tiles[m - 2] in rot_no:
                    turn(rot_no[tiles[m - 2]])

        @block.scalar
        def _(act):
            def put(t):
                act.wait_ge(turned, t + 1)
                for k in range(4, 8):
                    last = act.activation(hT[:, k, t * P:(t + 1) * P], g.ps[2 * (t % 2) + 1][:, (k - 4) * P:(k - 3) * P],
                                          ACT.Identity, scale=g.pcol2[:, 16 + k:17 + k])
                last.then_inc(put_a, 1)

            for t in range(TT):
                act.wait_ge(x_in[t % 2], 16 * (t // 2 + 1))
                for h in range(2):
                    act.activation(sq[:, :], xin[:, t % 2, h * 512:(h + 1) * 512], ACT.Square,
                                   accum_out=hss[:, 2 * (t % 2) + h:2 * (t % 2) + h + 1]).then_inc(chain_a, 1)
                    act.wait_ge(chain_a, 3 * t + h + 1)
                act.activation(ss[:, t:t + 1], hss[:, 2 * (t % 2):2 * (t % 2) + 1], ACT.Identity, bias=hss[:, 2 * (t % 2) + 1:2 * (t % 2) + 2]).then_inc(chain_a, 1)
                act.wait_ge(chain_a, 3 * t + 3)
                act.activation(rs[:, t:t + 1], ss[:, t:t + 1], ACT.Sqrt, scale=1.0 / D, bias=g.c("eps")).then_inc(rooted, 1)
                if t >= 1:
                    put(t - 1)
            put(TT - 1)
            for m, (n, t) in enumerate(tiles):
                kind = BLOCKS[n][2]
                bank = g.ps[m % 4]
                act.wait_ge(prod, m + 1)
                if kind in gain_of:
                    i = rot_no[n, t]
                    width = 128 if kind == "kva" else 512
                    if i >= 1:
                        act.wait_ge(hsum, i)
                    act.activation(sq[:, 0:width], bank[:, 0:width], ACT.Square).then_inc(squared, 1)
                    act.wait_ge(hsum, i + 1)
                    act.activation(hrs[:, 0:width // HD], hss[:, 0:width // HD], ACT.Sqrt, scale=1.0 / HD, bias=g.c("eps")).then_inc(hroot, 1)
                elif kind in ("ga", "gb"):
                    dst = (g.ga if kind == "ga" else g.gb)[:, t, :]
                    act.activation(dst, bank[:, :], ACT.Sigmoid).then_inc(sig_ok, 1)

        @block.vector
        def _(dve):
            step = Chain(dve, chain_v)

            def put(t):
                dve.wait_ge(turned, t + 1)
                for k in range(4):
                    last = dve.tensor_scalar(hT[:, k, t * P:(t + 1) * P], g.ps[2 * (t % 2)][:, k * P:(k + 1) * P],
                                             g.pcol2[:, 16 + k:17 + k], None, ALU.mult)
                last.then_inc(put_v, 1)

            dve.wait_ge(gain_in, 64)
            for i in (0, 2):
                step(dve.tensor_scalar(gains[:, i, :], gains[:, i, :], HD ** -0.5, None, ALU.mult))
            for t in range(TT):
                dve.wait_ge(rooted, t + 1)
                step(dve.reciprocal(rs[:, t:t + 1], rs[:, t:t + 1]))
                dve.tensor_scalar(xin[:, t % 2, :], xin[:, t % 2, :], rs[:, t:t + 1], None, ALU.mult).then_inc(scaled, 1)
                if t >= 1:
                    put(t - 1)
            put(TT - 1)
            dve.wait_ge(tab_in, 16)

            def store(i):
                n, t = rots[i]
                kind = BLOCKS[n][2]
                dve.wait_ge(rturned, i + 1)
                k = 2 if kind == "kva" else 4
                dst = {"qa": g.qaT, "kva": g.kaT, "qb": g.qbT, "kb": g.kbT}[kind]
                dve.tensor_copy(dst[:, :, t * P:(t + 1) * P], g.ps[4 + i % 2][:, 0:k * P].rearrange("p (k t) -> p k t", k=k)).then_inc(rput, 1)

            for m, (n, t) in enumerate(tiles):
                kind, bank = BLOCKS[n][2], g.ps[m % 4]
                if kind in gain_of:
                    i = rot_no[n, t]
                    nh = 2 if kind == "kva" else 8
                    width = nh * HD
                    dve.wait_ge(squared, i + 1)
                    dve.tensor_reduce(hss[:, 0:nh], sq[:, 0:width].rearrange("p (h d) -> p h d", d=HD), AX, ALU.add).then_inc(hsum, 1)
                    dve.wait_ge(hroot, i + 1)
                    step(dve.reciprocal(hrs[:, 0:nh], hrs[:, 0:nh]))
                    if kind == "kva":
                        dve.tensor_copy(g.va[:, t, :], bank[:, 128:256])
                    q = qn[:, i % 2, 0:width].rearrange("p (h d) -> p h d", d=HD)
                    dve.tensor_tensor(q, bank[:, 0:width].rearrange("p (h d) -> p h d", d=HD),
                                      hrs[:, 0:nh].unsqueeze(2).to_broadcast([P, nh, HD]), ALU.mult).then_inc(taken, 1)
                    dve.wait_ge(taken, m + 1)
                    step(dve.tensor_tensor(q, q, gains[:, gain_of[kind], :].unsqueeze(1).to_broadcast([P, nh, HD]), ALU.mult))
                    r = qr[:, i % 2, 0:width].rearrange("p (h d) -> p h d", d=HD)
                    cs = rope[:, t, 0:2, :].rearrange("p q c -> p (q c)").unsqueeze(1).to_broadcast([P, nh, HD])
                    if i >= 2:
                        dve.wait_ge(rturned, i - 1)
                    if i >= 1:
                        store(i - 1)
                    if kind == "kva":
                        r = qr[:, i % 2, 0:128].rearrange("p (h d) -> p h d", d=HD)
                    half = HD // 2
                    step(dve.tensor_tensor(r, q, cs, ALU.mult))
                    for h in range(2):
                        o = 1 - h
                        last = dve.tensor_tensor(q[:, :, h * half:(h + 1) * half], q[:, :, h * half:(h + 1) * half],
                                                 rope[:, t, 3 - h, :].unsqueeze(1).to_broadcast([P, nh, half]), ALU.mult)
                    step(last)
                    for h in range(2):
                        last = dve.tensor_tensor(r[:, :, h * half:(h + 1) * half], r[:, :, h * half:(h + 1) * half],
                                                 q[:, :, (1 - h) * half:(2 - h) * half], ALU.add)
                    if kind == "kva":
                        step(last)
                        dve.tensor_copy(q, r).then_inc(chain_p, 1)
                        dve.wait_ge(chain_p, t + 1)
                        d4 = qr[:, i % 2, 0:256].rearrange("p (h c d) -> p h c d", c=2, d=HD)
                        dve.tensor_copy(d4[:, :, 0], q)
                        last = dve.tensor_copy(d4[:, :, 1], q)
                    last.then_inc(rot, 1)
                elif kind == "vb":
                    if t == 0:
                        store(len([x for x in rots if x[0] < n]) - 1)
                    dve.wait_ge(prod, m + 1)
                    dve.tensor_copy(g.vb[:, t, :], bank[:, :]).then_inc(taken, 1)
                else:
                    i = gate_no[n, t]
                    dve.wait_ge(sig_ok, i + 1)
                    dst = (g.ga if kind == "ga" else g.gb)[:, t, :]
                    dve.tensor_tensor(dst, dst, bank[:, :], ALU.mult).then_inc(taken, 1)


def phase_second_attend(nc, g, ctx0):
    items = [(0, h, t) for h in range(AH) for t in range(TT)] + [(1, h, t) for h in range(BH) for t in range(TT)]
    with ExitStack() as ctx:
        bias = sb(nc, ctx, "bias_sb", [P, T + 2 * P])
        sinks = sb(nc, ctx, "sinks_sb", [P, AH])
        s = sb(nc, ctx, "scores", [P, 2, T])
        pr = sb(nc, ctx, "probs", [P, 2, T])
        pT = sb(nc, ctx, "probsT", [P, 2, KT, P])
        m = sb(nc, ctx, "row_max", [P, 4])
        l = sb(nc, ctx, "row_sum", [P, 4])
        e = sb(nc, ctx, "sink_exp", [P, 4])
        (loaded, qk, biased, maxed, exped, pturned, pcopied_v, pcopied_a, pv, out_ok, chain_v, chain_a) = sems(
            nc, ctx0, "at_loaded", "at_scores", "at_biased", "at_max", "at_exp", "at_turned", "at_copied_v", "at_copied_a", "at_pv", "at_out",
            "at_chain", "at_chain_a")
        block = ctx.enter_context(nc.Block())

        def keys(i):
            b, h, t = items[i]
            lo = 0 if b else max(0, t - 1)
            return lo, t + 1 - lo

        def parts(i):
            n = keys(i)[1] * P
            return [(c, min(n, c + 512)) for c in range(0, n, 512)]

        @block.sync
        def _(sp):
            sp.dma_start(bias[:, :], g.i["bias"]).then_inc(loaded, 16)
            sp.dma_start(sinks[:, :], g.i["sinks_a_2"].to_broadcast([P, AH])).then_inc(loaded, 16)

        @block.tensor
        def _(pe):
            def score(i):
                b, h, t = items[i]
                lo, n = keys(i)
                if i >= 2:
                    pe.wait_ge(biased, i - 1)
                half = slice(64 * (h % 2), 64 * (h % 2) + 64)
                q = (g.qbT if b else g.qaT)[half, h // 2, t * P:(t + 1) * P]
                k = g.kbT[half, h // 2] if b else g.kaT[half, h // (AH // AKV)]
                for j, (c0, c1) in enumerate(parts(i)):
                    mm = pe.matmul(g.ps[2 * (i % 2) + j][:, 0:c1 - c0], q, k[:, lo * P + c0:lo * P + c1], start=True, stop=True)
                mm.then_inc(qk, 1)

            def turn(i):
                lo, n = keys(i)
                pe.wait_ge(exped, i + 1)
                if i >= 1:
                    pe.wait_ge(pcopied_v, i)
                    pe.wait_ge(pcopied_a, i)
                for j in range(n):
                    mm = pe.transpose(g.ps[4 + j // 4][:, (j % 4) * P:(j % 4 + 1) * P], pr[:, i % 2, j * P:(j + 1) * P], g.c("ident"))
                mm.then_inc(pturned, 1)

            def value(i):
                b, h, t = items[i]
                lo, n = keys(i)
                pe.wait_ge(pcopied_v, i + 1)
                pe.wait_ge(pcopied_a, i + 1)
                if i >= 2:
                    pe.wait_ge(out_ok, i - 1)
                for j in range(n):
                    v = g.vb[:, lo + j, h * HD:(h + 1) * HD] if b else g.va[:, lo + j, h // (AH // AKV) * HD:(h // (AH // AKV) + 1) * HD]
                    mm = pe.matmul(g.ps[6 + i % 2][:, 0:HD], pT[:, i % 2, j, :], v, start=(j == 0), stop=(j == n - 1))
                mm.then_inc(pv, 1)

            N = len(items)
            for i in range(N + 3):
                if i < N:
                    score(i)
                if 2 <= i < N + 2:
                    turn(i - 2)
                if i >= 3:
                    value(i - 3)

        def copy(act, i):
            n = keys(i)[1]
            act.wait_ge(pcopied_v, i + 1)
            if n > 4:
                act.activation(pT[:, i % 2, 4:n, :].rearrange("p k t -> p (k t)"), g.ps[5][:, 0:(n - 4) * P], ACT.Copy).then_inc(pcopied_a, 1)
            else:
                act.nop().then_inc(pcopied_a, 1)

        @block.scalar
        def _(act):
            for i, (b, h, t) in enumerate(items):
                n = keys(i)[1]
                act.wait_ge(maxed, i + 1)
                if i >= 2:
                    act.wait_ge(pturned, i - 1)
                if not b:
                    act.activation(e[:, i % 4:i % 4 + 1], sinks[:, h:h + 1], ACT.Exp, bias=m[:, i % 4:i % 4 + 1])
                act.activation(pr[:, i % 2, 0:n * P], s[:, i % 2, 0:n * P], ACT.Exp, bias=m[:, i % 4:i % 4 + 1],
                               accum_out=l[:, i % 4:i % 4 + 1]).then_inc(exped, 1)
                if i >= 1:
                    copy(act, i - 1)
            copy(act, len(items) - 1)

        @block.vector
        def _(dve):
            step = Chain(dve, chain_v)
            dve.wait_ge(loaded, 32)

            def soft(i):
                b, h, t = items[i]
                lo, n = keys(i)
                dve.wait_ge(qk, i + 1)
                if i >= 2:
                    dve.wait_ge(exped, i - 1)
                if i >= 4:
                    dve.wait_ge(out_ok, i - 3)
                at = (KT - 1 - t) * P if b else T + (2 - n) * P
                mi = m[:, i % 4:i % 4 + 1]
                for j, (c0, c1) in enumerate(parts(i)):
                    last = dve.tensor_tensor(s[:, i % 2, c0:c1], g.ps[2 * (i % 2) + j][:, 0:c1 - c0], bias[:, at + c0:at + c1], ALU.add)
                last.then_inc(biased, 1)
                dve.wait_ge(biased, i + 1)
                step(dve.tensor_reduce(mi, s[:, i % 2, 0:n * P], AX, ALU.max))
                if b:
                    dve.tensor_scalar(mi, mi, -1.0, None, ALU.mult).then_inc(maxed, 1)
                else:
                    dve.tensor_scalar(mi, mi, sinks[:, h:h + 1], -1.0, ALU.max, ALU.mult).then_inc(maxed, 1)

            def put(i):
                n = min(4, keys(i)[1])
                dve.wait_ge(pturned, i + 1)
                if i >= 2:
                    dve.wait_ge(pv, i - 1)
                dve.tensor_copy(pT[:, i % 2, 0:n, :].rearrange("p k t -> p (k t)"), g.ps[4][:, 0:n * P]).then_inc(pcopied_v, 1)

            def finish(i):
                b, h, t = items[i]
                li = l[:, i % 4:i % 4 + 1]
                dve.wait_ge(exped, i + 1)
                if not b:
                    step(dve.tensor_tensor(li, li, e[:, i % 4:i % 4 + 1], ALU.add))
                step(dve.reciprocal(li, li))
                dve.wait_ge(pv, i + 1)
                gate = (g.gb if b else g.ga)[:, t, h * HD:(h + 1) * HD]
                dve.scalar_tensor_tensor(gate, g.ps[6 + i % 2][:, 0:HD], li, gate, ALU.mult, ALU.mult).then_inc(out_ok, 1)

            N = len(items)
            for i in range(N + 3):
                if i < N:
                    soft(i)
                if 2 <= i < N + 2:
                    put(i - 2)
                if i >= 3:
                    finish(i - 3)


def phase_second_out(nc, g, ctx0):
    with ExitStack() as ctx:
        wo = sb(nc, ctx, "w_out2_sb", [P, KT, D])
        mT = sb(nc, ctx, "mixT", [P, 2, KT, P])
        xin = sb(nc, ctx, "x2_again", [P, 2, D])
        x_in = ring_sems(nc, ctx0, "so_x_in", 2)
        w_in, turned, put_v, put_a, prod, ok = sems(nc, ctx0, "so_w_in", "so_turned", "so_put_v", "so_put_a", "so_prod", "so_ok")
        block = ctx.enter_context(nc.Block())
        out_v = g.out[0].rearrange("(t p) d -> t p d", p=P)

        @block.sync
        def _(sp):
            sp.dma_start(wo[:, :, :], g.i["w_out_2"].rearrange("l (k p) n -> p (l k) n", p=P)).then_inc(w_in, 16)

            def store(t):
                sp.wait_ge(ok, t + 1)
                sp.dma_start(out_v[t], xin[:, t % 2, :]).then_inc(g.out_done[t % 2], 16)

            for t in range(TT):
                if t >= 2:
                    sp.wait_ge(g.out_done[t % 2], 16 * (t // 2))
                sp.dma_start(xin[:, t % 2, :], g.x2_rows[t]).then_inc(x_in[t % 2], 16)
                if t >= 1:
                    store(t - 1)
            store(TT - 1)
            for r in range(2):
                sp.wait_ge(g.out_done[r], 16 * TT // 2)

        @block.tensor
        def _(pe):
            def turn(t):
                if t >= 1:
                    pe.wait_ge(put_v, t)
                    pe.wait_ge(put_a, t)
                for k in range(KT):
                    src = (g.ga if k < 4 else g.gb)[:, t, (k % 4) * P:(k % 4 + 1) * P]
                    mm = pe.transpose(g.ps[4 + k // 4][:, (k % 4) * P:(k % 4 + 1) * P], src, g.c("ident"))
                mm.then_inc(turned, 1)

            turn(0)
            pe.wait_ge(w_in, 16)
            for t in range(TT):
                pe.wait_ge(put_v, t + 1)
                pe.wait_ge(put_a, t + 1)
                if t + 1 < TT:
                    turn(t + 1)
                if t >= 2:
                    pe.wait_ge(ok, t - 1)
                for k in range(KT):
                    for h in range(2):
                        mm = pe.matmul(g.ps[2 * (t % 2) + h][:, :], mT[:, t % 2, k, :], wo[:, k, h * 512:(h + 1) * 512],
                                       start=(k == 0), stop=(k == KT - 1))
                mm.then_inc(prod, 1)

        @block.scalar
        def _(act):
            for t in range(TT):
                act.wait_ge(turned, t + 1)
                if t >= 2:
                    act.wait_ge(prod, t - 1)
                act.activation(mT[:, t % 2, 4:8, :].rearrange("p k t -> p (k t)"), g.ps[5][:, :], ACT.Copy).then_inc(put_a, 1)

        @block.vector
        def _(dve):
            def put(t):
                dve.wait_ge(turned, t + 1)
                if t >= 2:
                    dve.wait_ge(prod, t - 1)
                dve.tensor_copy(mT[:, t % 2, 0:4, :].rearrange("p k t -> p (k t)"), g.ps[4][:, :]).then_inc(put_v, 1)

            put(0)
            for t in range(TT):
                if t + 1 < TT:
                    put(t + 1)
                dve.wait_ge(prod, t + 1)
                dve.wait_ge(x_in[t % 2], 16 * (t // 2 + 1))
                for h in range(2):
                    w = slice(h * 512, (h + 1) * 512)
                    last = dve.tensor_tensor(xin[:, t % 2, w], xin[:, t % 2, w], g.ps[2 * (t % 2) + h][:, :], ALU.add)
                last.then_inc(ok, 1)


def phase_second(nc, g, signals):
    with ExitStack() as ctx:
        g.qaT = sb(nc, ctx, "qaT", [P, 4, T])
        g.kaT = sb(nc, ctx, "kaT", [P, AKV, T])
        g.qbT = sb(nc, ctx, "qbT", [P, 4, T])
        g.kbT = sb(nc, ctx, "kbT", [P, 4, T])
        g.va = sb(nc, ctx, "va", [P, TT, AKV * HD])
        g.vb = sb(nc, ctx, "vb", [P, TT, BH * HD])
        g.ga = sb(nc, ctx, "ga", [P, TT, AH * HD])
        g.gb = sb(nc, ctx, "gb", [P, TT, BH * HD])
        phase_second_project(nc, g, signals)
        phase_second_attend(nc, g, signals)
        phase_second_out(nc, g, signals)


def build(nc, args, out):
    g = Shared()
    g.i = args
    g.out = out
    g.rkv = nc.dram_tensor("rkv_scratch", [NCH, P, 4, HP, C], F32).ap()
    g.xn_rows = nc.dram_tensor("xn_rows", [T, D], F32).ap()
    g.moe = nc.dram_tensor("moe_rows", [T, D], F32).ap()
    g.x1_rows = nc.dram_tensor("x1_rows", [T, D], F32).ap()
    x2 = nc.dram_tensor("x2_rows", [T, D], F32).ap()
    g.x2_rows = x2.rearrange("(t p) d -> t p d", p=P)

    def flat(name):
        a = args[name]
        n = len(a.shape)
        if n == 1:
            return a
        names = " ".join("abcd"[:n])
        return a.rearrange(f"{names} -> ({names})")

    g.flat = flat
    with ExitStack() as ctx:
        g.ps = [ctx.enter_context(nc.psum_tensor(f"bank{b}", [P, 512], F32)) for b in range(8)]
        g.const = sb(nc, ctx, "const", [P, NCONST])
        g.pcol = sb(nc, ctx, "pcol", [P, NROWS])
        g.pcol2 = sb(nc, ctx, "pcol2", [P, 24])
        g.cond = sb(nc, ctx, "cond", [P, KT, 2])
        g.mod = sb(nc, ctx, "mod", [P, 48, 2])
        g.g2 = sb(nc, ctx, "g2_row", [P, D])
        g.a2 = sb(nc, ctx, "a2", [P, KT])
        g.valsT = sb(nc, ctx, "valsT", [P, NE])
        g.idxT = sb(nc, ctx, "idxT", [P, NE], U32)
        g.omu = sb(nc, ctx, "omu", [P, NRW])
        g.mus = sb(nc, ctx, "mus", [P, NRW, 6])

        def c(name):
            at, n = CONST_AT[name]
            return g.const[:, at:at + n]

        def p(name):
            at, n = ROW_AT[name]
            return g.pcol[:, at:at + n]

        g.c, g.p = c, p
        lasting = Signals(nc)
        g.combined = ring_sems(nc, lasting, "combined", 3)
        g.out_done = ring_sems(nc, lasting, "out_done", 2)
        signals = Signals(nc)
        phase_params(nc, g, signals)
        phase_modulation(nc, g, signals, "first", range(4))
        with ExitStack() as mid:
            g.bT = sb(nc, mid, "bT", [P, 4, T])
            g.yT = sb(nc, mid, "yT", [P, HP, T])
            g.lora = sb(nc, mid, "lora", [P, TA])
            g.xg = sb(nc, mid, "xg", [P, T])
            phase_project(nc, g, signals)
            phase_wkv(nc, g, signals)
            signals.clear()
            phase_heads_out(nc, g, signals)
            phase_modulation(nc, g, signals, "second", range(4, 12))
            phase_mix_out(nc, g, signals)
        signals.clear()
        phase_experts(nc, g, signals)
        phase_combine(nc, g, signals)
        signals.clear()
        phase_second(nc, g, signals)


_INS = ['x', 'c', 'ctx', 'c_ctx', 'ada_w', 'ada_b', 'norm1_g', 'norm2_g', 'w_in', 'shift_mu', 'w0', 'w_lora_up', 'a0',
        'a_lora_up', 'k_k', 'k_a', 'r_k', 'g_lora_up', 'gn_g', 'gn_b', 'conv_w', 'w_out', 'router_w', 'exp_w_gate',
        'exp_w_up', 'exp_w_down', 'final_g', 'norm_gain_2', 'w_in_2', 'q_norm_a_2', 'k_norm_a_2', 'sinks_a_2',
        'q_norm_b_2', 'k_norm_b_2', 'w_out_2']


def kernel(**inputs):
    import concourse.bacc as _bacc
    from concourse.bass_utils import run_bass_kernel_spmd as _run

    nc = _bacc.Bacc("TRN2", target_bir_lowering=False, num_devices=1)
    arrays, args = {}, {}
    for name in _INS:
        a = np.ascontiguousarray(inputs[name])
        arrays[f"in_{name}_dram"] = a
        args[name] = nc.dram_tensor(f"in_{name}_dram", a.shape, mybir.dt.from_np(a.dtype), kind="ExternalInput").ap()
    for name, a in (("consts", CONSTS), ("rope", _rope_tables()), ("bias", _bias_tables())):
        arrays[f"in_{name}_dram"] = a
        args[name] = nc.dram_tensor(f"in_{name}_dram", a.shape, F32, kind="ExternalInput").ap()
    out = nc.dram_tensor("out_0_dram", (1, T, D), F32, kind="ExternalOutput").ap()
    build(nc, args, out)
    r = _run(nc, [arrays], core_ids=[0])
    return r.results[0]["out_0_dram"]
```

```python
from contextlib import ExitStack

import numpy as np

import concourse.bass as bass
from concourse import mybir

F32 = mybir.dt.float32
F32R = mybir.dt.float32r
U32 = mybir.dt.uint32
ALU = mybir.AluOpType
ACT = mybir.ActivationFunctionType
AX = mybir.AxisListType.X

P = 128
D = 1024
KT = D // P
T = 1024
TT = T // P
TC = 256
TA = TC + T
GRID = 64
REP = 48
C = 64
NCH = TA // C
NCC = TC // C
HD = 64
HP = 4
NRW = 14
NE = 16
CAP = 128
KAPPA = float(np.exp(-0.5))
EPS = 1e-6
GN_EPS = 64e-5
NEG = -1e30

LEVELS = (1, 2, 4, 8, 16, 32)
CONST_AT = {}


def _constants():
    p = np.arange(P)[:, None]
    j = np.arange(P)[None, :]
    t = np.arange(C)[None, :]
    q = p % C
    parts = {
        "ident": (p == j),
        "head": (p // C == j // C),
        "chunk": np.broadcast_to((np.arange(4 * C) % C != 0)[None, :], (P, 4 * C)),
        "maskf": np.concatenate([q < t, q <= t], 1),
        "maskb": np.concatenate([q > t, q >= t], 1),
    }
    for m in LEVELS:
        between = (q // (2 * m) == t // (2 * m)) & (q // m != t // m)
        if m == 1:
            parts["lev1"] = between
        parts[f"lev{m}i"] = between | (q == t)
    parts["eps"] = np.full((P, 1), EPS)
    parts["gn_eps"] = np.full((P, 1), GN_EPS)
    parts["pick"] = np.concatenate([p % 4 == i for i in range(4)] + [p % 2 == i for i in range(2)], 1)
    at, cols = 0, []
    for name, a in parts.items():
        CONST_AT[name] = (at, a.shape[1])
        at += a.shape[1]
        cols.append(a)
    return np.ascontiguousarray(np.concatenate(cols, 1).astype(np.float32))


def _rope_tables():
    half = HD // 2
    inv = (np.float32(10000.0) ** (-np.arange(half, dtype=np.float32) / np.float32(half))).astype(np.float32)
    ang = (np.arange(T, dtype=np.float32)[:, None] * inv[None, :]).astype(np.float32)
    cos, sin = np.cos(ang), np.sin(ang)
    full = np.concatenate([cos, cos, -sin, sin], 1).astype(np.float32)
    return np.ascontiguousarray(full.reshape(TT, P, 4 * half).transpose(1, 0, 2).reshape(P, TT * 4 * half))


def _bias_tables():
    p = np.arange(P)[:, None]
    dist = p + (T - P) - np.arange(T)[None, :]
    n = ((dist >= 0) & (dist <= 128)).astype(np.float32)
    n += (dist >= 0) & (dist <= 512) & (dist % 4 == 0)
    n += (dist >= 0) & (dist <= 2048) & (dist % 16 == 0)
    dil = np.where(n > 0, np.log(np.maximum(n, 1.0)), NEG)
    da = p + P - np.arange(2 * P)[None, :]
    win = np.where((da >= 0) & (da <= 127), 0.0, NEG)
    return np.ascontiguousarray(np.concatenate([dil, win], 1).astype(np.float32))


CONSTS = _constants()
NCONST = CONSTS.shape[1]

ROWS = [("ada_b", 48), ("norm1_g", 8), ("norm2_g", 8), ("shift_mu", 14), ("w0", 8), ("a0", 8), ("k_k", 4),
        ("k_a", 4), ("r_k", 4), ("gn_g", 4), ("gn_b", 4), ("conv_w", 12)]
ROW_AT = {}
_n = 0
for _name, _k in ROWS:
    ROW_AT[_name] = (_n, _k)
    _n += _k
NROWS = _n
ROWS2 = [("c", 8), ("c_ctx", 8), ("norm_gain_2", 8)]


class Chain:

    def __init__(self, eng, sem):
        self.eng, self.sem, self.n = eng, sem, 0

    def __call__(self, ins):
        self.n += 1
        ins.then_inc(self.sem, 1)
        self.eng.wait_ge(self.sem, self.n)


class Shared:
    pass


def sb(nc, ctx, name, shape, dt=F32):
    return ctx.enter_context(nc.sbuf_tensor(name, shape, dt))


class Signals:

    def __init__(self, nc):
        self.nc, self.held = nc, []

    def new(self, name):
        self.held.append(self.nc.alloc_semaphore(name=name))
        return self.held[-1]

    def clear(self):
        self.nc.clear_and_free_semaphores(self.held)
        self.held = []
        self.nc.all_engine_barrier()


def sems(nc, signals, *names):
    return [signals.new(n) for n in names]


def ring_sems(nc, signals, name, n):
    return [signals.new(f"{name}{i}") for i in range(n)]


def phase_params(nc, g, ctx0):
    with ExitStack() as ctx:
        prow = sb(nc, ctx, "prow", [P, P])
        prow2 = sb(nc, ctx, "prow2", [24, P])
        sig = sb(nc, ctx, "sig_c", [P, 16])
        loaded, rows_t, cols, sig_ok, chain_v = sems(nc, ctx0, "par_loaded", "par_turned", "par_cols", "par_sig", "par_chain")
        block = ctx.enter_context(nc.Block())
        n_loads = len(ROWS) + len(ROWS2) + 1

        @block.sync
        def _(sp):
            sp.dma_start(g.const[:, :], g.i["consts"]).then_inc(loaded, 16)
            for name, k in ROWS:
                flat = g.flat(name)
                at = ROW_AT[name][0]
                sp.dma_start(prow[at:at + k, :], flat.rearrange("(r n) -> r n", n=P)).then_inc(loaded, 16)
            at = 0
            for name, k in ROWS2:
                sp.dma_start(prow2[at:at + k, :], g.flat(name).rearrange("(r n) -> r n", n=P)).then_inc(loaded, 16)
                at += k

        @block.tensor
        def _(pe):
            pe.wait_ge(loaded, 16 * n_loads)
            pe.transpose(g.ps[0][:, 0:NROWS], prow[0:NROWS, :], g.c("ident")[0:NROWS, 0:NROWS]).then_inc(rows_t, 1)
            pe.transpose(g.ps[1][:, 0:24], prow2[:, :], g.c("ident")[0:24, 0:24]).then_inc(rows_t, 1)

        @block.scalar
        def _(act):
            act.wait_ge(cols, 2)
            act.activation(sig[:, :], g.pcol2[:, 0:16], ACT.Sigmoid).then_inc(sig_ok, 1)

        @block.vector
        def _(dve):
            step = Chain(dve, chain_v)
            dve.wait_ge(rows_t, 2)
            dve.tensor_copy(g.pcol[:, :], g.ps[0][:, 0:NROWS]).then_inc(cols, 1)
            dve.tensor_copy(g.pcol2[:, :], g.ps[1][:, 0:24]).then_inc(cols, 1)
            dve.wait_ge(sig_ok, 1)
            step(dve.tensor_tensor(g.cond[:, :, :].rearrange("p k j -> p j k"),
                                   g.pcol2[:, 0:16].rearrange("p (j k) -> p j k", j=2),
                                   sig[:, :].rearrange("p (j k) -> p j k", j=2), ALU.mult))
            mu = g.p("shift_mu")
            dve.tensor_scalar(g.omu[:, :], mu, -1.0, 1.0, ALU.mult, ALU.add)
            for i in range(6):
                at = CONST_AT["pick"][0] + i
                last = dve.tensor_scalar(g.mus[:, :, i], mu, g.const[:, at:at + 1], None, ALU.mult)
            step(last)


def phase_modulation(nc, g, ctx0, tag, blocks):
    RING = 3
    with ExitStack() as ctx:
        w = sb(nc, ctx, f"ada_w_{tag}", [P, RING, KT, 512])
        w_in = ring_sems(nc, ctx0, f"ada_in_{tag}", RING)
        done, taken = sems(nc, ctx0, f"ada_done_{tag}", f"ada_taken_{tag}")
        block = ctx.enter_context(nc.Block())
        adaw = g.i["ada_w"].rearrange("l (k p) n -> p (l k) n", p=P)

        @block.sync
        def _(sp):
            for n, b in enumerate(blocks):
                if n >= RING:
                    sp.wait_ge(done, n - RING + 1)
                sp.dma_start(w[:, n % RING, :, :], adaw[:, :, b * 512:(b + 1) * 512]).then_inc(w_in[n % RING], 16)

        @block.tensor
        def _(pe):
            for n, b in enumerate(blocks):
                pe.wait_ge(w_in[n % RING], 16 * (n // RING + 1))
                if n >= 2:
                    pe.wait_ge(taken, n - 1)
                for m in range(4):
                    for k in range(KT):
                        mm = pe.matmul(g.ps[n % 2][:, m * P:m * P + REP * 2], w[:, n % RING, k, m * P:(m + 1) * P],
                                       g.cond[:, k, :].unsqueeze(1).to_broadcast([P, REP, 2]), start=(k == 0), stop=(k == KT - 1))
                mm.then_inc(done, 1)

        @block.vector
        def _(dve):
            for n, b in enumerate(blocks):
                dve.wait_ge(done, n + 1)
                dve.tensor_tensor(g.mod[:, 4 * b:4 * b + 4, :],
                                  g.ps[n % 2][:, :].rearrange("p (m j) -> p m j", j=P)[:, :, 0:2],
                                  g.p("ada_b")[:, 4 * b:4 * b + 4].unsqueeze(2).to_broadcast([P, 4, 2]),
                                  ALU.add).then_inc(taken, 1)


def phase_project(nc, g, ctx0):
    NX = TA // P
    XR, WR, SR, RR, MR = 3, 2, 3, 4, 2
    THIRDS = ((0, 512), (512, 1024), (1024, TA))
    order = []
    order.append(("rw", 0))
    for i in range(4):
        order += [("rw", 4 + i), ("b", i), ("c", i), ("u", i)]
    order += [("rw", j) for j in (1, 2, 3, 8, 9, 10, 11, 13, 12)]

    def column(kind, j):
        return j * P if kind == "rw" else NRW * P + "bcu".index(kind) * 512 + j * P

    NT = len(order)
    kept = [(n, j) for n, (kind, j) in enumerate(order) if kind == "rw" and j < 12]
    kept_no = {j: q for q, (n, j) in enumerate(kept)}
    HEADS = [n + 2 for n, (kind, j) in enumerate(order) if kind == "rw" and 4 <= j < 8]
    with ExitStack() as ctx:
        hTh = sb(nc, ctx, "hT_hi", [P, KT, TA], F32R)
        hTl = sb(nc, ctx, "hT_lo", [P, KT, TA], F32R)
        whole = sb(nc, ctx, "h_whole", [P, 3, KT, P])
        ss = sb(nc, ctx, "x_ss", [P, NX])
        rs = sb(nc, ctx, "x_rs", [P, NX])
        w = sb(nc, ctx, "w_in_ring", [P, WR, KT, P])
        wh = sb(nc, ctx, "w_in_hi", [P, SR, KT, P], F32R)
        wl = sb(nc, ctx, "w_in_lo", [P, SR, KT, P], F32R)
        raw = sb(nc, ctx, "raw", [P, RR, TA])
        flat_raw = raw[:, :, :].rearrange("p r t -> p (r t)")
        xin = flat_raw[:, 0:XR * D].rearrange("p (r d) -> p r d", r=XR)
        sq = flat_raw[:, XR * D:(XR + 1) * D]
        mix = sb(nc, ctx, "mix", [P, MR, TA])
        ksq = sb(nc, ctx, "ksq", [P, TA])
        kn = sb(nc, ctx, "kn", [P, TA])
        a1 = sb(nc, ctx, "a1", [P, KT, 2])
        xg_all = ksq
        x_in = ring_sems(nc, ctx0, "pj_x_in", XR)
        w_l = ring_sems(nc, ctx0, "pj_w_in", WR)
        stored = ring_sems(nc, ctx0, "pj_stored", 3)
        (sumsq, scaled, turned, put_v, put_a, ready, prod, copied, mixed, ksq_ok, khead, kk_ok, chain_v,
         khread, kcopied, rooted, kroot, h_hi, h_lo, w_hi, w_lo) = sems(nc, ctx0, "pj_sumsq", "pj_scaled", "pj_turned", "pj_put_v", "pj_put_a", "pj_ready", "pj_prod",
                      "pj_copied", "pj_mixed", "pj_ksq", "pj_khead", "pj_kk", "pj_chain", "pj_khread", "pj_kc", "pj_rooted", "pj_kroot",
                      "pj_h_hi", "pj_h_lo", "pj_w_hi", "pj_w_lo")
        block = ctx.enter_context(nc.Block())
        ctx_v = g.i["ctx"].rearrange("a (t p) d -> (a t) p d", p=P)
        x_v = g.i["x"].rearrange("a (t p) d -> (a t) p d", p=P)
        win = g.i["w_in"].rearrange("l (k p) n -> p (l k) n", p=P)
        scr = g.rkv.rearrange("c p a h t -> a h p c t")

        @block.sync
        def _(sp):
            def load_w(n):
                kind, j = order[n]
                if n >= WR:
                    sp.wait_ge(w_lo, n - WR + 1)
                at = column(kind, j)
                sp.dma_start(w[:, n % WR, :, :], win[:, :, at:at + P]).then_inc(w_l[n % WR], 16)

            for i in range(NX):
                if i >= XR:
                    sp.wait_ge(turned, i - XR + 1)
                src = ctx_v[i] if i < 2 else x_v[i - 2]
                sp.dma_start(xin[:, i % XR, :], src).then_inc(x_in[i % XR], 16)
                if i == XR - 1:
                    for n in range(WR):
                        load_w(n)
            for n in range(WR, NT):
                load_w(n)

        @block.gpsimd
        def _(pool):
            for i in range(NX):
                pool.wait_ge(h_hi, i + 1)
                pool.tensor_tensor(hTl[:, :, i * P:(i + 1) * P], whole[:, i % 3, :, :], hTh[:, :, i * P:(i + 1) * P], ALU.subtract).then_inc(h_lo, 1)
            for q, (n, j) in enumerate(kept):
                pool.wait_ge(mixed, n + 1)
                pool.dma_start(scr[j // 4, j % 4], mix[:, q % MR, :].rearrange("p (c t) -> p c t", t=C)).then_inc(stored[q % MR], 16)
                if 4 <= j < 8:
                    pool.wait_ge(kk_ok, j - 3)
                    pool.dma_start(scr[3, j % 4], kn[:, :].rearrange("p (c t) -> p c t", t=C)).then_inc(stored[2], 16)
            for r in range(MR):
                pool.wait_ge(stored[r], 16 * (len(kept) // MR))
            pool.wait_ge(stored[2], 16 * 4)

        def put_tile(act, i):
            j = 1 if i < 2 else 0
            act.wait_ge(ready, 1)
            act.wait_ge(turned, i + 1)
            if i >= 3:
                act.wait_ge(h_lo, i - 2)
            for k in range(4, 8):
                last = act.activation(whole[:, i % 3, k, :], g.ps[2 * (i % 2) + 1][:, (k - 4) * P:(k - 3) * P],
                                      ACT.Identity, scale=a1[:, k, j:j + 1], bias=g.mod[:, k, j:j + 1])
            last.then_inc(put_a, 1)

        def split_tile(act, i):
            act.wait_ge(put_a, i + 1)
            act.wait_ge(put_v, i + 1)
            act.activation(hTh[:, :, i * P:(i + 1) * P], whole[:, i % 3, :, :], ACT.Copy).then_inc(h_hi, 1)

        def split_w(act, n):
            act.wait_ge(w_l[n % WR], 16 * (n // WR + 1))
            if n >= SR:
                act.wait_ge(prod, n - SR + 1)
            act.activation(wh[:, n % SR, :, :], w[:, n % WR, :, :], ACT.Copy).then_inc(w_hi, 1)

        @block.scalar
        def _(act):
            for i in range(NX):
                act.wait_ge(x_in[i % XR], 16 * (i // XR + 1))
                act.activation(sq[:, :], xin[:, i % XR, :], ACT.Square, accum_out=ss[:, i:i + 1]).then_inc(sumsq, 1)
                act.wait_ge(sumsq, i + 1)
                act.activation(rs[:, i:i + 1], ss[:, i:i + 1], ACT.Sqrt, scale=1.0 / D, bias=g.c("eps")).then_inc(rooted, 1)
                if i >= 2:
                    put_tile(act, i - 2)
                if i >= 3:
                    split_tile(act, i - 3)
            put_tile(act, NX - 2)
            split_tile(act, NX - 3)
            put_tile(act, NX - 1)
            split_tile(act, NX - 2)
            split_tile(act, NX - 1)
            for n in range(SR):
                split_w(act, n)
            for n in range(NT):
                kind, j = order[n]
                act.wait_ge(prod, n + 1)
                if n >= RR:
                    act.wait_ge(mixed, n - RR + 1)
                a = 3 * (n % 2)
                if kind == "rw":
                    act.activation(raw[:, n % RR, 0:TC], g.ps[a][:, 0:TC], ACT.Copy)
                act.activation(raw[:, n % RR, TC:TC + 512], g.ps[a + 1][:, :], ACT.Copy)
                act.activation(raw[:, n % RR, TC + 512:TA], g.ps[a + 2][:, :], ACT.Copy).then_inc(copied, 1)
                if n + SR < NT:
                    split_w(act, n + SR)
                if n in HEADS:
                    for q, (lo, hi) in enumerate(THIRDS):
                        act.wait_ge(khread, 3 * HEADS.index(n) + q + 1)
                        act.activation(ksq[:, lo:hi], ksq[:, lo:hi], ACT.Sqrt).then_inc(kroot, 1)
                if kind == "rw" and 4 <= j < 8:
                    act.wait_ge(ksq_ok, j - 3)
                    act.activation(ksq[:, :], kn[:, :], ACT.Square).then_inc(kcopied, 1)

        @block.vector
        def _(dve):
            step = Chain(dve, chain_v)
            step(dve.tensor_scalar(a1[:, :, :], g.mod[:, 8:16, :], 1.0, None, ALU.add))
            dve.tensor_tensor(a1[:, :, :], a1[:, :, :], g.p("norm1_g").unsqueeze(2).to_broadcast([P, KT, 2]), ALU.mult).then_inc(ready, 1)

            def put(i):
                j = 1 if i < 2 else 0
                dve.wait_ge(ready, 1)
                dve.wait_ge(turned, i + 1)
                if i >= 3:
                    dve.wait_ge(h_lo, i - 2)
                for k in range(4):
                    last = dve.tensor_scalar(whole[:, i % 3, k, :], g.ps[2 * (i % 2)][:, k * P:(k + 1) * P],
                                             a1[:, k, j:j + 1], g.mod[:, k, j:j + 1], ALU.mult, ALU.add)
                last.then_inc(put_v, 1)

            for i in range(NX):
                dve.wait_ge(rooted, i + 1)
                step(dve.reciprocal(rs[:, i:i + 1], rs[:, i:i + 1]))
                dve.tensor_scalar(xin[:, i % XR, :], xin[:, i % XR, :], rs[:, i:i + 1], None, ALU.mult).then_inc(scaled, 1)
                if i >= 2:
                    put(i - 2)
            put(NX - 2)
            put(NX - 1)

            def split_lo(n):
                dve.wait_ge(w_hi, n + 1)
                dve.tensor_tensor(wl[:, n % SR, :, :], w[:, n % WR, :, :], wh[:, n % SR, :, :], ALU.subtract).then_inc(w_lo, 1)

            for n in range(SR):
                split_lo(n)

            def shift(n, j, dst):
                src = raw[:, n % RR, :]
                step(dve.tensor_scalar(dst, src, g.omu[:, j:j + 1], None, ALU.mult))
                s = src[:, TC:TA].rearrange("p (r c) -> p r c", c=GRID)
                d = dst[:, TC:TA].rearrange("p (r c) -> p r c", c=GRID)
                pairs = [(d[:, :, 1:], s[:, :, :-1]), (d[:, :, :-1], s[:, :, 1:]),
                         (d[:, 1:, :], s[:, :-1, :]), (d[:, :-1, :], s[:, 1:, :]),
                         (dst[:, 1:TC], src[:, 0:TC - 1]), (dst[:, 0:TC - 1], src[:, 1:TC])]
                for i, (o, f) in enumerate(pairs):
                    ins = dve.scalar_tensor_tensor(o, f, g.mus[:, j, i:i + 1], o, ALU.mult, ALU.add)
                    if i < 5:
                        step(ins)
                return ins

            def finish_key(h):
                for q, (lo, hi) in enumerate(THIRDS):
                    dve.wait_ge(khead, 3 * h + q + 1)
                    dve.tensor_scalar(ksq[:, lo:hi], g.ps[6 + q % 2][:, 0:hi - lo], 1e-24, None, ALU.max).then_inc(khread, 1)
                for q, (lo, hi) in enumerate(THIRDS):
                    sl = ksq[:, lo:hi]
                    dve.wait_ge(kroot, 3 * h + q + 1)
                    step(dve.reciprocal(sl, sl))
                    last = dve.tensor_tensor(kn[:, lo:hi], kn[:, lo:hi], sl, ALU.mult)
                last.then_inc(kk_ok, 1)

            for n in range(NT):
                kind, j = order[n]
                if n + SR < NT:
                    split_lo(n + SR)
                if n in HEADS:
                    finish_key(HEADS.index(n))
                if kind == "rw":
                    dve.wait_ge(copied, n + 1)
                    slot = kept_no.get(j, 0) % MR
                    if j < 12 and kept_no[j] >= MR:
                        dve.wait_ge(stored[slot], 16 * (kept_no[j] // MR))
                    dst = mix[:, slot, :] if j < 12 else g.lora[:, :] if j == 12 else xg_all[:, :]
                    shift(n, j, dst).then_inc(mixed, 1)
                    dve.wait_ge(mixed, n + 1)
                if kind == "rw" and 4 <= j < 8:
                    h = j - 4
                    if h >= 1:
                        dve.wait_ge(stored[2], 16 * h)
                    dve.tensor_scalar(kn[:, :], dst, g.p("k_k")[:, h:h + 1], None, ALU.mult).then_inc(ksq_ok, 1)
                    dve.wait_ge(ksq_ok, h + 1)
                elif kind == "rw" and j == 13:
                    dve.tensor_copy(g.xg[:, :], xg_all[:, TC:TA])
                elif kind == "u":
                    dve.wait_ge(copied, n + 1)
                    rb, rc, ru = (raw[:, m % RR, TC:TA] for m in (n - 2, n - 1, n))
                    cw = g.p("conv_w")
                    o = g.bT[:, j, :]
                    step(dve.tensor_tensor(ru, rc, ru, ALU.mult))
                    step(dve.tensor_scalar(o, ru, cw[:, 4 + j:5 + j], None, ALU.mult))
                    step(dve.scalar_tensor_tensor(o[:, 1:], ru[:, :-1], cw[:, j:j + 1], o[:, 1:], ALU.mult, ALU.add))
                    step(dve.scalar_tensor_tensor(o[:, :-1], ru[:, 1:], cw[:, 8 + j:9 + j], o[:, :-1], ALU.mult, ALU.add))
                    dve.tensor_tensor(o, o, rb, ALU.mult).then_inc(mixed, 3)

        @block.tensor
        def _(pe):
            for i in range(NX):
                pe.wait_ge(scaled, i + 1)
                if i >= 2:
                    pe.wait_ge(put_v, i - 1)
                    pe.wait_ge(put_a, i - 1)
                for k in range(KT):
                    mm = pe.transpose(g.ps[2 * (i % 2) + k // 4][:, (k % 4) * P:(k % 4 + 1) * P],
                                      xin[:, i % XR, k * P:(k + 1) * P], g.c("ident"))
                mm.then_inc(turned, 1)
            pe.wait_ge(h_lo, NX)
            for n in range(NT):
                kind, j = order[n]
                pe.wait_ge(w_lo, n + 1)
                if n >= 2:
                    pe.wait_ge(copied, n - 1)
                a = 3 * (n % 2)
                parts = ((wl, hTh), (wh, hTl), (wh, hTh))
                for k in range(KT):
                    for p, (lhs, rhs) in enumerate(parts):
                        lhsT = lhs[:, n % SR, k, :]
                        at = dict(start=(k == 0 and p == 0), stop=(k == KT - 1 and p == 2))
                        if kind == "rw":
                            pe.matmul(g.ps[a][:, 0:TC], lhsT, rhs[:, k, 0:TC], **at)
                        pe.matmul(g.ps[a + 1][:, :], lhsT, rhs[:, k, TC:TC + 512], **at)
                        mm = pe.matmul(g.ps[a + 2][:, :], lhsT, rhs[:, k, TC + 512:TA], **at)
                mm.then_inc(prod, 1)
                if n in HEADS:
                    h = HEADS.index(n)
                    pe.wait_ge(kcopied, h + 1)
                    for q, (lo, hi) in enumerate(THIRDS):
                        if 3 * h + q >= 2:
                            pe.wait_ge(khread, 3 * h + q - 1)
                        pe.matmul(g.ps[6 + q % 2][:, 0:hi - lo], g.c("head"), ksq[:, lo:hi],
                                  start=True, stop=True).then_inc(khead, 1)


def phase_wkv(nc, g, ctx0):
    NU = 4
    SS = NCH // 2
    LV = range(1, len(LEVELS))
    LAST = LV[-1]
    levels_pe = [f"{k}{l}" for l in LV for k in ("zd" if l == LAST else "zdt")]
    names = {
        "pe": ["gram", "turn", "turnx"] + levels_pe + ["r0", "u", "s"],
        "dve": ["gram", "ai"] + [f"{k}{l}" for l in LV for k in ("z" if l == LAST else "zt")] + ["s"],
        "act": ["turn", "turnx"] + [f"d{l}" for l in LV] + ["r0", "u"],
        "pool": ["y0"],
        "lora": ["lora"], "dve_f": ["z", "cum", "feat"], "act_f": ["sig", "exp"], "pool_f": ["av", "ar"],
    }

    def at(engine, ss, name):
        return ss * len(names[engine]) + names[engine].index(name) + 1

    def step_of(ss, u):
        return 2 * ss + u // 2

    def chunk_of(ss, u):
        s = step_of(ss, u)
        return s if u % 2 == 0 else (NCC - 1 - s if s < NCC else NCH - 1 + NCC - s)

    def pairs(ap):
        return ap.rearrange("p (h n) -> p h n", h=HP)

    with ExitStack() as ctx:
        up = sb(nc, ctx, "lora_up", [P, 2, HP * P])
        unit = []
        for u in range(NU):
            b = Shared()
            b.chunk = sb(nc, ctx, f"chunk{u}", [P, 4, HP, C])
            work = sb(nc, ctx, f"work{u}", [P, 6, HP, C])
            feat = work if u < 2 else sb(nc, ctx, f"feat{u}", [P, 6, HP, C])
            b.sw, b.a, b.x, b.gx, b.pi, b.kd = (feat[:, i] for i in range(6))
            b.z = feat[:, 0:2]
            b.xg = feat[:, 2:4]
            b.t, b.y, b.w = (work[:, 2 * i:2 * i + 2].rearrange("p a h t -> p (a h t)") for i in range(3))
            b.r0, b.u = b.w, b.t
            b.ar = sb(nc, ctx, f"ar{u}", [P, HP, 2, C])
            b.arbd = sb(nc, ctx, f"arbd{u}", [P, HP, 2, P])
            b.gb = sb(nc, ctx, f"gb{u}", [P, HP, 2, P])
            b.gk = sb(nc, ctx, f"gk{u}", [P, HP, 2, P])
            b.end = sb(nc, ctx, f"end{u}", [P, HP])
            b.bbd, b.kbd, b.vbd, b.ai = (sb(nc, ctx, f"{n}{u}", [P, HP, P]) for n in ("bbd", "kbd", "vbd", "ai"))
            b.A, b.B = g.ps[2 * u], g.ps[2 * u + 1]
            unit.append(b)
        sbd = [[sb(nc, ctx, f"sbd{d}{q}", [P, HP, P]) for q in range(2)] for d in range(2)]
        chunk_in = ring_sems(nc, ctx0, "wk_chunk_in", NU)
        pe_done = ring_sems(nc, ctx0, "wk_products", NU)
        dve_done = ring_sems(nc, ctx0, "wk_vector", NU)
        act_done = ring_sems(nc, ctx0, "wk_scalar", NU)
        pool_done = ring_sems(nc, ctx0, "wk_pool", NU)
        lora_done = ring_sems(nc, ctx0, "wk_logits", 2)
        dve_f = ring_sems(nc, ctx0, "wk_vector_features", NU)
        act_f = ring_sems(nc, ctx0, "wk_scalar_features", NU)
        pool_f = ring_sems(nc, ctx0, "wk_pool_features", NU)
        y_done = ring_sems(nc, ctx0, "wk_y", NU)
        y_taken = ring_sems(nc, ctx0, "wk_y_taken", NU)
        up_in, zeroed, tanh_ok, chain_v, chain_a, chain_p = sems(
            nc, ctx0, "wk_up_in", "wk_zeroed", "wk_tanh", "wk_chain", "wk_chain_a", "wk_chain_p")
        block = ctx.enter_context(nc.Block())

        def nx(ss):
            return max(0, ss + 1 - NCC // 2)

        HALVES = (slice(0, C), slice(C, P))

        @block.sync
        def _(sp):
            for d in range(2):
                sp.dma_start(up[0:64, d, :], g.i["w_lora_up"][0, d]).then_inc(up_in, 16)
                sp.dma_start(up[64:128, d, :], g.i["a_lora_up"][0, d]).then_inc(up_in, 16)
            for ss in range(SS):
                for u in range(NU):
                    if ss >= 1:
                        sp.wait_ge(dve_f[u], at("dve_f", ss - 1, "feat"))
                        sp.wait_ge(pool_f[u], at("pool_f", ss - 1, "av"))
                    sp.dma_start(unit[u].chunk[:, :, :, :], g.rkv[chunk_of(ss, u)]).then_inc(chunk_in[u], 16)

        @block.gpsimd
        def _(pool):
            step = Chain(pool, chain_p)
            for b in unit:
                for m in (b.bbd, b.kbd, b.vbd):
                    pool.memset(m[:, :, :], 0.0)
                for m in (b.arbd, b.gb, b.gk):
                    pool.memset(m[:, :, :, :], 0.0)
            pool.memset(sbd[0][0][:, :, :], 0.0)
            pool.memset(sbd[1][0][:, :, :], 0.0).then_inc(zeroed, 1)
            pool.wait_ge(zeroed, 1)
            one = g.c("ident").unsqueeze(1).to_broadcast([P, HP, P])

            def features(ss, units):
                for u in units:
                    b = unit[u]
                    pool.wait_ge(chunk_in[u], 16 * (ss + 1))
                    if ss >= 1:
                        pool.wait_ge(pe_done[u], at("pe", ss - 1, "s"))
                        if nx(ss - 1):
                            pool.wait_ge(y_done[u], nx(ss - 1))
                    step(pool.tensor_copy(b.vbd[HALVES[0], :, HALVES[0]], b.chunk[HALVES[0], 2]))
                    pool.tensor_copy(b.vbd[HALVES[1], :, HALVES[1]], b.chunk[HALVES[1], 2]).then_inc(pool_f[u], 1)
                    pool.wait_ge(pool_f[u], at("pool_f", ss, "av"))
                for u in units:
                    b = unit[u]
                    pool.wait_ge(dve_f[u], at("dve_f", ss, "feat"))
                    step(pool.tensor_copy(b.arbd[HALVES[0], :, :, HALVES[0]], b.ar[HALVES[0]]))
                    pool.tensor_copy(b.arbd[HALVES[1], :, :, HALVES[1]], b.ar[HALVES[1]]).then_inc(pool_f[u], 1)
                    pool.wait_ge(pool_f[u], at("pool_f", ss, "ar"))

            features(0, (0, 1, 2, 3))
            for ss in range(SS):
                for u, b in enumerate(unit):
                    pool.wait_ge(dve_done[u], at("dve", ss, "gram"))
                    y = b.y.rearrange("p (h a t) -> p h a t", h=HP, a=2)
                    x = b.gb[:, :, 0].rearrange("p h (a t) -> p h a t", a=2)
                    for hp in range(HP):
                        last = pool.tensor_tensor(y[:, hp], x[:, hp], g.c("lev1").unsqueeze(1).to_broadcast([P, 2, C]), ALU.mult)
                    step(last)
                    pool.tensor_tensor(pairs(b.y), pairs(b.y), one, ALU.add).then_inc(pool_done[u], 1)
                if ss + 1 < SS:
                    features(ss + 1, (0, 1))
                    features(ss + 1, (2, 3))

        @block.scalar
        def _(act):
            step = Chain(act, chain_a)
            act.activation(g.lora[0:64, :], g.lora[0:64, :], ACT.Tanh).then_inc(tanh_ok, 1)
            act.wait_ge(zeroed, 1)

            def features(ss):
                for u, b in enumerate(unit):
                    act.wait_ge(dve_f[u], at("dve_f", ss, "z"))
                    act.activation(b.z, b.z, ACT.Sigmoid).then_inc(act_f[u], 1)
                for u, b in enumerate(unit):
                    act.wait_ge(dve_f[u], at("dve_f", ss, "cum"))
                    step(act.activation(b.pi, b.gx, ACT.Exp, scale=KAPPA))
                    act.activation(b.xg, b.xg, ACT.Exp, scale=-KAPPA).then_inc(act_f[u], 1)

            features(0)
            for ss in range(SS):
                for u, b in enumerate(unit):
                    act.wait_ge(pe_done[u], at("pe", ss, "turn"))
                    act.activation(b.bbd[:, :, :], pairs(b.A[:, :]), ACT.Copy)
                    act.activation(b.kbd[:, :, :], pairs(b.B[:, :]), ACT.Copy).then_inc(act_done[u], 1)
                for u, b in enumerate(unit):
                    act.wait_ge(pe_done[u], at("pe", ss, "turnx"))
                    act.activation(b.vbd[:, :, :], pairs(b.A[:, :]), ACT.Copy).then_inc(act_done[u], 1)
                for l in LV:
                    for u, b in enumerate(unit):
                        act.wait_ge(pe_done[u], at("pe", ss, f"d{l}"))
                        act.activation(b.y, b.B[:, :], ACT.Copy).then_inc(act_done[u], 1)
                for s2 in range(2):
                    for name in ("r0", "u"):
                        for d in range(2):
                            u, b = 2 * s2 + d, unit[2 * s2 + d]
                            act.wait_ge(pe_done[u], at("pe", ss, name))
                            act.activation(b.r0 if name == "r0" else b.u, (b.A if name == "r0" else b.B)[:, :], ACT.Copy).then_inc(act_done[u], 1)
                if ss + 1 < SS:
                    features(ss + 1)

        @block.vector
        def _(dve):
            step = Chain(dve, chain_v)

            def over_tokens(ap):
                return ap.unsqueeze(2).to_broadcast([P, HP, C])

            def blocks(ap):
                return ap.rearrange("p (n t) -> p n t", t=C)

            def over_blocks(ap):
                return ap.unsqueeze(1).to_broadcast([P, 2 * HP, C])

            one = g.c("ident").unsqueeze(1).to_broadcast([P, HP, P])
            flat = "p h t -> p (h t)"
            def logits(ss):
                for u, b in enumerate(unit):
                    d = u % 2
                    dve.wait_ge(lora_done[d], ss + 1)
                    if ss >= 1 and nx(ss - 1) and u < 2:
                        dve.wait_ge(y_done[u], nx(ss - 1))
                    q = u // 2 if d == 0 else 1 - u // 2
                    for bank, dst, bias in ((unit[d].A, b.sw, g.p("w0")), (unit[d].B, b.a, g.p("a0"))):
                        last = dve.tensor_tensor(dst, pairs(bank[:, :])[:, :, q * C:(q + 1) * C],
                                                 over_tokens(bias[:, d * HP:(d + 1) * HP]), ALU.add)
                    last.then_inc(dve_f[u], 1)

            def sums(ss):
                for u, b in enumerate(unit):
                    d = u % 2
                    dve.wait_ge(act_f[u], at("act_f", ss, "sig"))
                    run = b.gx if d == 0 else b.kd
                    step(dve.tensor_tensor_scan(run.rearrange(flat), g.c("chunk"), b.sw.rearrange(flat), 0.0, ALU.mult, ALU.add))
                    if d == 0:
                        step(dve.tensor_tensor(b.x, run, b.sw, ALU.subtract))
                    else:
                        step(dve.tensor_tensor(b.x, over_tokens(run[:, :, C - 1]), run, ALU.subtract))
                        step(dve.tensor_tensor(b.gx, b.x, b.sw, ALU.add))
                    dve.wait_ge(chunk_in[u], 16 * (ss + 1))
                    step(dve.scalar_tensor_tensor(b.kd, b.a, -1.0, over_tokens(g.p("k_a")), ALU.add, ALU.mult))
                    dve.scalar_tensor_tensor(b.kd, b.kd, 1.0, b.chunk[:, 1], ALU.add, ALU.mult).then_inc(dve_f[u], 1)

            def features(ss, units):
                for u in units:
                    b, d = unit[u], u % 2
                    dve.wait_ge(act_f[u], at("act_f", ss, "exp"))
                    dve.wait_ge(dve_f[u], at("dve_f", ss, "cum"))
                    if ss >= 1:
                        dve.wait_ge(pool_f[u], at("pool_f", ss - 1, "ar"))
                        dve.wait_ge(dve_done[u], at("dve", ss - 1, "s"))
                    dve.scalar_tensor_tensor(b.ar[:, :, 0], b.chunk[:, 3], -1.0, b.x, ALU.mult, ALU.mult)
                    dve.tensor_tensor(b.ar[:, :, 1], b.chunk[:, 0], b.gx, ALU.mult)
                    dve.tensor_copy(b.end[:, :], b.gx[:, :, C - 1 if d == 0 else 0])
                    step(dve.tensor_tensor(b.sw, b.a, b.pi, ALU.mult))
                    for h in HALVES:
                        dve.tensor_tensor(b.bbd[h, :, h], b.chunk[h, 3], b.sw[h], ALU.mult)
                        last = dve.tensor_tensor(b.kbd[h, :, h], b.kd[h], b.pi[h], ALU.mult)
                    last.then_inc(dve_f[u], 1)

            logits(0)
            sums(0)
            dve.wait_ge(zeroed, 1)
            features(0, (0, 1, 2, 3))
            for ss in range(SS):
                for u, b in enumerate(unit):
                    mask = g.c("maskf" if u % 2 == 0 else "maskb").rearrange("p (a t) -> p a t", a=2)
                    dve.wait_ge(pe_done[u], at("pe", ss, "gram"))
                    for bank, dst in ((b.A, b.gb), (b.B, b.gk)):
                        for h in HALVES:
                            last = dve.tensor_tensor(dst[h, :, :, h], bank[h, :].rearrange("p (h a t) -> p h a t", h=HP, a=2),
                                                     mask[h].unsqueeze(1).to_broadcast([C, HP, 2, C]), ALU.mult)
                    last.then_inc(dve_done[u], 1)
                for u, b in enumerate(unit):
                    dve.wait_ge(pe_done[u], at("pe", ss, "turnx"))
                    step(dve.tensor_tensor(b.ai[:, :, :], pairs(b.B[:, :]), one, ALU.add))
                    dve.tensor_tensor(blocks(b.t), blocks(b.ai[:, :, :].rearrange("p h n -> p (h n)")),
                                      over_blocks(g.c("lev1i")), ALU.mult).then_inc(dve_done[u], 1)
                for l in LV:
                    lev = over_blocks(g.c(f"lev{LEVELS[l]}i"))
                    for u, b in enumerate(unit):
                        dve.wait_ge(pe_done[u], at("pe", ss, f"z{l}"))
                        dve.tensor_tensor(blocks(b.w), blocks(b.A[:, :]), lev, ALU.mult).then_inc(dve_done[u], 1)
                    if l < LAST:
                        for u, b in enumerate(unit):
                            dve.wait_ge(pe_done[u], at("pe", ss, f"t{l}"))
                            dve.tensor_copy(b.t, b.A[:, :]).then_inc(dve_done[u], 1)
                for s2 in range(2):
                    for d in range(2):
                        u, b = 2 * s2 + d, unit[2 * s2 + d]
                        new = sbd[d][1 - s2]
                        dve.wait_ge(pe_done[u], at("pe", ss, "s"))
                        step(dve.tensor_tensor(new[:, :, :], pairs(b.A[:, :]), sbd[d][s2][:, :, :], ALU.add))
                        dve.tensor_tensor(new[:, :, :], new[:, :, :], b.end[:, :].unsqueeze(2).to_broadcast([P, HP, P]),
                                          ALU.mult).then_inc(dve_done[u], 1)
                    for d in range(2):
                        u, b = 2 * s2 + d, unit[2 * s2 + d]
                        s, c = step_of(ss, u), chunk_of(ss, u) - NCC
                        if s < NCC:
                            continue
                        dve.wait_ge(y_done[u], nx(ss))
                        first = s < NCC + (NCH - NCC) // 2
                        if s == NCC + (NCH - NCC) // 2:
                            for q in range(NU):
                                dve.wait_ge(y_taken[q], nx(ss - 1))
                        for h in HALVES:
                            dst = g.yT[h, :, c * C:(c + 1) * C]
                            src = pairs(b.B[h, :])[:, :, h]
                            last = dve.tensor_copy(dst, src) if first else dve.tensor_tensor(dst, dst, src, ALU.add)
                        last.then_inc(y_taken[u], 1)
                    if s2 == 0 and ss + 1 < SS:
                        logits(ss + 1)
                        sums(ss + 1)
                        features(ss + 1, (0, 1))
                if ss + 1 < SS:
                    features(ss + 1, (2, 3))

        @block.tensor
        def _(pe):
            def each(bank, *terms):
                for h in range(HP):
                    for i, (st, mv) in enumerate(terms):
                        mm = pe.matmul(bank[:, h * P:(h + 1) * P], st[:, h], mv[:, h], start=(i == 0), stop=(i == len(terms) - 1))
                return mm

            def turn(bank, src):
                for h in range(HP):
                    mm = pe.transpose(bank[:, h * P:(h + 1) * P], src[:, h], g.c("ident"))
                return mm

            pe.wait_ge(up_in, 64)
            pe.wait_ge(tanh_ok, 1)
            def logits(ss):
                for d in range(2):
                    at0 = min(chunk_of(ss, d), chunk_of(ss, d + 2)) * C
                    if ss >= 1:
                        pe.wait_ge(dve_done[d], at("dve", ss - 1, "s"))
                        if nx(ss - 1):
                            pe.wait_ge(y_taken[d], nx(ss - 1))
                    for h, bank in ((slice(0, 64), unit[d].A), (slice(64, 128), unit[d].B)):
                        for hp in range(HP):
                            mm = pe.matmul(bank[:, hp * P:(hp + 1) * P], up[h, d, hp * P:(hp + 1) * P],
                                           g.lora[h, at0:at0 + 2 * C], start=True, stop=True)
                    mm.then_inc(lora_done[d], 1)

            logits(0)
            for ss in range(SS):
                for u, b in enumerate(unit):
                    pe.wait_ge(dve_f[u], at("dve_f", ss, "feat"))
                    pe.wait_ge(dve_f[(u + 2) % 4], at("dve_f", ss, "z"))
                    if u >= 2 and nx(ss - 1):
                        pe.wait_ge(y_taken[u], nx(ss - 1))
                    ar = b.ar[:, :, :, :].rearrange("p h a t -> p h (a t)")
                    each(b.A, (b.bbd, ar))
                    each(b.B, (b.kbd, ar)).then_inc(pe_done[u], 1)
                for u, b in enumerate(unit):
                    pe.wait_ge(dve_done[u], at("dve", ss, "gram"))
                    turn(b.A, b.bbd)
                    turn(b.B, b.kbd).then_inc(pe_done[u], 1)
                for u, b in enumerate(unit):
                    pe.wait_ge(act_done[u], at("act", ss, "turn"))
                    pe.wait_ge(pool_f[u], at("pool_f", ss, "av"))
                    turn(b.A, b.vbd)
                    turn(b.B, b.gb[:, :, 0]).then_inc(pe_done[u], 1)
                for l in LV:
                    for u, b in enumerate(unit):
                        if l == 1:
                            pe.wait_ge(act_done[u], at("act", ss, "turnx"))
                            pe.wait_ge(dve_done[u], at("dve", ss, "ai"))
                            pe.wait_ge(pool_done[u], at("pool", ss, "y0"))
                        else:
                            pe.wait_ge(act_done[u], at("act", ss, f"d{l - 1}"))
                            pe.wait_ge(dve_done[u], at("dve", ss, f"t{l - 1}"))
                        each(b.A, (b.ai, pairs(b.y))).then_inc(pe_done[u], 1)
                    for u, b in enumerate(unit):
                        pe.wait_ge(dve_done[u], at("dve", ss, f"z{l}"))
                        each(b.B, (pairs(b.t), pairs(b.w))).then_inc(pe_done[u], 1)
                    if l < LAST:
                        for u, b in enumerate(unit):
                            pe.wait_ge(act_done[u], at("act", ss, f"d{l}"))
                            turn(b.A, pairs(b.y)).then_inc(pe_done[u], 1)
                for s2 in range(2):
                    for d in range(2):
                        u, b = 2 * s2 + d, unit[2 * s2 + d]
                        o, last = (u + 2) % 4, (ss if s2 else ss - 1)
                        if last >= 0:
                            pe.wait_ge(dve_done[o], at("dve", last, "s"))
                        pe.wait_ge(act_done[u], at("act", ss, f"d{LAST}"))
                        pe.wait_ge(pool_f[u], at("pool_f", ss, "ar"))
                        each(b.A, (b.arbd[:, :, 0], sbd[d][s2]), (b.gk[:, :, 0], b.vbd)).then_inc(pe_done[u], 1)
                    for d in range(2):
                        u, b = 2 * s2 + d, unit[2 * s2 + d]
                        pe.wait_ge(act_done[u], at("act", ss, "r0"))
                        each(b.B, (pairs(b.y), pairs(b.r0))).then_inc(pe_done[u], 1)
                    if s2 == 1 and ss + 1 < SS:
                        logits(ss + 1)
                    for d in range(2):
                        u, b = 2 * s2 + d, unit[2 * s2 + d]
                        pe.wait_ge(act_done[u], at("act", ss, "u"))
                        each(b.A, (b.bbd, pairs(b.u)), (b.kbd, b.vbd)).then_inc(pe_done[u], 1)
                    for d in range(2):
                        u, b = 2 * s2 + d, unit[2 * s2 + d]
                        if step_of(ss, u) < NCC:
                            continue
                        each(b.B, (sbd[d][s2], b.arbd[:, :, 1]), (pairs(b.u), b.gb[:, :, 1]), (b.vbd, b.gk[:, :, 1])).then_inc(y_done[u], 1)


def phase_heads_out(nc, g, ctx0, blocks):
    HALF = T // 2
    NP_ = 2 * HP
    pieces = [(hp, q) for hp in range(HP) for q in range(2)]
    NBANK, RING = 6, 2
    kinds = ["mean"] * NP_ + ["a0", "a1"] * NP_ + ["gate"] * NP_ + ["var", "bonus"] * NP_
    seq, seen = {}, {}
    for q, kind in enumerate(kinds):
        seq[kind, seen.get(kind, 0)] = q
        seen[kind] = seen.get(kind, 0) + 1
    with ExitStack() as ctx:
        up = sb(nc, ctx, "lora_up2", [P, 2, HP * P])
        gup = sb(nc, ctx, "g_up", [P, HP * P])
        rk = sb(nc, ctx, "rkv_back", [P, NCH - NCC, 3, HP, C])
        sq = sb(nc, ctx, "gn_sq", [P, HP, T])
        gt = sb(nc, ctx, "gate_t", [P, HP, T])
        rks = sb(nc, ctx, "rks", [P, HP, T])
        sa = sb(nc, ctx, "sig_a", [P, 2, 2, HALF])
        w = sb(nc, ctx, "ada_w_second", [P, RING, KT, 512])
        w_in = ring_sems(nc, ctx0, "ada_in_second", RING)
        modded, taken = sems(nc, ctx0, "ada_done_second", "ada_taken_second")
        adaw = g.i["ada_w"].rearrange("l (k p) n -> p (l k) n", p=P)
        loaded, rk_in, chain_v = sems(nc, ctx0, "ho_loaded", "ho_rkv_in", "ho_chain")
        done = {k: ctx0.new(f"ho_{k}") for k in ("mean", "a", "gate", "var", "bonus")}
        free = ring_sems(nc, ctx0, "ho_bank_free", NBANK)
        xg_ok, sig_a, a_read, squared, rooted, gated, rks_ok = sems(
            nc, ctx0, "ho_xg", "ho_sig_a", "ho_a_read", "ho_squared", "ho_rooted", "ho_gated", "ho_rks")
        block = ctx.enter_context(nc.Block())

        def bank(kind, i):
            return seq[kind, i] % NBANK

        def tok(t, i):
            hp, q = pieces[i]
            return t[:, hp, q * HALF:(q + 1) * HALF]

        def chunks(i, a):
            hp, q = pieces[i]
            n = (NCH - NCC) // 2
            return rk[:, q * n:(q + 1) * n, a, hp, :]

        def ch(ap):
            return ap.rearrange("p (c t) -> p c t", t=C)

        @block.sync
        def _(sp):
            for d in range(2):
                sp.dma_start(up[64:128, d, :], g.i["a_lora_up"][0, d]).then_inc(loaded, 16)
            sp.dma_start(gup[:, :], g.i["g_lora_up"][0]).then_inc(loaded, 16)
            sp.dma_start(rk[:, :, :, :, :], g.rkv[NCC:NCH, :, 0:3].rearrange("c p a h t -> p c a h t")).then_inc(rk_in, 16)
            for n, b in enumerate(blocks):
                if n >= RING:
                    sp.wait_ge(modded, n - RING + 1)
                sp.dma_start(w[:, n % RING, :, :], adaw[:, :, b * 512:(b + 1) * 512]).then_inc(w_in[n % RING], 16)

        @block.tensor
        def _(pe):
            def into(kind, i):
                q = seq[kind, i]
                if q >= NBANK:
                    pe.wait_ge(free[q % NBANK], q // NBANK)
                return g.ps[q % NBANK][:, 0:HALF]

            def modulation(n):
                pe.wait_ge(w_in[n % RING], 16 * (n // RING + 1))
                if n >= 2:
                    pe.wait_ge(taken, n - 1)
                for m in range(4):
                    for k in range(KT):
                        mm = pe.matmul(g.ps[6 + n % 2][:, m * P:m * P + REP * 2], w[:, n % RING, k, m * P:(m + 1) * P],
                                       g.cond[:, k, :].unsqueeze(1).to_broadcast([P, REP, 2]), start=(k == 0), stop=(k == KT - 1))
                mm.then_inc(modded, 1)

            for i in range(NP_):
                pe.matmul(into("mean", i), g.c("head"), tok(g.yT, i), start=True, stop=True).then_inc(done["mean"], 1)
            pe.wait_ge(loaded, 48)
            for i, (hp, q) in enumerate(pieces):
                for d in range(2):
                    pe.matmul(into(f"a{d}", i), up[64:128, d, hp * P:(hp + 1) * P],
                              g.lora[64:128, TC + q * HALF:TC + (q + 1) * HALF], start=True, stop=True).then_inc(done["a"], 1)
            pe.wait_ge(xg_ok, 1)
            for i, (hp, q) in enumerate(pieces):
                pe.matmul(into("gate", i), gup[:, hp * P:(hp + 1) * P], g.xg[:, q * HALF:(q + 1) * HALF],
                          start=True, stop=True).then_inc(done["gate"], 1)
            for i in range(NP_):
                pe.wait_ge(squared, i + 1)
                pe.matmul(into("var", i), g.c("head"), tok(sq, i), start=True, stop=True).then_inc(done["var"], 1)
                pe.wait_ge(rks_ok, i + 1)
                pe.matmul(into("bonus", i), g.c("head"), tok(rks, i), start=True, stop=True).then_inc(done["bonus"], 1)
                modulation(i)

        @block.scalar
        def _(act):
            act.activation(g.xg[:, :], g.xg[:, :], ACT.Sigmoid).then_inc(xg_ok, 1)
            for i, (hp, q) in enumerate(pieces):
                if i >= 2:
                    act.wait_ge(a_read, i - 1)
                for d in range(2):
                    act.wait_ge(done["a"], 2 * i + d + 1)
                    b = bank(f"a{d}", i)
                    act.activation(sa[:, i % 2, d, :], g.ps[b][:, :], ACT.Sigmoid,
                                   bias=g.p("a0")[:, d * HP + hp:d * HP + hp + 1]).then_inc(free[b], 1)
            for i in range(NP_):
                act.wait_ge(done["gate"], i + 1)
                act.activation(tok(gt, i), g.ps[bank("gate", i)][:, :], ACT.Copy).then_inc(free[bank("gate", i)], 1)
            for i in range(NP_):
                act.wait_ge(free[bank("mean", i)], seq["mean", i] // NBANK + 1)
                act.activation(tok(sq, i), tok(g.yT, i), ACT.Square).then_inc(squared, 1)
            for i in range(NP_):
                act.wait_ge(done["var"], i + 1)
                act.activation(tok(sq, i), g.ps[bank("var", i)][:, :], ACT.Sqrt, scale=1.0 / HD, bias=g.c("gn_eps")).then_inc(free[bank("var", i)], 1)

        @block.vector
        def _(dve):
            step = Chain(dve, chain_v)
            for i in range(NP_):
                b = bank("mean", i)
                dve.wait_ge(done["mean"], i + 1)
                dve.scalar_tensor_tensor(tok(g.yT, i), g.ps[b][:, :], -1.0 / HD, tok(g.yT, i), ALU.mult, ALU.add).then_inc(free[b], 1)
            dve.wait_ge(rk_in, 16)
            for i, (hp, q) in enumerate(pieces):
                dve.wait_ge(free[bank("a1", i)], seq["a1", i] // NBANK + 1)
                dve.wait_ge(free[bank("a0", i)], seq["a0", i] // NBANK + 1)
                o = tok(rks, i)
                dve.tensor_tensor(o, sa[:, i % 2, 0, :], sa[:, i % 2, 1, :], ALU.add).then_inc(a_read, 1)
                dve.wait_ge(a_read, i + 1)
                step(dve.tensor_scalar(o, o, -2.0, g.p("k_a")[:, hp:hp + 1], ALU.add, ALU.mult))
                step(dve.scalar_tensor_tensor(ch(o), ch(o), 2.0, chunks(i, 1), ALU.add, ALU.mult))
                dve.scalar_tensor_tensor(ch(o), ch(o), g.p("r_k")[:, hp:hp + 1], chunks(i, 0), ALU.mult, ALU.mult).then_inc(rks_ok, 1)
            for i, (hp, q) in enumerate(pieces):
                b, o, s = bank("var", i), tok(g.yT, i), tok(sq, i)
                dve.wait_ge(free[b], seq["var", i] // NBANK + 1)
                step(dve.reciprocal(s, s))
                step(dve.tensor_tensor(o, o, s, ALU.mult))
                step(dve.tensor_scalar(o, o, g.p("gn_g")[:, hp:hp + 1], g.p("gn_b")[:, hp:hp + 1], ALU.mult, ALU.add))
                b = bank("bonus", i)
                dve.wait_ge(done["bonus"], i + 1)
                dve.tensor_tensor(ch(s), ch(g.ps[b][:, :]), chunks(i, 2), ALU.mult).then_inc(free[b], 1)
                dve.wait_ge(free[b], seq["bonus", i] // NBANK + 1)
                step(dve.tensor_tensor(o, o, s, ALU.add))
                dve.wait_ge(free[bank("gate", i)], seq["gate", i] // NBANK + 1)
                step(dve.tensor_tensor(o, o, tok(gt, i), ALU.mult))
                dve.wait_ge(modded, i + 1)
                m = 4 * blocks[i]
                dve.tensor_tensor(g.mod[:, m:m + 4, :],
                                  g.ps[6 + i % 2][:, :].rearrange("p (m j) -> p m j", j=P)[:, :, 0:2],
                                  g.p("ada_b")[:, m:m + 4].unsqueeze(2).to_broadcast([P, 4, 2]),
                                  ALU.add).then_inc(taken, 1)


def phase_mix_out(nc, g, ctx0):
    with ExitStack() as ctx:
        wraw = sb(nc, ctx, "w_out_raw", [P, 3, D])
        wh = sb(nc, ctx, "w_out_hi", [P, KT, D], F32R)
        wl = sb(nc, ctx, "w_out_lo", [P, KT, D], F32R)
        mh = sb(nc, ctx, "mix_hi", [P, 2, KT, P], F32R)
        ml = sb(nc, ctx, "mix_lo", [P, 2, KT, P], F32R)
        ones = sb(nc, ctx, "ones", [P, P])
        diag = sb(nc, ctx, "diag", [P, 4, P])
        g1 = sb(nc, ctx, "g1_row", [P, D])
        xin = sb(nc, ctx, "x_again", [P, 2, D])
        x1 = sb(nc, ctx, "x1", [P, 2, D])
        sq = sb(nc, ctx, "x1_sq", [P, D])
        ss = sb(nc, ctx, "x1_ss", [P, TT])
        rs = sb(nc, ctx, "x1_rs", [P, TT])
        xn = sb(nc, ctx, "x1n", [P, 2, D])
        h2 = sb(nc, ctx, "h2T", [P, 2, KT, P])
        rw = sb(nc, ctx, "router", [P, KT, NE])
        aff = sb(nc, ctx, "aff", [P, TT, NE])
        mx = sb(nc, ctx, "aff_max", [P, TT])
        w_hi, w_lo, m_hi, m_lo, rw_in, row_ok, row_done, gcols, chain_v, chain_a = sems(
            nc, ctx0, "mo_w_hi", "mo_w_lo", "mo_mix_hi", "mo_mix_lo", "mo_router_in", "mo_row", "mo_row_done", "mo_cols", "mo_chain", "mo_chain_a")
        x_in = ring_sems(nc, ctx0, "mo_x_in", 2)
        w_in = ring_sems(nc, ctx0, "mo_w_in", 3)
        st1 = ring_sems(nc, ctx0, "mo_x1_out", 2)
        stn = ring_sems(nc, ctx0, "mo_xn_out", 2)
        prod, x1_ok, sumsq, xn_ok, turned, h2_ok, logit, ex_ok, shifted, aff_ok, aff_t, diag_ok = sems(
            nc, ctx0, "mo_prod", "mo_x1", "mo_sumsq", "mo_xn", "mo_turned", "mo_h2", "mo_logits", "mo_exp", "mo_shifted",
            "mo_aff", "mo_aff_turned", "mo_diag")
        block = ctx.enter_context(nc.Block())
        x_v = g.i["x"].rearrange("a (t p) d -> (a t) p d", p=P)
        x1_v = g.x1_rows.rearrange("(t p) d -> t p d", p=P)
        xn_v = g.xn_rows.rearrange("(t p) d -> t p d", p=P)

        def store(sp, t):
            sp.wait_ge(x1_ok, t + 1)
            sp.dma_start(x1_v[t], x1[:, t % 2, :]).then_inc(st1[t % 2], 16)
            sp.wait_ge(xn_ok, t + 1)
            sp.dma_start(xn_v[t], xn[:, t % 2, :]).then_inc(stn[t % 2], 16)

        @block.sync
        def _(sp):
            for k in range(KT):
                if k >= 3:
                    sp.wait_ge(w_lo, k - 2)
                sp.dma_start(wraw[:, k % 3, :], g.i["w_out"][0, k * P:(k + 1) * P, :]).then_inc(w_in[k % 3], 16)
            sp.dma_start(rw[:, :, :], g.i["router_w"].rearrange("l (k p) n -> p (l k) n", p=P)).then_inc(rw_in, 16)
            for t in range(TT):
                if t >= 2:
                    sp.wait_ge(x1_ok, t - 1)
                sp.dma_start(xin[:, t % 2, :], x_v[t]).then_inc(x_in[t % 2], 16)
                if t >= 1:
                    store(sp, t - 1)
            store(sp, TT - 1)
            for r in range(2):
                sp.wait_ge(st1[r], 16 * TT // 2)
                sp.wait_ge(stn[r], 16 * TT // 2)

        @block.gpsimd
        def _(pool):
            for t in range(TT):
                pool.wait_ge(m_hi, t + 1)
                if t >= 2:
                    pool.wait_ge(prod, t - 1)
                pool.tensor_tensor(ml[:, t % 2, 0:4, :], g.yT[:, :, t * P:(t + 1) * P], mh[:, t % 2, 0:4, :], ALU.subtract)
                pool.tensor_tensor(ml[:, t % 2, 4:8, :], g.bT[:, :, t * P:(t + 1) * P], mh[:, t % 2, 4:8, :], ALU.subtract).then_inc(m_lo, 1)

        @block.tensor
        def _(pe):
            pe.wait_ge(row_ok, 1)
            for n in range(4):
                pe.wait_ge(diag_ok, n + 1)
                if n >= 2:
                    pe.wait_ge(row_done, n - 1)
                for k in range(4):
                    mm = pe.matmul(g.ps[n % 2][:, k * P:(k + 1) * P], ones[:, :], diag[:, k, :], start=True, stop=True)
                mm.then_inc(gcols, 1)
            pe.wait_ge(row_done, 4)

            def turn(t):
                pe.wait_ge(xn_ok, t + 1)
                if t >= 1:
                    pe.wait_ge(h2_ok, t)
                for k in range(KT):
                    mm = pe.transpose(g.ps[4 + k // 4][:, (k % 4) * P:(k % 4 + 1) * P], xn[:, t % 2, k * P:(k + 1) * P], g.c("ident"))
                mm.then_inc(turned, 1)

            def route(t):
                pe.wait_ge(h2_ok, t + 1)
                for k in range(KT):
                    mm = pe.matmul(g.ps[6][:, t * NE:(t + 6) * NE], h2[:, t % 2, k, :],
                                   rw[:, k, :].unsqueeze(1).to_broadcast([P, 6, NE]), start=(k == 0), stop=(k == KT - 1))
                mm.then_inc(logit, 1)

            pe.wait_ge(rw_in, 16)
            for t in range(TT):
                if t >= 2:
                    pe.wait_ge(x1_ok, t - 1)
                pe.wait_ge(m_lo, t + 1)
                for k in range(KT):
                    if t == 0:
                        pe.wait_ge(w_lo, k + 1)
                    for p, (lhs, rhs) in enumerate(((ml, wh), (mh, wl), (mh, wh))):
                        for h in range(2):
                            mm = pe.matmul(g.ps[2 * (t % 2) + h][:, :], lhs[:, t % 2, k, :], rhs[:, k, h * 512:(h + 1) * 512],
                                           start=(k == 0 and p == 0), stop=(k == KT - 1 and p == 2))
                mm.then_inc(prod, 1)
                if t >= 1:
                    turn(t - 1)
                if t >= 2:
                    route(t - 2)
            turn(TT - 1)
            route(TT - 2)
            route(TT - 1)
            pe.wait_ge(aff_ok, 1)
            for t in range(TT):
                mm = pe.transpose(g.ps[t // 4][0:NE, (t % 4) * P:(t % 4 + 1) * P], aff[:, t, :], g.c("ident"))
            mm.then_inc(aff_t, 1)

        @block.scalar
        def _(act):
            def split_mix(t):
                if t >= 2:
                    act.wait_ge(prod, t - 1)
                act.activation(mh[:, t % 2, 0:4, :], g.yT[:, :, t * P:(t + 1) * P], ACT.Copy)
                act.activation(mh[:, t % 2, 4:8, :], g.bT[:, :, t * P:(t + 1) * P], ACT.Copy).then_inc(m_hi, 1)

            split_mix(0)
            split_mix(1)
            for k in range(KT):
                act.wait_ge(w_in[k % 3], 16 * (k // 3 + 1))
                act.activation(wh[:, k, :], wraw[:, k % 3, :], ACT.Copy).then_inc(w_hi, 1)
            for t in range(TT):
                act.wait_ge(x1_ok, t + 1)
                act.activation(sq[:, :], x1[:, t % 2, :], ACT.Square, accum_out=ss[:, t:t + 1]).then_inc(chain_a, 1)
                act.wait_ge(chain_a, t + 1)
                act.activation(rs[:, t:t + 1], ss[:, t:t + 1], ACT.Sqrt, scale=1.0 / D, bias=g.c("eps")).then_inc(sumsq, 1)
                if t + 2 < TT:
                    split_mix(t + 2)
                act.wait_ge(turned, t + 1)
                if t >= 2:
                    act.wait_ge(logit, t - 1)
                for k in range(KT):
                    last = act.activation(h2[:, t % 2, k, :], g.ps[4 + k // 4][:, (k % 4) * P:(k % 4 + 1) * P], ACT.Identity,
                                          scale=g.a2[:, k:k + 1], bias=g.mod[:, 24 + k, 0:1])
                last.then_inc(h2_ok, 1)
            act.wait_ge(shifted, 1)
            act.activation(aff[:, :, :], aff[:, :, :], ACT.Exp).then_inc(ex_ok, 1)

        @block.vector
        def _(dve):
            step = Chain(dve, chain_v)
            dve.memset(ones[:, :], 1.0).then_inc(row_ok, 1)
            for n in range(4):
                base = (16, 20, 40, 44)[n]
                if n >= 1:
                    dve.wait_ge(gcols, n)
                for k in range(4):
                    last = dve.tensor_scalar(diag[:, k, :], g.c("ident"), g.mod[:, base + k, 0:1], None, ALU.mult)
                last.then_inc(diag_ok, 1)
                dve.wait_ge(gcols, n + 1)
                dst = g1 if n < 2 else g.g2
                dve.tensor_copy(dst[:, (n % 2) * 512:(n % 2 + 1) * 512], g.ps[n % 2][:, :]).then_inc(row_done, 1)
            dve.wait_ge(row_done, 4)
            for k in range(KT):
                dve.wait_ge(w_hi, k + 1)
                dve.tensor_tensor(wl[:, k, :], wraw[:, k % 3, :], wh[:, k, :], ALU.subtract).then_inc(w_lo, 1)
            step(dve.tensor_scalar(g.a2[:, :], g.mod[:, 32:40, 0], 1.0, None, ALU.add))
            step(dve.tensor_tensor(g.a2[:, :], g.a2[:, :], g.p("norm2_g"), ALU.mult))
            for t in range(TT):
                dve.wait_ge(prod, t + 1)
                dve.wait_ge(x_in[t % 2], 16 * (t // 2 + 1))
                if t >= 2:
                    dve.wait_ge(st1[t % 2], 16 * (t // 2))
                    dve.wait_ge(stn[t % 2], 16 * (t // 2))
                for h in range(2):
                    w = slice(h * 512, (h + 1) * 512)
                    last = dve.tensor_tensor(x1[:, t % 2, w], g.ps[2 * (t % 2) + h][:, :], g1[:, w], ALU.mult)
                step(last)
                dve.tensor_tensor(x1[:, t % 2, :], x1[:, t % 2, :], xin[:, t % 2, :], ALU.add).then_inc(x1_ok, 1)
                dve.wait_ge(sumsq, t + 1)
                if t >= 2:
                    dve.wait_ge(turned, t - 1)
                step(dve.reciprocal(rs[:, t:t + 1], rs[:, t:t + 1]))
                dve.tensor_scalar(xn[:, t % 2, :], x1[:, t % 2, :], rs[:, t:t + 1], None, ALU.mult).then_inc(xn_ok, 1)
            dve.wait_ge(logit, TT)
            lg = g.ps[6][:, 0:TT * NE].rearrange("p (t e) -> p t e", e=NE)

            def wide(ap):
                return ap.unsqueeze(2).to_broadcast([P, TT, NE])

            step(dve.tensor_reduce(mx[:, :], lg, AX, ALU.max))
            dve.tensor_tensor(aff[:, :, :], lg, wide(mx[:, :]), ALU.subtract).then_inc(shifted, 1)
            dve.wait_ge(ex_ok, 1)
            step(dve.tensor_reduce(mx[:, :], aff[:, :, :], AX, ALU.add))
            step(dve.reciprocal(mx[:, :], mx[:, :]))
            dve.tensor_tensor(aff[:, :, :], aff[:, :, :], wide(mx[:, :]), ALU.mult).then_inc(aff_ok, 1)
            dve.wait_ge(aff_t, 1)
            dve.tensor_copy(g.affT[:, 0:512], g.ps[0][0:NE, :])
            dve.tensor_copy(g.affT[:, 512:T], g.ps[1][0:NE, :])


def phase_experts(nc, g, ctx0):
    RING, RH = 3, 3
    HALF = KT // 2
    loads = []
    for e in range(NE):
        loads += [("gate", e, 0), ("gate", e, 1), ("up", e, 0), ("up", e, 1)]
        if e >= 1:
            loads += [("down", e - 1, 0), ("down", e - 1, 1)]
    loads += [("down", NE - 1, 0), ("down", NE - 1, 1)]
    place = {x: n for n, x in enumerate(loads)}
    with ExitStack() as ctx:
        w = sb(nc, ctx, "exp_w", [P, RING, HALF, D])
        wl = sb(nc, ctx, "exp_w_lo", [P, RH, HALF, D], F32R)
        wh = sb(nc, ctx, "exp_w_hi", [P, RH, HALF, D], F32R)
        xs = sb(nc, ctx, "xs", [P, 2, D])
        xsT = sb(nc, ctx, "xsT", [P, KT, P])
        xsl = sb(nc, ctx, "xsT_lo", [P, KT, P], F32R)
        xsh = sb(nc, ctx, "xsT_hi", [P, KT, P], F32R)
        sg = sb(nc, ctx, "sg", [P, D])
        hid = sb(nc, ctx, "hid", [P, D])
        hidh = sb(nc, ctx, "hidT_hi", [P, KT, P], F32R)
        hidl = sb(nc, ctx, "hidT_lo", [P, KT, P], F32R)
        o = sb(nc, ctx, "exp_out", [P, 2, D])
        vals = sb(nc, ctx, "vals", [NE, CAP])
        idx = sb(nc, ctx, "idx", [NE, CAP], U32)
        idxf = sb(nc, ctx, "idxf", [NE, CAP])
        zero = hid
        w_in = ring_sems(nc, ctx0, "ex_w_in", RING)
        x_in = ring_sems(nc, ctx0, "ex_x_in", 2)
        (w_read, hi_ok, lo_ok, xs_t, xs_put, xs_hi, xs_ok, sig, gs, hid_ok, hid_t, hid_hi, hidT_ok, o_ok, added, zeroed,
         z_ok, top, top_t, picked, chain_v) = sems(
            nc, ctx0, "ex_w_read", "ex_w_hi", "ex_w_lo", "ex_xs_turned", "ex_xs_put", "ex_xs_hi", "ex_xsT", "ex_sig",
            "ex_gs", "ex_hid", "ex_hid_turned", "ex_hid_hi", "ex_hidT", "ex_out", "ex_added", "ex_zeroed", "ex_zero_row",
            "ex_top", "ex_top_turned", "ex_picked", "ex_chain")
        block = ctx.enter_context(nc.Block())

        def after(kind, e):
            return place[kind, e, 1] + 1

        src = {"gate": g.i["exp_w_gate"], "up": g.i["exp_w_up"], "down": g.i["exp_w_down"]}
        tasks = {}
        for e in range(NE):
            tasks[after("gate", e)] = ("gate", e)
            tasks[after("up", e)] = ("up", e)
            tasks[after("down", e)] = ("down", e)

        @block.sync
        def _(sp):
            for n, (kind, e, h) in enumerate(loads):
                if n >= RING:
                    sp.wait_ge(lo_ok, n - RING + 1)
                sp.dma_start(w[:, n % RING, :, :], src[kind][0, e].rearrange("(k p) n -> p k n", p=P)[:, h * HALF:(h + 1) * HALF, :]).then_inc(w_in[n % RING], 16)

        @block.gpsimd
        def _(pool):
            def gather(e):
                if e >= 2:
                    pool.wait_ge(xs_t, e - 1)
                pool.indirect_dma_start(xs[:, e % 2, :], None, g.xn_rows, bass.IndirectOffsetOnAxis(ap=g.idxT[:, e:e + 1], axis=0)).then_inc(x_in[e % 2], 16)

            pool.memset(zero[:, :], 0.0).then_inc(z_ok, 1)
            pool.wait_ge(z_ok, 1)
            moe_v = g.moe.rearrange("(t p) d -> t p d", p=P)
            for t in range(TT):
                pool.dma_start(moe_v[t], zero[:, :]).then_inc(zeroed, 16)
            pool.wait_ge(zeroed, 16 * TT)
            pool.wait_ge(picked, 1)
            gather(0)
            gather(1)
            for e in range(NE):
                if e + 2 < NE:
                    gather(e + 2)
                pool.wait_ge(o_ok, e + 1)
                if e >= 1:
                    pool.wait_ge(added, 16 * e)
                pool.indirect_dma_start(g.moe, bass.IndirectOffsetOnAxis(ap=g.idxT[:, e:e + 1], axis=0), o[:, e % 2, :], None,
                                        compute_op=ALU.add).then_inc(added, 16)
            pool.wait_ge(added, 16 * NE)

        @block.tensor
        def _(pe):
            def turn_xs(e):
                pe.wait_ge(x_in[e % 2], 16 * (e // 2 + 1))
                if e >= 2:
                    pe.wait_ge(hidT_ok, e - 1)
                v = xs[:, e % 2, :].rearrange("p (k q) -> p k q", k=KT)
                for k in range(KT):
                    mm = pe.transpose(g.ps[k // 4][:, (k % 4) * P:(k % 4 + 1) * P], v[:, k], g.c("ident"))
                mm.then_inc(xs_t, 1)

            def turn_hid(e):
                pe.wait_ge(hid_ok, e + 1)
                if e + 1 < NE:
                    pe.wait_ge(xs_put, e + 2)
                v = hid[:, :].rearrange("p (k q) -> p k q", k=KT)
                for k in range(KT):
                    mm = pe.transpose(g.ps[k // 4][:, (k % 4) * P:(k % 4 + 1) * P], v[:, k], g.c("ident"))
                mm.then_inc(hid_t, 1)

            def product(kind, e, bank, lhs_hi, lhs_lo):
                for h in range(2):
                    n = place[kind, e, h]
                    pe.wait_ge(lo_ok, n + 1)
                    for k in range(HALF):
                        kk = h * HALF + k
                        for p, (lhs, wide) in enumerate(((lhs_lo, wh[:, n % RH]), (lhs_hi, wl[:, n % RH]), (lhs_hi, wh[:, n % RH]))):
                            for q in range(2):
                                mm = pe.matmul(g.ps[bank + q][:, :], lhs[:, kk, :], wide[:, k, q * 512:(q + 1) * 512],
                                               start=(kk == 0 and p == 0), stop=(kk == KT - 1 and p == 2))
                    mm.then_inc(w_read, 1)

            pe.wait_ge(top, 1)
            pe.transpose(g.ps[7][:, 0:NE], vals[:, :], g.c("ident")[0:NE, 0:NE])
            pe.transpose(g.ps[7][:, NE:2 * NE], idxf[:, :], g.c("ident")[0:NE, 0:NE]).then_inc(top_t, 1)
            turn_xs(0)
            for e in range(NE + 1):
                if e < NE:
                    pe.wait_ge(xs_ok, e + 1)
                    if e >= 1:
                        pe.wait_ge(hid_ok, e)
                    product("gate", e, 2, xsh, xsl)
                    product("up", e, 4, xsh, xsl)
                if e + 1 < NE:
                    turn_xs(e + 1)
                if e >= 1:
                    pe.wait_ge(hidT_ok, e)
                    pe.wait_ge(picked, 1)
                    if e >= 2:
                        pe.wait_ge(o_ok, e - 1)
                    product("down", e - 1, 6, hidh, hidl)
                if e < NE:
                    turn_hid(e)

        @block.scalar
        def _(act):
            def split(n):
                act.wait_ge(w_in[n % RING], 16 * (n // RING + 1))
                if n >= RH:
                    act.wait_ge(w_read, n - RH + 1)
                for k in range(HALF):
                    last = act.activation(wh[:, n % RH, k, :], w[:, n % RING, k, :], ACT.Copy)
                last.then_inc(hi_ok, 1)

            def put_xs(e):
                act.wait_ge(xs_t, e + 1)
                for k in range(KT):
                    last = act.activation(xsT[:, k, :], g.ps[k // 4][:, (k % 4) * P:(k % 4 + 1) * P], ACT.Identity,
                                          scale=g.a2[:, k:k + 1], bias=g.mod[:, 24 + k, 0:1])
                last.then_inc(xs_put, 1)
                act.wait_ge(xs_put, e + 1)
                act.activation(xsh[:, :, :], xsT[:, :, :], ACT.Copy).then_inc(xs_hi, 1)

            split(0)
            split(1)
            put_xs(0)
            split(2)
            for n in range(1, len(loads) + 1):
                kind, e = tasks.get(n, ("", 0))
                if kind == "gate":
                    act.wait_ge(w_read, n)
                    if e >= 1:
                        act.wait_ge(hid_ok, e)
                    act.activation(sg[:, 0:512], g.ps[2][:, :], ACT.Sigmoid).then_inc(sig, 1)
                    act.activation(sg[:, 512:D], g.ps[3][:, :], ACT.Sigmoid).then_inc(sig, 1)
                if kind == "up" and e + 1 < NE:
                    put_xs(e + 1)
                turned = 0 if (kind, e) == ("up", 0) else e + 1 if kind == "down" and e + 1 < NE else -1
                if turned >= 0:
                    act.wait_ge(hid_t, turned + 1)
                    for q in range(2):
                        last = act.activation(hidh[:, 4 * q:4 * q + 4, :].rearrange("p k t -> p (k t)"), g.ps[q][:, :], ACT.Copy)
                    last.then_inc(hid_hi, 1)
                if n + 2 < len(loads):
                    split(n + 2)

        @block.vector
        def _(dve):
            step = Chain(dve, chain_v)

            def split(n):
                dve.wait_ge(hi_ok, n + 1)
                if n >= RH:
                    dve.wait_ge(w_read, n - RH + 1)
                dve.tensor_tensor(wl[:, n % RH, :, :], w[:, n % RING, :, :], wh[:, n % RH, :, :], ALU.subtract).then_inc(lo_ok, 1)

            def split_xs(e):
                dve.wait_ge(xs_hi, e + 1)
                dve.tensor_tensor(xsl[:, :, :], xsT[:, :, :], xsh[:, :, :], ALU.subtract).then_inc(xs_ok, 1)

            def split_hid(e):
                dve.wait_ge(hid_hi, e + 1)
                for q in range(2):
                    last = dve.tensor_tensor(hidl[:, 4 * q:4 * q + 4, :].rearrange("p k t -> p (k t)"), g.ps[q][:, :],
                                             hidh[:, 4 * q:4 * q + 4, :].rearrange("p k t -> p (k t)"), ALU.subtract)
                last.then_inc(hidT_ok, 1)

            for r in range(CAP // 8):
                v = vals[:, 8 * r:8 * r + 8]
                step(dve.max(v, g.affT[:, :]))
                step(dve.max_index(idx[:, 8 * r:8 * r + 8], v, g.affT[:, :]))
                step(dve.match_replace(g.affT[:, :], v, g.affT[:, :], -1.0))
            dve.tensor_copy(idxf[:, :], idx[:, :]).then_inc(top, 1)
            split(0)
            dve.wait_ge(top_t, 1)
            dve.tensor_copy(g.valsT[:, :], g.ps[7][:, 0:NE])
            dve.tensor_copy(g.idxT[:, :], g.ps[7][:, NE:2 * NE]).then_inc(picked, 1)
            split(1)
            split_xs(0)
            split(2)
            dve.wait_ge(zeroed, 16 * TT)
            for n in range(1, len(loads) + 1):
                kind, e = tasks.get(n, ("", 0))
                if kind == "gate":
                    for q in range(2):
                        s = slice(q * 512, (q + 1) * 512)
                        dve.wait_ge(sig, 2 * e + q + 1)
                        if e >= 1:
                            dve.wait_ge(hid_t, e)
                        dve.tensor_tensor(hid[:, s], sg[:, s], g.ps[2 + q][:, :], ALU.mult).then_inc(gs, 1)
                if kind == "up":
                    dve.wait_ge(gs, 2 * e + 2)
                    dve.wait_ge(w_read, n)
                    for q in range(2):
                        s = slice(q * 512, (q + 1) * 512)
                        last = dve.tensor_tensor(hid[:, s], hid[:, s], g.ps[4 + q][:, :], ALU.mult)
                    last.then_inc(hid_ok, 1)
                    if e + 1 < NE:
                        split_xs(e + 1)
                if kind == "down":
                    dve.wait_ge(w_read, n)
                    if e >= 2:
                        dve.wait_ge(added, 16 * (e - 1))
                    for q in range(2):
                        s = slice(q * 512, (q + 1) * 512)
                        last = dve.tensor_scalar(o[:, e % 2, s], g.ps[6 + q][:, :], g.valsT[:, e:e + 1], None, ALU.mult)
                    last.then_inc(o_ok, 1)
                turned = 0 if (kind, e) == ("up", 0) else e + 1 if kind == "down" and e + 1 < NE else -1
                if turned >= 0:
                    split_hid(turned)
                if n + 2 < len(loads):
                    split(n + 2)


def phase_combine(nc, g, ctx0):
    XR = 4
    with ExitStack() as ctx:
        x1 = sb(nc, ctx, "cb_x1", [P, XR, D])
        mo = sb(nc, ctx, "cb_moe", [P, 3, D])
        sq = sb(nc, ctx, "cb_sq", [P, D])
        fg = sb(nc, ctx, "final_row", [P, D])
        ss = sb(nc, ctx, "cb_ss", [P, 2, TT])
        rs = sb(nc, ctx, "cb_rs", [P, 2, TT])
        xn = sb(nc, ctx, "cb_xn", [P, 2, D])
        whole = sb(nc, ctx, "cb_whole", [P, 3, KT, P])
        hh = sb(nc, ctx, "cb_hi", [P, 2, KT, P], F32R)
        hl = sb(nc, ctx, "cb_lo", [P, 2, KT, P], F32R)
        ins = ring_sems(nc, ctx0, "cb_x1_in", XR)
        mins = ring_sems(nc, ctx0, "cb_moe_in", 3)
        outs, h_out = g.combined, g.h_out
        (row_in, gated, x2_ok, rooted, ok, rooted2, scaled, turned, put_v, put_a, h_hi, h_lo, chain_v, chain_a) = sems(
            nc, ctx0, "cb_row", "cb_gated", "cb_x2", "cb_rooted", "cb_ok", "cb_rooted2", "cb_scaled", "cb_turned",
            "cb_put_v", "cb_put_a", "cb_h_hi", "cb_h_lo", "cb_chain", "cb_chain_a")
        block = ctx.enter_context(nc.Block())
        x1_v = g.x1_rows.rearrange("(t p) d -> t p d", p=P)
        mo_v = g.moe.rearrange("(t p) d -> t p d", p=P)

        @block.sync
        def _(sp):
            def load(t):
                if t >= XR:
                    sp.wait_ge(outs[t % XR], 16 * (t // XR))
                    sp.wait_ge(scaled, t - XR + 1)
                sp.dma_start(x1[:, t % XR, :], x1_v[t]).then_inc(ins[t % XR], 16)
                if t >= 3:
                    sp.wait_ge(x2_ok, t - 2)
                sp.dma_start(mo[:, t % 3, :], mo_v[t]).then_inc(mins[t % 3], 16)

            for i in range(TT + 2):
                if i < TT:
                    load(i)
                if i == 0:
                    sp.dma_start(fg[:, :], g.i["final_g"].rearrange("(a d) -> a d", a=1).to_broadcast([P, D])).then_inc(row_in, 16)
                if 2 <= i < TT + 2:
                    sp.wait_ge(ok, i - 1)
                    sp.dma_start(g.x2_rows[i - 2], x1[:, (i - 2) % XR, :]).then_inc(outs[(i - 2) % XR], 16)
            for r in range(XR):
                sp.wait_ge(outs[r], 16 * (TT // XR))

        @block.gpsimd
        def _(pool):
            def gate(t):
                pool.wait_ge(mins[t % 3], 16 * (t // 3 + 1))
                pool.tensor_tensor(mo[:, t % 3, :], mo[:, t % 3, :], g.g2[:, :], ALU.mult).then_inc(gated, 1)

            gate(0)
            for i in range(TT + 3):
                if i + 1 < TT:
                    gate(i + 1)
                if i >= 3:
                    n = i - 3
                    pool.wait_ge(h_hi, n + 1)
                    if n >= 2:
                        pool.wait_ge(h_out[n % 2], 32 * (n // 2))
                    pool.tensor_tensor(hl[:, n % 2, :, :], whole[:, n % 3, :, :], hh[:, n % 2, :, :], ALU.subtract).then_inc(h_lo, 1)

        @block.tensor
        def _(pe):
            for t in range(TT):
                pe.wait_ge(scaled, t + 1)
                if t >= 2:
                    pe.wait_ge(put_v, t - 1)
                    pe.wait_ge(put_a, t - 1)
                for k in range(KT):
                    mm = pe.transpose(g.ps[2 * (t % 2) + k // 4][:, (k % 4) * P:(k % 4 + 1) * P], xn[:, t % 2, k * P:(k + 1) * P], g.c("ident"))
                mm.then_inc(turned, 1)

        @block.scalar
        def _(act):
            def root(t, j, done):
                act.wait_ge(x2_ok if j == 0 else ok, t + 1)
                act.activation(sq[:, :], x1[:, t % XR, :], ACT.Square, accum_out=ss[:, j, t:t + 1]).then_inc(chain_a, 1)
                root.n += 1
                act.wait_ge(chain_a, root.n)
                act.activation(rs[:, j, t:t + 1], ss[:, j, t:t + 1], ACT.Sqrt, scale=1.0 / D, bias=g.c("eps")).then_inc(done, 1)

            def store(t):
                act.wait_ge(h_lo, t + 1)
                act.dma_start(g.h3[0, t], hh[:, t % 2, :, :].bitcast(F32).rearrange("p k t -> p (k t)")).then_inc(h_out[t % 2], 16)
                act.dma_start(g.h3[1, t], hl[:, t % 2, :, :].bitcast(F32).rearrange("p k t -> p (k t)")).then_inc(h_out[t % 2], 16)

            root.n = 0
            for i in range(TT + 3):
                if i < TT:
                    root(i, 0, rooted)
                if 1 <= i < TT + 1:
                    root(i - 1, 1, rooted2)
                if i >= 4:
                    store(i - 4)
                if i >= 3:
                    t = i - 3
                    act.wait_ge(turned, t + 1)
                    if t >= 3:
                        act.wait_ge(h_lo, t - 2)
                    for k in range(4, 8):
                        last = act.activation(whole[:, t % 3, k, :], g.ps[2 * (t % 2) + 1][:, (k - 4) * P:(k - 3) * P],
                                              ACT.Identity, scale=g.pcol2[:, 16 + k:17 + k])
                    last.then_inc(put_a, 1)
                    act.wait_ge(put_a, t + 1)
                    act.wait_ge(put_v, t + 1)
                    if t >= 2:
                        act.wait_ge(h_out[t % 2], 32 * (t // 2))
                    act.activation(hh[:, t % 2, :, :], whole[:, t % 3, :, :], ACT.Copy).then_inc(h_hi, 1)
            store(TT - 1)
            for r in range(2):
                act.wait_ge(h_out[r], 32 * (TT // 2))

        @block.vector
        def _(dve):
            step = Chain(dve, chain_v)
            dve.wait_ge(row_in, 16)
            for i in range(TT + 3):
                if i < TT:
                    dve.wait_ge(gated, i + 1)
                    dve.wait_ge(ins[i % XR], 16 * (i // XR + 1))
                    dve.tensor_tensor(x1[:, i % XR, :], x1[:, i % XR, :], mo[:, i % 3, :], ALU.add).then_inc(x2_ok, 1)
                if 1 <= i < TT + 1:
                    t = i - 1
                    dve.wait_ge(rooted, t + 1)
                    step(dve.reciprocal(rs[:, 0, t:t + 1], rs[:, 0, t:t + 1]))
                    dve.scalar_tensor_tensor(x1[:, t % XR, :], x1[:, t % XR, :], rs[:, 0, t:t + 1], fg[:, :], ALU.mult, ALU.mult).then_inc(ok, 1)
                if 2 <= i < TT + 2:
                    t = i - 2
                    dve.wait_ge(rooted2, t + 1)
                    if t >= 2:
                        dve.wait_ge(turned, t - 1)
                    step(dve.reciprocal(rs[:, 1, t:t + 1], rs[:, 1, t:t + 1]))
                    dve.tensor_scalar(xn[:, t % 2, :], x1[:, t % XR, :], rs[:, 1, t:t + 1], None, ALU.mult).then_inc(scaled, 1)
                if i >= 3:
                    t = i - 3
                    dve.wait_ge(turned, t + 1)
                    if t >= 3:
                        dve.wait_ge(h_lo, t - 2)
                    for k in range(4):
                        last = dve.tensor_scalar(whole[:, t % 3, k, :], g.ps[2 * (t % 2)][:, k * P:(k + 1) * P],
                                                 g.pcol2[:, 16 + k:17 + k], None, ALU.mult)
                    last.then_inc(put_v, 1)


BLOCKS = [(0, 512, "qa"), (512, 256, "kva"), (768, 512, "ga"), (1280, 512, "qb"), (1792, 512, "kb"), (2304, 512, "vb"),
          (2816, 512, "gb")]
AH, AKV, BH = 8, 2, 8


def phase_second_project(nc, g, ctx0):
    NB = len(BLOCKS)
    HT = TT // 2
    tiles = [(n, half * HT + t) for half in range(2) for n in range(NB) for t in range(HT)]
    pieces = [(half * NB + n, k) for half in range(2) for n in range(NB) for k in range(KT)]
    WR, SR = 6, 14
    with ExitStack() as ctx:
        hTh = sb(nc, ctx, "h3_hi", [P, HT, KT, P], F32R)
        hTl = sb(nc, ctx, "h3_lo", [P, HT, KT, P], F32R)
        wh = sb(nc, ctx, "w2_hi", [P, SR, 512], F32R)
        wl = sb(nc, ctx, "w2_lo", [P, SR, 512], F32R)
        hss = sb(nc, ctx, "h_ss", [P, 8])
        hrs = sb(nc, ctx, "h_rs", [P, 8])
        A, B = (x[:, :, :].rearrange("p t n -> p (t n)") for x in (g.oa, g.ob))
        w = A[:, 0:WR * 512].rearrange("p (r n) -> p r n", r=WR)
        gt = A[:, WR * 512:(WR + 2) * 512].rearrange("p (r n) -> p r n", r=2)
        rope = B[:, 0:1024].rearrange("p (t q c) -> p t q c", t=TT, q=4)
        gains = B[:, 1024:1280].rearrange("p (i d) -> p i d", d=HD)
        sq = B[:, 1280:1792]
        qn = B[:, 1792:2816].rearrange("p (r n) -> p r n", r=2)
        qr = B[:, 2816:3840].rearrange("p (r n) -> p r n", r=2)
        h_in = ring_sems(nc, ctx0, "sp_h_in", HT)
        w_in = ring_sems(nc, ctx0, "sp_w_in", WR)
        w_hi, w_lo, released = sems(nc, ctx0, "sp_w_hi", "sp_w_lo", "sp_w_read")
        (tab_in, gain_in, prod, squared, hroot, hsum, taken, rot, rturned, rput, chain_v, sig_ok, chain_p) = sems(
            nc, ctx0, "sp_tab_in", "sp_gain_in", "sp_prod", "sp_squared", "sp_hroot", "sp_hsum", "sp_taken", "sp_rot",
            "sp_rturned", "sp_rput", "sp_chain", "sp_sig", "sp_chain_p")
        block = ctx.enter_context(nc.Block())
        ROT = ("qa", "kva", "qb", "kb")
        rots = [(n, t) for n, t in tiles if BLOCKS[n][2] in ROT]
        rot_no = {x: i for i, x in enumerate(rots)}
        gates = [(n, t) for n, t in tiles if BLOCKS[n][2] in ("ga", "gb")]
        gate_no = {x: i for i, x in enumerate(gates)}
        gain_of = {"qa": 0, "kva": 1, "qb": 2, "kb": 3}

        def width(q):
            return BLOCKS[pieces[q][0] % NB][1]

        def wait_slot(eng, q):
            if q >= SR:
                blk, k = pieces[q - SR]
                if k < KT - 1:
                    eng.wait_ge(released, (KT - 1) * blk + k + 1)
                else:
                    eng.wait_ge(prod, HT * (blk + 1))

        @block.sync
        def _(sp):
            for q, (blk, k) in enumerate(pieces):
                if q >= WR:
                    sp.wait_ge(w_lo, q - WR + 1)
                at = BLOCKS[blk % NB][0]
                sp.dma_start(w[:, q % WR, 0:width(q)], g.i["w_in_2"][0, k * P:(k + 1) * P, at:at + width(q)]).then_inc(w_in[q % WR], 16)
                if q == WR - 1:
                    sp.dma_start(rope[:, :, :, :], g.i["rope"].rearrange("p (t q c) -> p t q c", t=TT, q=4)).then_inc(tab_in, 16)
                    for i, name in enumerate(("q_norm_a_2", "k_norm_a_2", "q_norm_b_2", "k_norm_b_2")):
                        sp.dma_start(gains[:, i, :], g.i[name].to_broadcast([P, HD])).then_inc(gain_in, 16)

        @block.gpsimd
        def _(pool):
            def load_h(t):
                if t >= HT:
                    pool.wait_ge(prod, HT * (NB - 1) + t - HT + 1)
                for part, dst in ((0, hTh), (1, hTl)):
                    pool.dma_start(dst[:, t % HT, :, :].rearrange("p k t -> p (k t)"), g.h3[part, t]).then_inc(h_in[t % HT], 16)

            for t in range(HT):
                load_h(t)
            pool.wait_ge(w_lo, KT)
            for q, (blk, k) in enumerate(pieces):
                if q < KT:
                    continue
                pool.wait_ge(w_hi, q + 1)
                pool.tensor_tensor(wl[:, q % SR, 0:width(q)], w[:, q % WR, 0:width(q)], wh[:, q % SR, 0:width(q)], ALU.subtract).then_inc(w_lo, 1)
                if blk == NB and k in (2, 5):
                    load_h(HT + k // 3)
                if blk == NB and k == KT - 1:
                    load_h(HT + 2)
                    load_h(HT + 3)

        @block.tensor
        def _(pe):
            def turn(i):
                n, t = rots[i]
                pe.wait_ge(rot, i + 1)
                if i >= 2:
                    pe.wait_ge(rput, i - 1)
                bank = g.ps[4 + i % 2]
                for k in range(4 if BLOCKS[n][2] != "kva" else 2):
                    mm = pe.transpose(bank[:, k * P:(k + 1) * P], qr[:, i % 2, k * P:(k + 1) * P], g.c("ident"))
                mm.then_inc(rturned, 1)

            for m, (n, t) in enumerate(tiles):
                blk, cols = m // HT, BLOCKS[n][1]
                if n == 0:
                    pe.wait_ge(h_in[t % HT], 32 * (t // HT + 1))
                if m >= 4:
                    pe.wait_ge(taken, m - 3)
                for k in range(KT):
                    q = KT * blk + k
                    if t % HT == 0:
                        pe.wait_ge(w_lo, q + 1)
                    for p, (lhs, rhs) in enumerate(((hTl, wh), (hTh, wl), (hTh, wh))):
                        mm = pe.matmul(g.ps[m % 4][:, 0:cols], lhs[:, t % HT, k, :], rhs[:, q % SR, 0:cols],
                                       start=(k == 0 and p == 0), stop=(k == KT - 1 and p == 2))
                    if t % HT == HT - 1 and k < KT - 1:
                        mm.then_inc(released, 1)
                mm.then_inc(prod, 1)
                if m >= 2 and tiles[m - 2] in rot_no:
                    turn(rot_no[tiles[m - 2]])

        @block.scalar
        def _(act):
            def split(q):
                act.wait_ge(w_in[q % WR], 16 * (q // WR + 1))
                wait_slot(act, q)
                act.activation(wh[:, q % SR, 0:width(q)], w[:, q % WR, 0:width(q)], ACT.Copy).then_inc(w_hi, 1)

            def store_gate(i):
                n, t = gates[i]
                act.wait_ge(taken, tiles.index((n, t)) + 1)
                act.dma_start(g.gates[t][:, (0 if BLOCKS[n][2] == "ga" else 512):(512 if BLOCKS[n][2] == "ga" else D)],
                              gt[:, i % 2, :]).then_inc(g.gates_out[i % 2], 16)

            for q in range(KT):
                split(q)
            for m, (n, t) in enumerate(tiles):
                kind = BLOCKS[n][2]
                bank = g.ps[m % 4]
                act.wait_ge(prod, m + 1)
                if kind in gain_of:
                    i = rot_no[n, t]
                    wide = 128 if kind == "kva" else 512
                    if i >= 1:
                        act.wait_ge(hsum, i)
                    act.activation(sq[:, 0:wide], bank[:, 0:wide], ACT.Square).then_inc(squared, 1)
                    act.wait_ge(hsum, i + 1)
                    act.activation(hrs[:, 0:wide // HD], hss[:, 0:wide // HD], ACT.Sqrt, scale=1.0 / HD, bias=g.c("eps")).then_inc(hroot, 1)
                elif kind in ("ga", "gb"):
                    i = gate_no[n, t]
                    if i >= 2:
                        act.wait_ge(g.gates_out[i % 2], 16 * (i // 2))
                    act.activation(gt[:, i % 2, :], bank[:, :], ACT.Sigmoid).then_inc(sig_ok, 1)
                if m >= 1 and tiles[m - 1] in gate_no:
                    store_gate(gate_no[tiles[m - 1]])
                for k in {0: (0, 1, 2), 1: (3, 4, 5), 2: (6, 7), 3: ()}[m % HT]:
                    if m // HT + 1 < 2 * NB:
                        split(KT * (m // HT + 1) + k)
            store_gate(len(gates) - 1)
            for r in range(2):
                act.wait_ge(g.gates_out[r], 16 * len(gates) // 2)

        @block.vector
        def _(dve):
            step = Chain(dve, chain_v)

            for q in range(KT):
                dve.wait_ge(w_hi, q + 1)
                dve.tensor_tensor(wl[:, q, :], w[:, q % WR, :], wh[:, q, :], ALU.subtract).then_inc(w_lo, 1)
            dve.wait_ge(gain_in, 64)
            for i in (0, 2):
                step(dve.tensor_scalar(gains[:, i, :], gains[:, i, :], HD ** -0.5, None, ALU.mult))
            dve.wait_ge(tab_in, 16)
            stored = set()

            def store(i):
                if i in stored:
                    return
                stored.add(i)
                n, t = rots[i]
                kind = BLOCKS[n][2]
                dve.wait_ge(rturned, i + 1)
                k = 2 if kind == "kva" else 4
                dst = {"qa": g.qaT, "kva": g.kaT, "qb": g.qbT, "kb": g.kbT}[kind]
                dve.tensor_copy(dst[:, :, t * P:(t + 1) * P], g.ps[4 + i % 2][:, 0:k * P].rearrange("p (k t) -> p k t", k=k)).then_inc(rput, 1)

            for m, (n, t) in enumerate(tiles):
                kind, bank = BLOCKS[n][2], g.ps[m % 4]
                if kind in gain_of:
                    i = rot_no[n, t]
                    nh = 2 if kind == "kva" else 8
                    wide = nh * HD
                    dve.wait_ge(squared, i + 1)
                    dve.tensor_reduce(hss[:, 0:nh], sq[:, 0:wide].rearrange("p (h d) -> p h d", d=HD), AX, ALU.add).then_inc(hsum, 1)
                    dve.wait_ge(hroot, i + 1)
                    step(dve.reciprocal(hrs[:, 0:nh], hrs[:, 0:nh]))
                    if kind == "kva":
                        dve.tensor_copy(g.va[:, t, :], bank[:, 128:256])
                    q = qn[:, i % 2, 0:wide].rearrange("p (h d) -> p h d", d=HD)
                    dve.tensor_tensor(q, bank[:, 0:wide].rearrange("p (h d) -> p h d", d=HD),
                                      hrs[:, 0:nh].unsqueeze(2).to_broadcast([P, nh, HD]), ALU.mult).then_inc(taken, 1)
                    dve.wait_ge(taken, m + 1)
                    step(dve.tensor_tensor(q, q, gains[:, gain_of[kind], :].unsqueeze(1).to_broadcast([P, nh, HD]), ALU.mult))
                    r = qr[:, i % 2, 0:wide].rearrange("p (h d) -> p h d", d=HD)
                    cs = rope[:, t, 0:2, :].rearrange("p q c -> p (q c)").unsqueeze(1).to_broadcast([P, nh, HD])
                    if i >= 2:
                        dve.wait_ge(rturned, i - 1)
                    if i >= 1:
                        store(i - 1)
                    if kind == "kva":
                        r = qr[:, i % 2, 0:128].rearrange("p (h d) -> p h d", d=HD)
                    half = HD // 2
                    step(dve.tensor_tensor(r, q, cs, ALU.mult))
                    for h in range(2):
                        o = 1 - h
                        last = dve.tensor_tensor(q[:, :, h * half:(h + 1) * half], q[:, :, h * half:(h + 1) * half],
                                                 rope[:, t, 3 - h, :].unsqueeze(1).to_broadcast([P, nh, half]), ALU.mult)
                    step(last)
                    for h in range(2):
                        last = dve.tensor_tensor(r[:, :, h * half:(h + 1) * half], r[:, :, h * half:(h + 1) * half],
                                                 q[:, :, (1 - h) * half:(2 - h) * half], ALU.add)
                    if kind == "kva":
                        step(last)
                        dve.tensor_copy(q, r).then_inc(chain_p, 1)
                        dve.wait_ge(chain_p, t + 1)
                        d4 = qr[:, i % 2, 0:256].rearrange("p (h c d) -> p h c d", c=2, d=HD)
                        dve.tensor_copy(d4[:, :, 0], q)
                        last = dve.tensor_copy(d4[:, :, 1], q)
                    last.then_inc(rot, 1)
                elif kind == "vb":
                    if t % HT == 0:
                        store(rot_no[tiles[m - 1]])
                    dve.wait_ge(prod, m + 1)
                    dve.tensor_copy(g.vb[:, t, :], bank[:, :]).then_inc(taken, 1)
                else:
                    i = gate_no[n, t]
                    dve.wait_ge(sig_ok, i + 1)
                    dve.tensor_tensor(gt[:, i % 2, :], gt[:, i % 2, :], bank[:, :], ALU.mult).then_inc(taken, 1)


def phase_second_attend(nc, g, ctx0):
    items = [(0, h, t) for h in range(AH) for t in range(TT)] + [(1, h, t) for t in range(TT) for h in range(BH)]
    with ExitStack() as ctx:
        bias = sb(nc, ctx, "bias_sb", [P, T + 2 * P])
        sinks = sb(nc, ctx, "sinks_sb", [P, AH])
        s = sb(nc, ctx, "scores", [P, 2, T])
        pr = sb(nc, ctx, "probs", [P, 2, T])
        pT = sb(nc, ctx, "probsT", [P, 2, KT, P])
        m = sb(nc, ctx, "row_max", [P, 4])
        l = sb(nc, ctx, "row_sum", [P, 4])
        e = sb(nc, ctx, "sink_exp", [P, 4])
        (loaded, qk, biased, maxed, exped, pturned, pcopied_v, pcopied_a, pv, out_ok, chain_v, chain_a) = sems(
            nc, ctx0, "at_loaded", "at_scores", "at_biased", "at_max", "at_exp", "at_turned", "at_copied_v", "at_copied_a", "at_pv", "at_out",
            "at_chain", "at_chain_a")
        block = ctx.enter_context(nc.Block())

        def keys(i):
            b, h, t = items[i]
            lo = 0 if b else max(0, t - 1)
            return lo, t + 1 - lo

        def parts(i):
            n = keys(i)[1] * P
            return [(c, min(n, c + 512)) for c in range(0, n, 512)]

        @block.sync
        def _(sp):
            sp.dma_start(bias[:, :], g.i["bias"]).then_inc(loaded, 16)
            sp.dma_start(sinks[:, :], g.i["sinks_a_2"].to_broadcast([P, AH])).then_inc(loaded, 16)

        @block.tensor
        def _(pe):
            pe.wait_ge(loaded, 32)

            def score(i):
                b, h, t = items[i]
                lo, n = keys(i)
                if 2 <= i and not items[i - 2][0]:
                    pe.wait_ge(exped, i - 1)
                elif i >= 2:
                    pe.wait_ge(biased, i - 1)
                half = slice(64 * (h % 2), 64 * (h % 2) + 64)
                q = (g.qbT if b else g.qaT)[half, h // 2, t * P:(t + 1) * P]
                k = g.kbT[half, h // 2] if b else g.kaT[half, h // (AH // AKV)]
                for j, (c0, c1) in enumerate(parts(i)):
                    mm = pe.matmul(g.ps[2 * (i % 2) + j][:, 0:c1 - c0], q, k[:, lo * P + c0:lo * P + c1], start=True, stop=bool(b))
                if not b:
                    at = T + (2 - n) * P
                    mm = pe.matmul(g.ps[2 * (i % 2)][:, 0:n * P], g.c("ident"), bias[:, at:at + n * P], start=False, stop=True)
                mm.then_inc(qk, 1)

            def turn(i):
                lo, n = keys(i)
                pe.wait_ge(exped, i + 1)
                if i >= 1:
                    pe.wait_ge(pcopied_v, i)
                    pe.wait_ge(pcopied_a, i)
                for j in range(n):
                    mm = pe.transpose(g.ps[4 + j // 4][:, (j % 4) * P:(j % 4 + 1) * P], pr[:, i % 2, j * P:(j + 1) * P], g.c("ident"))
                mm.then_inc(pturned, 1)

            def value(i):
                b, h, t = items[i]
                lo, n = keys(i)
                pe.wait_ge(pcopied_v, i + 1)
                pe.wait_ge(pcopied_a, i + 1)
                if i >= 2:
                    pe.wait_ge(out_ok, i - 1)
                for j in range(n):
                    v = g.vb[:, lo + j, h // 2 * P:(h // 2 + 1) * P] if b else g.va[:, lo + j, :]
                    mm = pe.matmul(g.ps[6 + i % 2][:, 0:P], pT[:, i % 2, j, :], v, start=(j == 0), stop=(j == n - 1))
                mm.then_inc(pv, 1)

            N = len(items)
            for i in range(N + 3):
                if i < N:
                    score(i)
                if 2 <= i < N + 2:
                    turn(i - 2)
                if i >= 3:
                    value(i - 3)

        def copy(act, i):
            n = keys(i)[1]
            act.wait_ge(pcopied_v, i + 1)
            if n > 4:
                act.activation(pT[:, i % 2, 4:n, :].rearrange("p k t -> p (k t)"), g.ps[5][:, 0:(n - 4) * P], ACT.Copy).then_inc(pcopied_a, 1)
            else:
                act.nop().then_inc(pcopied_a, 1)

        @block.scalar
        def _(act):
            for i, (b, h, t) in enumerate(items):
                n = keys(i)[1]
                act.wait_ge(maxed, i + 1)
                if i >= 2:
                    act.wait_ge(pturned, i - 1)
                if not b:
                    act.activation(e[:, i % 4:i % 4 + 1], sinks[:, h:h + 1], ACT.Exp, bias=m[:, i % 4:i % 4 + 1])
                src = s[:, i % 2, 0:n * P] if b else g.ps[2 * (i % 2)][:, 0:n * P]
                act.activation(pr[:, i % 2, 0:n * P], src, ACT.Exp, bias=m[:, i % 4:i % 4 + 1],
                               accum_out=l[:, i % 4:i % 4 + 1]).then_inc(exped, 1)
                if i >= 1:
                    copy(act, i - 1)
            copy(act, len(items) - 1)

        @block.vector
        def _(dve):
            step = Chain(dve, chain_v)
            dve.wait_ge(loaded, 32)

            def soft(i):
                b, h, t = items[i]
                lo, n = keys(i)
                dve.wait_ge(qk, i + 1)
                if i >= 2:
                    dve.wait_ge(exped, i - 1)
                if i >= 4:
                    dve.wait_ge(out_ok, i - 3)
                mi = m[:, i % 4:i % 4 + 1]
                if not b:
                    dve.tensor_reduce(mi, g.ps[2 * (i % 2)][:, 0:n * P], AX, ALU.max).then_inc(biased, 1)
                    dve.wait_ge(biased, i + 1)
                    dve.tensor_scalar(mi, mi, sinks[:, h:h + 1], -1.0, ALU.max, ALU.mult).then_inc(maxed, 1)
                    return
                at = (KT - 1 - t) * P
                for j, (c0, c1) in enumerate(parts(i)):
                    last = dve.tensor_tensor(s[:, i % 2, c0:c1], g.ps[2 * (i % 2) + j][:, 0:c1 - c0], bias[:, at + c0:at + c1], ALU.add)
                last.then_inc(biased, 1)
                dve.wait_ge(biased, i + 1)
                step(dve.tensor_reduce(mi, s[:, i % 2, 0:n * P], AX, ALU.max))
                dve.tensor_scalar(mi, mi, -1.0, None, ALU.mult).then_inc(maxed, 1)

            def put(i):
                n = min(4, keys(i)[1])
                dve.wait_ge(pturned, i + 1)
                if i >= 2:
                    dve.wait_ge(pv, i - 1)
                dve.tensor_copy(pT[:, i % 2, 0:n, :].rearrange("p k t -> p (k t)"), g.ps[4][:, 0:n * P]).then_inc(pcopied_v, 1)

            def finish(i):
                b, h, t = items[i]
                li = l[:, i % 4:i % 4 + 1]
                dve.wait_ge(exped, i + 1)
                if not b:
                    step(dve.tensor_tensor(li, li, e[:, i % 4:i % 4 + 1], ALU.add))
                step(dve.reciprocal(li, li))
                dve.wait_ge(pv, i + 1)
                o = (g.ob if b else g.oa)[:, t, h * HD:(h + 1) * HD]
                at = (h % 2 if b else h // (AH // AKV)) * HD
                dve.tensor_scalar(o, g.ps[6 + i % 2][:, at:at + HD], li, None, ALU.mult).then_inc(out_ok, 1)

            N = len(items)
            for i in range(N + 3):
                if i < N:
                    soft(i)
                if 2 <= i < N + 2:
                    put(i - 2)
                if i >= 3:
                    finish(i - 3)


def phase_second_out(nc, g, ctx0):
    with ExitStack() as ctx:
        wraw = sb(nc, ctx, "w_out2_raw", [P, 3, D])
        wh = sb(nc, ctx, "w_out2_hi", [P, KT, D], F32R)
        wl = sb(nc, ctx, "w_out2_lo", [P, KT, D], F32R)
        mh = sb(nc, ctx, "mix2_hi", [P, 2, KT, P], F32R)
        ml = sb(nc, ctx, "mix2_lo", [P, 2, KT, P], F32R)
        xin = sb(nc, ctx, "x2_again", [P, 2, D])
        gt = sb(nc, ctx, "gates_back", [P, 2, D])
        mix = sb(nc, ctx, "mix2", [P, 2, D])
        x_in = ring_sems(nc, ctx0, "so_x_in", 2)
        g_in = ring_sems(nc, ctx0, "so_gates_in", 2)
        w_in = ring_sems(nc, ctx0, "so_w_in", 3)
        gated, w_hi, w_lo, turned, m_hi, m_lo, prod, ok = sems(
            nc, ctx0, "so_gated", "so_w_hi", "so_w_lo", "so_turned", "so_mix_hi", "so_mix_lo", "so_prod", "so_ok")
        block = ctx.enter_context(nc.Block())
        out_v = g.out[0].rearrange("(t p) d -> t p d", p=P)

        @block.sync
        def _(sp):
            def load_gates(t):
                if t >= 2:
                    sp.wait_ge(gated, t - 1)
                sp.dma_start(gt[:, t % 2, :], g.gates[t]).then_inc(g_in[t % 2], 16)

            load_gates(0)
            load_gates(1)
            for k in range(KT):
                if k >= 3:
                    sp.wait_ge(w_lo, k - 2)
                sp.dma_start(wraw[:, k % 3, :], g.i["w_out_2"][0, k * P:(k + 1) * P, :]).then_inc(w_in[k % 3], 16)

            def store(t):
                sp.wait_ge(ok, t + 1)
                sp.dma_start(out_v[t], xin[:, t % 2, :]).then_inc(g.out_done[t % 2], 16)

            for t in range(TT):
                if t >= 2:
                    sp.wait_ge(g.out_done[t % 2], 16 * (t // 2))
                sp.dma_start(xin[:, t % 2, :], g.x2_rows[t]).then_inc(x_in[t % 2], 16)
                if t + 2 < TT:
                    load_gates(t + 2)
                if t >= 1:
                    store(t - 1)
            store(TT - 1)
            for r in range(2):
                sp.wait_ge(g.out_done[r], 16 * TT // 2)

        @block.tensor
        def _(pe):
            def turn(t):
                pe.wait_ge(gated, t + 1)
                if t >= 1:
                    pe.wait_ge(m_lo, t)
                for k in range(KT):
                    mm = pe.transpose(g.ps[4 + k // 4][:, (k % 4) * P:(k % 4 + 1) * P], mix[:, t % 2, k * P:(k + 1) * P], g.c("ident"))
                mm.then_inc(turned, 1)

            turn(0)
            for t in range(TT):
                pe.wait_ge(m_lo, t + 1)
                if t + 1 < TT:
                    turn(t + 1)
                if t >= 2:
                    pe.wait_ge(ok, t - 1)
                for k in range(KT):
                    if t == 0:
                        pe.wait_ge(w_lo, k + 1)
                    for p, (lhs, rhs) in enumerate(((ml, wh), (mh, wl), (mh, wh))):
                        for h in range(2):
                            mm = pe.matmul(g.ps[2 * (t % 2) + h][:, :], lhs[:, t % 2, k, :], rhs[:, k, h * 512:(h + 1) * 512],
                                           start=(k == 0 and p == 0), stop=(k == KT - 1 and p == 2))
                mm.then_inc(prod, 1)

        @block.scalar
        def _(act):
            def split(t):
                act.wait_ge(turned, t + 1)
                if t >= 2:
                    act.wait_ge(prod, t - 1)
                for q in range(2):
                    last = act.activation(mh[:, t % 2, 4 * q:4 * q + 4, :].rearrange("p k t -> p (k t)"), g.ps[4 + q][:, :], ACT.Copy)
                last.then_inc(m_hi, 1)

            split(0)
            for k in range(KT):
                act.wait_ge(w_in[k % 3], 16 * (k // 3 + 1))
                act.activation(wh[:, k, :], wraw[:, k % 3, :], ACT.Copy).then_inc(w_hi, 1)
            for t in range(1, TT):
                split(t)

        @block.vector
        def _(dve):
            def gate(t):
                dve.wait_ge(g_in[t % 2], 16 * (t // 2 + 1))
                if t >= 2:
                    dve.wait_ge(turned, t - 1)
                dve.tensor_tensor(mix[:, t % 2, 0:512], g.oa[:, t, :], gt[:, t % 2, 0:512], ALU.mult)
                dve.tensor_tensor(mix[:, t % 2, 512:D], g.ob[:, t, :], gt[:, t % 2, 512:D], ALU.mult).then_inc(gated, 1)

            def put(t):
                dve.wait_ge(m_hi, t + 1)
                for q in range(2):
                    last = dve.tensor_tensor(ml[:, t % 2, 4 * q:4 * q + 4, :].rearrange("p k t -> p (k t)"), g.ps[4 + q][:, :],
                                             mh[:, t % 2, 4 * q:4 * q + 4, :].rearrange("p k t -> p (k t)"), ALU.subtract)
                last.then_inc(m_lo, 1)

            gate(0)
            gate(1)
            put(0)
            for k in range(KT):
                dve.wait_ge(w_hi, k + 1)
                dve.tensor_tensor(wl[:, k, :], wraw[:, k % 3, :], wh[:, k, :], ALU.subtract).then_inc(w_lo, 1)
            for t in range(TT):
                if t + 1 < TT:
                    put(t + 1)
                if t + 2 < TT:
                    gate(t + 2)
                dve.wait_ge(prod, t + 1)
                dve.wait_ge(x_in[t % 2], 16 * (t // 2 + 1))
                for h in range(2):
                    w = slice(h * 512, (h + 1) * 512)
                    last = dve.tensor_tensor(xin[:, t % 2, w], xin[:, t % 2, w], g.ps[2 * (t % 2) + h][:, :], ALU.add)
                last.then_inc(ok, 1)


def phase_second(nc, g, signals):
    with ExitStack() as ctx:
        g.oa = sb(nc, ctx, "heads_a", [P, TT, AH * HD])
        g.ob = sb(nc, ctx, "heads_b", [P, TT, BH * HD])
        with ExitStack() as heads:
            g.qaT = sb(nc, heads, "qaT", [P, 4, T])
            g.kaT = sb(nc, heads, "kaT", [P, AKV, T])
            g.qbT = sb(nc, heads, "qbT", [P, 4, T])
            g.kbT = sb(nc, heads, "kbT", [P, 4, T])
            g.va = sb(nc, heads, "va", [P, TT, AKV * HD])
            g.vb = sb(nc, heads, "vb", [P, TT, BH * HD])
            phase_second_project(nc, g, signals)
            phase_second_attend(nc, g, signals)
        phase_second_out(nc, g, signals)


def build(nc, args, out):
    g = Shared()
    g.i = args
    g.out = out
    g.rkv = nc.dram_tensor("rkv_scratch", [NCH, P, 4, HP, C], F32).ap()
    g.xn_rows = nc.dram_tensor("xn_rows", [T, D], F32).ap()
    g.h3 = nc.dram_tensor("h3_tiles", [2, TT, P, D], F32).ap()
    g.gates = nc.dram_tensor("gates", [TT, P, D], F32).ap()
    g.moe = nc.dram_tensor("moe_rows", [T, D], F32).ap()
    g.x1_rows = nc.dram_tensor("x1_rows", [T, D], F32).ap()
    x2 = nc.dram_tensor("x2_rows", [T, D], F32).ap()
    g.x2_rows = x2.rearrange("(t p) d -> t p d", p=P)

    def flat(name):
        a = args[name]
        n = len(a.shape)
        if n == 1:
            return a
        names = " ".join("abcd"[:n])
        return a.rearrange(f"{names} -> ({names})")

    g.flat = flat
    with ExitStack() as ctx:
        g.ps = [ctx.enter_context(nc.psum_tensor(f"bank{b}", [P, 512], F32)) for b in range(8)]
        g.const = sb(nc, ctx, "const", [P, NCONST])
        g.pcol = sb(nc, ctx, "pcol", [P, NROWS])
        g.pcol2 = sb(nc, ctx, "pcol2", [P, 24])
        g.cond = sb(nc, ctx, "cond", [P, KT, 2])
        g.mod = sb(nc, ctx, "mod", [P, 48, 2])
        g.a2 = sb(nc, ctx, "a2", [P, KT])
        g.valsT = sb(nc, ctx, "valsT", [P, NE])
        g.idxT = sb(nc, ctx, "idxT", [P, NE], U32)
        g.omu = sb(nc, ctx, "omu", [P, NRW])
        g.mus = sb(nc, ctx, "mus", [P, NRW, 6])

        def c(name):
            at, n = CONST_AT[name]
            return g.const[:, at:at + n]

        def p(name):
            at, n = ROW_AT[name]
            return g.pcol[:, at:at + n]

        g.c, g.p = c, p
        lasting = Signals(nc)
        g.combined = ring_sems(nc, lasting, "combined", 4)
        g.h_out = ring_sems(nc, lasting, "h3_stored", 2)
        g.gates_out = ring_sems(nc, lasting, "gates_stored", 2)
        g.out_done = ring_sems(nc, lasting, "out_done", 2)
        signals = Signals(nc)
        phase_params(nc, g, signals)
        phase_modulation(nc, g, signals, "first", range(4))
        with ExitStack() as first:
            g.g2 = sb(nc, first, "g2_row", [P, D])
            g.affT = sb(nc, first, "affT", [NE, T])
            with ExitStack() as mid:
                g.bT = sb(nc, mid, "bT", [P, 4, T])
                g.lora = sb(nc, mid, "lora", [P, TA])
                g.xg = sb(nc, mid, "xg", [P, T])
                phase_project(nc, g, signals)
                g.yT = sb(nc, mid, "yT", [P, HP, T])
                phase_wkv(nc, g, signals)
                signals.clear()
                phase_heads_out(nc, g, signals, range(4, 12))
                phase_mix_out(nc, g, signals)
            signals.clear()
            phase_experts(nc, g, signals)
            phase_combine(nc, g, signals)
        signals.clear()
        phase_second(nc, g, signals)


_INS = ['x', 'c', 'ctx', 'c_ctx', 'ada_w', 'ada_b', 'norm1_g', 'norm2_g', 'w_in', 'shift_mu', 'w0', 'w_lora_up', 'a0',
        'a_lora_up', 'k_k', 'k_a', 'r_k', 'g_lora_up', 'gn_g', 'gn_b', 'conv_w', 'w_out', 'router_w', 'exp_w_gate',
        'exp_w_up', 'exp_w_down', 'final_g', 'norm_gain_2', 'w_in_2', 'q_norm_a_2', 'k_norm_a_2', 'sinks_a_2',
        'q_norm_b_2', 'k_norm_b_2', 'w_out_2']


def kernel(**inputs):
    import concourse.bacc as _bacc
    from concourse.bass_utils import run_bass_kernel_spmd as _run

    nc = _bacc.Bacc("TRN2", target_bir_lowering=False, num_devices=1)
    arrays, args = {}, {}
    for name in _INS:
        a = np.ascontiguousarray(inputs[name])
        arrays[f"in_{name}_dram"] = a
        args[name] = nc.dram_tensor(f"in_{name}_dram", a.shape, mybir.dt.from_np(a.dtype), kind="ExternalInput").ap()
    for name, a in (("consts", CONSTS), ("rope", _rope_tables()), ("bias", _bias_tables())):
        arrays[f"in_{name}_dram"] = a
        args[name] = nc.dram_tensor(f"in_{name}_dram", a.shape, F32, kind="ExternalInput").ap()
    out = nc.dram_tensor("out_0_dram", (1, T, D), F32, kind="ExternalOutput").ap()
    build(nc, args, out)
    r = _run(nc, [arrays], core_ids=[0])
    return r.results[0]["out_0_dram"]
```
